# Optimizing a Trainium2 kernel written in Bass

```python
import math
import jax, jax.numpy as jnp
from jax import lax
import numpy as np
import jax
import jax.numpy as jnp

D_MODEL = 1024
BATCH = 1
SEQ = 512
DEPTH = 1

D_MIX = D_MODEL
N_GROUPS = 4
GROUP = D_MIX // N_GROUPS
HEAD_DIM = 64
LRU_BLOCKS = GROUP // HEAD_DIM
LRU_BLOCK_DIM = GROUP // LRU_BLOCKS
LRU_CONV = 4
LRU_C = 8.0
SC_CONV = 3
FOX_HEADS = GROUP // HEAD_DIM
NSA_HEADS = GROUP // HEAD_DIM
CMP_LEN = 32
CMP_STRIDE = 16
CMP_HIDDEN = 128
SLC_BLOCK = 64
SLC_TOPK = 16
WINDOW = 512
Q_BLOCK = 128
REL_BUCKETS = 32
REL_MAX_DIST = 128
D_FF = ((8 * D_MODEL // 3 + 255) // 256) * 256
NEG_INF = -1e30
BIG = 1e30
RMS_EPS = 1e-6

C_LRU_X = 0
C_LRU_G = C_LRU_X + GROUP
C_SC_B = C_LRU_G + GROUP
C_SC_C = C_SC_B + GROUP
C_SC_X = C_SC_C + GROUP
C_FOX_Q = C_SC_X + GROUP
C_FOX_K = C_FOX_Q + GROUP
C_FOX_V = C_FOX_K + GROUP
C_FOX_F = C_FOX_V + GROUP
C_NSA_Q = C_FOX_F + FOX_HEADS
C_NSA_KV = C_NSA_Q + GROUP
C_NSA_G = C_NSA_KV + 6 * HEAD_DIM
N_IN = C_NSA_G + 3 * NSA_HEADS


def rms_norm(x, g):
    xf = x.astype(jnp.float32)
    y = xf * lax.rsqrt(jnp.mean(xf * xf, axis=-1, keepdims=True) + RMS_EPS)
    return (y * g.astype(jnp.float32)).astype(x.dtype)

def cols(z, start, width):
    return z[..., start:start + width]

def causal_dwconv(x, w):
    k_len, ch = w.shape
    return lax.conv_general_dilated(x, w[:, None, :], window_strides=(1,), padding=[(k_len - 1, 0)],
                                    dimension_numbers=('NWC', 'WIO', 'NWC'), feature_group_count=ch)

def masked_softmax(s, mask):
    p = jax.nn.softmax(jnp.where(mask, s, NEG_INF), axis=-1)
    return jnp.where(mask, p, 0.0)

def rel_bucket(dist):
    max_exact = REL_BUCKETS // 2
    d = jnp.maximum(dist, 0)
    large = max_exact + (jnp.log(jnp.maximum(d, 1).astype(jnp.float32) / max_exact)
                         / math.log(REL_MAX_DIST / max_exact) * (REL_BUCKETS - max_exact)).astype(jnp.int32)
    large = jnp.minimum(large, REL_BUCKETS - 1)
    return jnp.where(d < max_exact, d, large)

def rg_lru_mixer(xr, gate, conv_w, conv_b, w_gates, b_gates, lam):
    bsz, s_len, _ = xr.shape
    xc = causal_dwconv(xr, conv_w) + conv_b
    xb = xc.reshape(bsz, s_len, LRU_BLOCKS, LRU_BLOCK_DIM)
    r = jax.nn.sigmoid(jnp.einsum('bshi,hij->bshj', xb, w_gates[0]).reshape(bsz, s_len, GROUP) + b_gates[0])
    i = jax.nn.sigmoid(jnp.einsum('bshi,hij->bshj', xb, w_gates[1]).reshape(bsz, s_len, GROUP) + b_gates[1])
    log_a = (-LRU_C * jax.nn.softplus(-lam.astype(jnp.float32))) * r.astype(jnp.float32)
    a = jnp.exp(log_a)
    b = jnp.sqrt(-jnp.expm1(2.0 * log_a)) * (i * xc).astype(jnp.float32)

    def combine(left, right):
        a1, b1 = left
        a2, b2 = right
        return a1 * a2, a2 * b1 + b2

    _, h = lax.associative_scan(combine, (a, b), axis=1)
    return h.astype(xr.dtype) * jax.nn.gelu(gate)

def short_conv_mixer(bg, cg, xs, conv_w):
    return bg * causal_dwconv(cg * xs, conv_w)

def fox_mixer(q, k, v, f_logit, f_bias, qk_gain):
    bsz, s_len, _ = q.shape
    h, d = FOX_HEADS, HEAD_DIM
    q = rms_norm(q.reshape(bsz, s_len, h, d), qk_gain[0])
    k = rms_norm(k.reshape(bsz, s_len, h, d), qk_gain[1])
    v = v.reshape(bsz, s_len, h, d)
    logf = jax.nn.log_sigmoid((f_logit + f_bias).astype(jnp.float32))
    c = lax.cumsum(logf, axis=1).transpose(0, 2, 1)
    nb = s_len // Q_BLOCK
    qb = q.reshape(bsz, nb, Q_BLOCK, h, d).swapaxes(0, 1)
    cb = c.reshape(bsz, h, nb, Q_BLOCK).transpose(2, 0, 1, 3)
    kpos = jnp.arange(s_len)
    scale = HEAD_DIM ** -0.5

    def block(args):
        qi, ci, bi = args
        t = bi * Q_BLOCK + jnp.arange(Q_BLOCK)
        s = jnp.einsum('bqhd,bkhd->bhqk', qi, k).astype(jnp.float32) * scale + (ci[..., :, None] - c[..., None, :])
        p = masked_softmax(s, kpos[None, :] <= t[:, None])
        return jnp.einsum('bhqk,bkhd->bqhd', p.astype(v.dtype), v)

    o = lax.map(block, (qb, cb, jnp.arange(nb)))
    return o.swapaxes(0, 1).reshape(bsz, s_len, GROUP)

def compress(kx, pos, w1, w2):
    s_len = kx.shape[1]
    n_cmp = (s_len - CMP_LEN) // CMP_STRIDE + 1
    idx = jnp.arange(n_cmp)[:, None] * CMP_STRIDE + jnp.arange(CMP_LEN)[None, :]
    blocks = kx[:, idx] + pos
    hid = jax.nn.gelu(jnp.einsum('bnld,ldm->bnm', blocks, w1))
    return hid @ w2

def nsa_mixer(q, kc_in, vc_in, ks_in, vs_in, kw_in, vw_in, g_logit, g_bias, qk_gain, cmp_pos, cmp_w1, cmp_w2, rel_bias):
    bsz, s_len, _ = q.shape
    h, d = NSA_HEADS, HEAD_DIM
    f32 = jnp.float32
    q = rms_norm(q.reshape(bsz, s_len, h, d), qk_gain[0])
    kc = rms_norm(compress(kc_in, cmp_pos[0], cmp_w1[0], cmp_w2[0]), qk_gain[1])
    vc = compress(vc_in, cmp_pos[1], cmp_w1[1], cmp_w2[1])
    ks_ = rms_norm(ks_in, qk_gain[2])
    kw = rms_norm(kw_in, qk_gain[3])
    gates = jax.nn.sigmoid(g_logit + g_bias).reshape(bsz, s_len, 3, h)
    n_cmp = kc.shape[1]
    n_slc = s_len // SLC_BLOCK
    top = min(SLC_TOPK, n_slc)
    cmp_start = jnp.arange(n_cmp) * CMP_STRIDE
    cmp_end = cmp_start + CMP_LEN - 1
    slc_start = jnp.arange(n_slc) * SLC_BLOCK
    overlap = jnp.clip(jnp.minimum(cmp_start[:, None] + CMP_LEN, slc_start[None, :] + SLC_BLOCK)
                       - jnp.maximum(cmp_start[:, None], slc_start[None, :]), 0, CMP_LEN).astype(f32)
    ks_blk = ks_.reshape(bsz, n_slc, SLC_BLOCK, d)
    vs_blk = vs_in.reshape(bsz, n_slc, SLC_BLOCK, d)
    kw_pad = jnp.pad(kw, ((0, 0), (WINDOW, 0), (0, 0)))
    vw_pad = jnp.pad(vw_in, ((0, 0), (WINDOW, 0), (0, 0)))
    nb = s_len // Q_BLOCK
    qb = q.reshape(bsz, nb, Q_BLOCK, h, d).swapaxes(0, 1)
    gb = gates.reshape(bsz, nb, Q_BLOCK, 3, h).swapaxes(0, 1)
    bidx = jnp.arange(bsz)[:, None, None]
    jblk = jnp.arange(n_slc)
    scale = HEAD_DIM ** -0.5

    def block(args):
        qi, gi, bi = args
        t = bi * Q_BLOCK + jnp.arange(Q_BLOCK)
        dist_c = t[:, None] - cmp_end[None, :]
        s_c = (jnp.einsum('bqhd,bnd->bhqn', qi, kc).astype(f32) * scale
               + rel_bias[rel_bucket(dist_c)].transpose(2, 0, 1))
        p_c = masked_softmax(s_c, dist_c >= 0)
        o_c = jnp.einsum('bhqn,bnd->bqhd', p_c.astype(vc.dtype), vc)
        imp = jnp.einsum('bhqn,nm->bqm', p_c, overlap)
        cur = t // SLC_BLOCK
        forced = (jblk[None, :] == 0) | (jblk[None, :] == cur[:, None]) | (jblk[None, :] == cur[:, None] - 1)
        imp = jnp.where(forced, BIG, imp)
        imp = jnp.where(jblk[None, :] <= cur[:, None], imp, -jnp.inf)
        _, sel = lax.top_k(imp, top)
        k_sel = ks_blk[bidx, sel].reshape(bsz, Q_BLOCK, top * SLC_BLOCK, d)
        v_sel = vs_blk[bidx, sel].reshape(bsz, Q_BLOCK, top * SLC_BLOCK, d)
        pos_sel = (sel[..., None] * SLC_BLOCK + jnp.arange(SLC_BLOCK)).reshape(bsz, Q_BLOCK, top * SLC_BLOCK)
        dist_s = t[None, :, None] - pos_sel
        s_s = (jnp.einsum('bqhd,bqnd->bhqn', qi, k_sel).astype(f32) * scale
               + rel_bias[rel_bucket(dist_s)].transpose(0, 3, 1, 2))
        p_s = masked_softmax(s_s, (dist_s >= 0)[:, None])
        o_s = jnp.einsum('bhqn,bqnd->bqhd', p_s.astype(v_sel.dtype), v_sel)
        k_win = lax.dynamic_slice_in_dim(kw_pad, bi * Q_BLOCK, WINDOW + Q_BLOCK, axis=1)
        v_win = lax.dynamic_slice_in_dim(vw_pad, bi * Q_BLOCK, WINDOW + Q_BLOCK, axis=1)
        pos_w = bi * Q_BLOCK - WINDOW + jnp.arange(WINDOW + Q_BLOCK)
        dist_w = t[:, None] - pos_w[None, :]
        mask_w = (dist_w >= 0) & (dist_w < WINDOW) & (pos_w[None, :] >= 0)
        s_w = (jnp.einsum('bqhd,bnd->bhqn', qi, k_win).astype(f32) * scale
               + rel_bias[rel_bucket(dist_w)].transpose(2, 0, 1))
        p_w = masked_softmax(s_w, mask_w)
        o_w = jnp.einsum('bhqn,bnd->bqhd', p_w.astype(v_win.dtype), v_win)
        return gi[:, :, 0, :, None] * o_c + gi[:, :, 1, :, None] * o_s + gi[:, :, 2, :, None] * o_w

    o = lax.map(block, (qb, gb, jnp.arange(nb)))
    return o.swapaxes(0, 1).reshape(bsz, s_len, GROUP)

def first_inputs(seed: int = 0) -> dict:
    key = jax.random.key(seed)
    ks = jax.random.split(key, 24)
    f32 = jnp.float32
    nl = DEPTH

    def nrm(k, shape, scale):
        return jax.random.normal(k, shape, f32) * scale

    u = jax.random.uniform(ks[7], (nl, GROUP), f32, 0.9, 0.999)
    return {
        'x': jax.random.normal(ks[0], (BATCH, SEQ, D_MODEL), f32),
        'norm_mix': 1.0 + nrm(ks[1], (nl, D_MODEL), 0.02),
        'w_in': nrm(ks[2], (nl, D_MODEL, N_IN), D_MODEL ** -0.5),
        'lru_conv_w': nrm(ks[3], (nl, LRU_CONV, GROUP), LRU_CONV ** -0.5),
        'lru_conv_b': nrm(ks[4], (nl, GROUP), 0.02),
        'lru_w_gates': nrm(ks[5], (nl, 2, LRU_BLOCKS, LRU_BLOCK_DIM, LRU_BLOCK_DIM), LRU_BLOCK_DIM ** -0.5),
        'lru_b_gates': nrm(ks[6], (nl, 2, GROUP), 0.02),
        'lru_lambda': jnp.log(u) - jnp.log1p(-u),
        'sc_conv_w': nrm(ks[8], (nl, SC_CONV, GROUP), SC_CONV ** -0.5),
        'fox_f_bias': 3.0 + nrm(ks[9], (nl, FOX_HEADS), 0.1),
        'fox_qk_norm': 1.0 + nrm(ks[10], (nl, 2, HEAD_DIM), 0.02),
        'nsa_qk_norm': 1.0 + nrm(ks[11], (nl, 4, HEAD_DIM), 0.02),
        'nsa_cmp_pos': nrm(ks[12], (nl, 2, CMP_LEN, HEAD_DIM), 0.1),
        'nsa_cmp_w1': nrm(ks[13], (nl, 2, CMP_LEN, HEAD_DIM, CMP_HIDDEN), (CMP_LEN * HEAD_DIM) ** -0.5),
        'nsa_cmp_w2': nrm(ks[14], (nl, 2, CMP_HIDDEN, HEAD_DIM), CMP_HIDDEN ** -0.5),
        'nsa_gate_bias': nrm(ks[15], (nl, 3 * NSA_HEADS), 0.02),
        'rel_bias': nrm(ks[16], (REL_BUCKETS, NSA_HEADS), 0.2),
        'out_norm': 1.0 + nrm(ks[17], (nl, N_GROUPS, GROUP), 0.02),
        'w_out': nrm(ks[18], (nl, D_MIX, D_MODEL), D_MIX ** -0.5),
        'norm_ffn': 1.0 + nrm(ks[19], (nl, D_MODEL), 0.02),
        'w_gate_up': nrm(ks[20], (nl, D_MODEL, 2 * D_FF), D_MODEL ** -0.5),
        'w_down': nrm(ks[21], (nl, D_FF, D_MODEL), D_FF ** -0.5),
    }

def first_block(x, norm_mix, w_in, lru_conv_w, lru_conv_b, lru_w_gates, lru_b_gates, lru_lambda, sc_conv_w,
              fox_f_bias, fox_qk_norm, nsa_qk_norm, nsa_cmp_pos, nsa_cmp_w1, nsa_cmp_w2, nsa_gate_bias,
              rel_bias, out_norm, w_out, norm_ffn, w_gate_up, w_down):
    for l in range(DEPTH):
        z = rms_norm(x, norm_mix[l]) @ w_in[l]
        y_a = rg_lru_mixer(cols(z, C_LRU_X, GROUP), cols(z, C_LRU_G, GROUP), lru_conv_w[l], lru_conv_b[l],
                           lru_w_gates[l], lru_b_gates[l], lru_lambda[l])
        y_b = short_conv_mixer(cols(z, C_SC_B, GROUP), cols(z, C_SC_C, GROUP), cols(z, C_SC_X, GROUP), sc_conv_w[l])
        y_c = fox_mixer(cols(z, C_FOX_Q, GROUP), cols(z, C_FOX_K, GROUP), cols(z, C_FOX_V, GROUP),
                        cols(z, C_FOX_F, FOX_HEADS), fox_f_bias[l], fox_qk_norm[l])
        kv = [cols(z, C_NSA_KV + j * HEAD_DIM, HEAD_DIM) for j in range(6)]
        y_d = nsa_mixer(cols(z, C_NSA_Q, GROUP), kv[0], kv[1], kv[2], kv[3], kv[4], kv[5],
                        cols(z, C_NSA_G, 3 * NSA_HEADS), nsa_gate_bias[l], nsa_qk_norm[l],
                        nsa_cmp_pos[l], nsa_cmp_w1[l], nsa_cmp_w2[l], rel_bias)
        mixed = jnp.concatenate([rms_norm(y_a, out_norm[l, 0]), rms_norm(y_b, out_norm[l, 1]),
                                 rms_norm(y_c, out_norm[l, 2]), rms_norm(y_d, out_norm[l, 3])], axis=-1)
        x = x + mixed @ w_out[l]
        gu = rms_norm(x, norm_ffn[l]) @ w_gate_up[l]
        x = x + (jax.nn.silu(gu[..., :D_FF]) * gu[..., D_FF:]) @ w_down[l]
    return x


DEPTH_2 = 2

GRID_W = 64
CTX_LEN = 256
N_AB_LAYERS = (DEPTH_2 + 1) // 2
N_C_LAYERS = DEPTH_2 // 2

RW_HEADS = 8
RW_HEAD_DIM = 64
RW_DIM = RW_HEADS * RW_HEAD_DIM
DECAY_LORA = 64
ICLR_LORA = 64
GATE_LORA = 128
RW_COLS = 3 * RW_DIM + 2 * DECAY_LORA + 2 * ICLR_LORA + GATE_LORA
RW_SPLITS = (RW_DIM, 2 * RW_DIM, 3 * RW_DIM, 3 * RW_DIM + DECAY_LORA, 3 * RW_DIM + 2 * DECAY_LORA,
             3 * RW_DIM + 2 * DECAY_LORA + ICLR_LORA, 3 * RW_DIM + 2 * DECAY_LORA + 2 * ICLR_LORA)
LN_X_EPS = 64e-5

MLA_HEADS = 8
MLA_NOPE = 64
MLA_ROPE = 32
MLA_V = 64
MLA_QK = MLA_NOPE + MLA_ROPE
MLA_Q_RANK = 384
MLA_KV_RANK = 256
MLA_COLS = MLA_Q_RANK + MLA_KV_RANK + MLA_ROPE
AB_IN = RW_COLS + MLA_COLS
AB_OUT = RW_DIM + MLA_HEADS * MLA_V

GQA_HEADS = 16
GQA_KV_HEADS = 4
GQA_HEAD_DIM = 64
GQA_IN = (GQA_HEADS + 2 * GQA_KV_HEADS) * GQA_HEAD_DIM

N_EXPERTS = 16
EXPERTS_PER_GROUP = N_EXPERTS // N_GROUPS
TOP_K = 2
EXPERT_FF = 256
SHARED_FF = 256

ROPE_THETA = 10000.0
NORM_EPS = 1e-6


def rmsnorm(x, g):
    xf = x.astype(jnp.float32)
    y = xf * lax.rsqrt(jnp.mean(xf * xf, axis=-1, keepdims=True) + NORM_EPS)
    return y.astype(x.dtype) * g

def ada_mods(cvec, w, b):
    m = jax.nn.silu(cvec) @ w + b
    return jnp.split(m[:, None, :], 6, axis=-1)

def modulate(h, shift, scale):
    return h * (1.0 + scale) + shift

def rope_1d(x, pos):
    half = x.shape[-1] // 2
    inv = ROPE_THETA ** (-jnp.arange(half, dtype=jnp.float32) / half)
    ang = pos[:, None] * inv[None, :]
    cos = jnp.cos(ang)[None, :, None, :].astype(x.dtype)
    sin = jnp.sin(ang)[None, :, None, :].astype(x.dtype)
    x1, x2 = x[..., :half], x[..., half:]
    return jnp.concatenate([x1 * cos - x2 * sin, x2 * cos + x1 * sin], axis=-1)

def axial_rope(x, row, col):
    h = x.shape[-1] // 2
    return jnp.concatenate([rope_1d(x[..., :h], row), rope_1d(x[..., h:], col)], axis=-1)

def ctx_attention(q, k, v, scale):
    B, L, H, d = q.shape
    Hk = k.shape[2]
    qg = q.reshape(B, L, Hk, H // Hk, d)
    s = jnp.einsum('bqkgd,bskd->bkgqs', qg, k).astype(jnp.float32) * scale
    p = jax.nn.softmax(s, axis=-1).astype(v.dtype)
    o = jnp.einsum('bkgqs,bskd->bqkgd', p, v)
    return o.reshape(B, L, H, v.shape[-1])

def latent_attention(q, k_lat, v_lat, k_ctx, v_ctx, scale):
    B, S, H, d = q.shape
    Hk = k_lat.shape[2]
    G = H // Hk
    dv = v_lat.shape[-1]
    n_ctx = k_ctx.shape[1]
    n_blk = S // Q_BLOCK
    qb = q.reshape(B, n_blk, Q_BLOCK, Hk, G, d).transpose(1, 0, 2, 3, 4, 5)

    def one_block(qblk):
        s_ctx = jnp.einsum('bqkgd,bskd->bkgqs', qblk, k_ctx)
        s_lat = jnp.einsum('bqkgd,bskd->bkgqs', qblk, k_lat)
        s = jnp.concatenate([s_ctx, s_lat], axis=-1).astype(jnp.float32) * scale
        p = jax.nn.softmax(s, axis=-1).astype(v_lat.dtype)
        return (jnp.einsum('bkgqs,bskd->bqkgd', p[..., :n_ctx], v_ctx)
                + jnp.einsum('bkgqs,bskd->bqkgd', p[..., n_ctx:], v_lat))

    o = lax.map(one_block, qb)
    return o.transpose(1, 0, 2, 3, 4, 5).reshape(B, S, H, dv)

def centred_shift_mix(p, mu):
    prev = jnp.pad(p[:, :-1], ((0, 0), (1, 0), (0, 0)))
    nxt = jnp.pad(p[:, 1:], ((0, 0), (0, 1), (0, 0)))
    return p + mu * (0.5 * (prev + nxt) - p)

def wkv7_scan(state0, r, w, k, v, a_vec, b_vec, reverse):
    xs = tuple(t.transpose(1, 0, 2, 3) for t in (r, w, k, v, a_vec, b_vec))

    def step(S, inp):
        r_t, w_t, k_t, v_t, a_t, b_t = inp
        sa = jnp.einsum('bhij,bhj->bhi', S, a_t)
        S = (S * w_t[:, :, None, :] + sa[..., None] * b_t[:, :, None, :]
             + v_t[..., None] * k_t[:, :, None, :])
        return S, jnp.einsum('bhij,bhj->bhi', S, r_t)

    s_fin, ys = lax.scan(step, state0, xs, reverse=reverse)
    return s_fin, ys.transpose(1, 0, 2, 3)

def rwkv_prep(p, prm):
    p = centred_shift_mix(p, prm['mu'])
    r, k, v, w1f, w1b, a1f, a1b, g1 = jnp.split(p, RW_SPLITS, axis=-1)
    B, L = p.shape[:2]

    def heads(t):
        return t.astype(jnp.float32).reshape(B, L, RW_HEADS, RW_HEAD_DIM)

    kk = heads(k * prm['k_k'])
    kk = kk * lax.rsqrt(jnp.sum(kk * kk, axis=-1, keepdims=True) + 1e-12)
    kf = k.astype(jnp.float32)
    dirs = []
    for d, (w1, a1) in enumerate(((w1f, a1f), (w1b, a1b))):
        z = (prm['w0'][d] + jnp.tanh(w1) @ prm['w2'][d]).astype(jnp.float32)
        decay = jnp.exp(-jnp.exp(-jax.nn.softplus(-z) - 0.5))
        a = jax.nn.sigmoid((prm['a0'][d] + a1 @ prm['a2'][d]).astype(jnp.float32))
        k_d = kf * (1.0 + (a - 1.0) * prm['k_a'])
        dirs.append((heads(decay), heads(k_d), -kk, kk * heads(a)))
    g = jax.nn.sigmoid(g1) @ prm['g2']
    return heads(r), heads(v), dirs, g

def rwkv_scans(r, v, dirs, states0):
    ys, finals = [], []
    for d, (decay, k_d, a_vec, b_vec) in enumerate(dirs):
        s_fin, y_d = wkv7_scan(states0[d], r, decay, k_d, v, a_vec, b_vec, reverse=(d == 1))
        ys.append(y_d)
        finals.append(s_fin)
    return ys[0] + ys[1], (finals[0], finals[1])

def rwkv_out(y, r, v, dirs, g, prm):
    B, L = y.shape[:2]
    mean = jnp.mean(y, axis=-1, keepdims=True)
    var = jnp.mean(jnp.square(y - mean), axis=-1, keepdims=True)
    yn = ((y - mean) * lax.rsqrt(var + LN_X_EPS)).reshape(B, L, RW_DIM) * prm['ln_w'] + prm['ln_b']
    k_sum = dirs[0][1] + dirs[1][1]
    bonus = jnp.sum(r * k_sum * prm['r_k'], axis=-1, keepdims=True) * v
    return ((yn + bonus.reshape(B, L, RW_DIM)) * g).astype(g.dtype)

def mla_qkv(p, prm, pos):
    B, L = p.shape[:2]
    q_a, kv_a, k_rope = jnp.split(p, [MLA_Q_RANK, MLA_Q_RANK + MLA_KV_RANK], axis=-1)
    q = (rmsnorm(q_a, prm['g_qa']) @ prm['w_q_up']).reshape(B, L, MLA_HEADS, MLA_QK)
    kv = (rmsnorm(kv_a, prm['g_kva']) @ prm['w_kv_up']).reshape(B, L, MLA_HEADS, MLA_NOPE + MLA_V)
    k_nope, v = kv[..., :MLA_NOPE], kv[..., MLA_NOPE:]
    k_rope = jnp.broadcast_to(k_rope[:, :, None, :], (B, L, MLA_HEADS, MLA_ROPE))
    k = jnp.concatenate([k_nope, k_rope], axis=-1)
    q = rmsnorm(q, prm['g_q'])
    k = rmsnorm(k, prm['g_k'])
    if pos is not None:
        row, col = pos
        q = jnp.concatenate([q[..., :MLA_NOPE], axial_rope(q[..., MLA_NOPE:], row, col)], axis=-1)
        k = jnp.concatenate([k[..., :MLA_NOPE], axial_rope(k[..., MLA_NOPE:], row, col)], axis=-1)
    return q, k, v

def mixer_ab(hc, hl, row, col, need_ctx, prm):
    B, S = hl.shape[:2]
    pc = hc @ prm['w_in']
    pl = hl @ prm['w_in']
    r_c, v_c, dirs_c, g_c = rwkv_prep(pc[..., :RW_COLS], prm)
    r_l, v_l, dirs_l, g_l = rwkv_prep(pl[..., :RW_COLS], prm)
    zero = jnp.zeros((B, RW_HEADS, RW_HEAD_DIM, RW_HEAD_DIM), jnp.float32)
    y_c, states_c = rwkv_scans(r_c, v_c, dirs_c, (zero, zero))
    y_l, _ = rwkv_scans(r_l, v_l, dirs_l, states_c)
    q_c, k_c, vm_c = mla_qkv(pc[..., RW_COLS:], prm, None)
    q_l, k_l, vm_l = mla_qkv(pl[..., RW_COLS:], prm, (row, col))
    scale = MLA_QK ** -0.5
    o_l = latent_attention(q_l, k_l, vm_l, k_c, vm_c, scale).reshape(B, S, MLA_HEADS * MLA_V)
    out_l = jnp.concatenate([rwkv_out(y_l, r_l, v_l, dirs_l, g_l, prm), o_l], axis=-1) @ prm['w_out']
    if not need_ctx:
        return None, out_l
    C = hc.shape[1]
    o_c = ctx_attention(q_c, k_c, vm_c, scale).reshape(B, C, MLA_HEADS * MLA_V)
    out_c = jnp.concatenate([rwkv_out(y_c, r_c, v_c, dirs_c, g_c, prm), o_c], axis=-1) @ prm['w_out']
    return out_c, out_l

def gqa_qkv(h, prm, pos):
    B, L = h.shape[:2]
    p = h @ prm['w_in']
    q, k, v = jnp.split(p, [GQA_HEADS * GQA_HEAD_DIM, (GQA_HEADS + GQA_KV_HEADS) * GQA_HEAD_DIM], axis=-1)
    q = rmsnorm(q.reshape(B, L, GQA_HEADS, GQA_HEAD_DIM), prm['g_q'])
    k = rmsnorm(k.reshape(B, L, GQA_KV_HEADS, GQA_HEAD_DIM), prm['g_k'])
    v = v.reshape(B, L, GQA_KV_HEADS, GQA_HEAD_DIM)
    if pos is not None:
        q = axial_rope(q, pos[0], pos[1])
        k = axial_rope(k, pos[0], pos[1])
    return q, k, v

def mixer_gqa(hc, hl, row, col, need_ctx, prm):
    B, S = hl.shape[:2]
    q_c, k_c, v_c = gqa_qkv(hc, prm, None)
    q_l, k_l, v_l = gqa_qkv(hl, prm, (row, col))
    scale = GQA_HEAD_DIM ** -0.5
    out_l = latent_attention(q_l, k_l, v_l, k_c, v_c, scale).reshape(B, S, GQA_HEADS * GQA_HEAD_DIM) @ prm['w_out']
    if not need_ctx:
        return None, out_l
    C = hc.shape[1]
    out_c = ctx_attention(q_c, k_c, v_c, scale).reshape(B, C, GQA_HEADS * GQA_HEAD_DIM) @ prm['w_out']
    return out_c, out_l

def moe_ffn(h, prm):
    B, L, D = h.shape
    t = h.reshape(B * L, D)
    scores = jax.nn.sigmoid((t @ prm['router_w']).astype(jnp.float32))
    grouped = (scores + prm['router_b']).reshape(-1, N_GROUPS, EXPERTS_PER_GROUP)
    group_score = jnp.sum(lax.top_k(grouped, 2)[0], axis=-1)
    grp = jnp.argmax(group_score, axis=-1)
    in_group = jnp.take_along_axis(grouped, grp[:, None, None], axis=1)[:, 0]
    _, local = lax.top_k(in_group, TOP_K)
    idx = grp[:, None] * EXPERTS_PER_GROUP + local
    wts = jnp.take_along_axis(scores, idx, axis=-1)
    wts = wts / jnp.sum(wts, axis=-1, keepdims=True)
    combine = jnp.einsum('tk,tke->te', wts, jax.nn.one_hot(idx, N_EXPERTS, dtype=jnp.float32)).astype(h.dtype)
    g = jnp.einsum('td,edf->tef', t, prm['w_gate'])
    u = jnp.einsum('td,edf->tef', t, prm['w_up'])
    y = jnp.einsum('tef,efd->td', jax.nn.silu(g) * u * combine[..., None], prm['w_down'])
    y = y + (jax.nn.silu(t @ prm['sh_gate']) * (t @ prm['sh_up'])) @ prm['sh_down']
    return y.reshape(B, L, D)

def second_inputs(seed: int = 0) -> dict:
    key = jax.random.key(seed)
    ks = iter(jax.random.split(key, 64))

    def nrm(shape, scale):
        return jax.random.normal(next(ks), shape, jnp.float32) * scale

    def unif(shape, lo, hi):
        return jax.random.uniform(next(ks), shape, jnp.float32, lo, hi)

    def gain(shape):
        return 1.0 + nrm(shape, 0.05)

    D = D_MODEL
    A, Cn = N_AB_LAYERS, N_C_LAYERS
    return {
        'x': nrm((BATCH, SEQ, D), 1.0),
        'c': nrm((BATCH, D), 1.0),
        'ctx': nrm((BATCH, CTX_LEN, D), 1.0),
        'c_ctx': nrm((D,), 1.0),
        'ada_w': nrm((DEPTH_2, D, 6 * D), 0.5 * D ** -0.5),
        'ada_b': nrm((DEPTH_2, 6 * D), 0.02),
        'norm1_g': gain((DEPTH_2, D)),
        'norm2_g': gain((DEPTH_2, D)),
        'ab_w_in': nrm((A, D, AB_IN), D ** -0.5),
        'ab_w_out': nrm((A, AB_OUT, D), AB_OUT ** -0.5),
        'rw_mu': unif((A, RW_COLS), 0.0, 1.0),
        'rw_w0': unif((A, 2, RW_DIM), -6.0, -1.0),
        'rw_w2': nrm((A, 2, DECAY_LORA, RW_DIM), 0.5 * DECAY_LORA ** -0.5),
        'rw_a0': nrm((A, 2, RW_DIM), 0.5),
        'rw_a2': nrm((A, 2, ICLR_LORA, RW_DIM), 0.5 * ICLR_LORA ** -0.5),
        'rw_k_k': 0.85 + nrm((A, RW_DIM), 0.05),
        'rw_k_a': gain((A, RW_DIM)),
        'rw_r_k': nrm((A, RW_HEADS, RW_HEAD_DIM), 0.1),
        'rw_g2': nrm((A, GATE_LORA, RW_DIM), GATE_LORA ** -0.5),
        'rw_ln_w': gain((A, RW_DIM)),
        'rw_ln_b': nrm((A, RW_DIM), 0.02),
        'mla_g_qa': gain((A, MLA_Q_RANK)),
        'mla_w_q_up': nrm((A, MLA_Q_RANK, MLA_HEADS * MLA_QK), MLA_Q_RANK ** -0.5),
        'mla_g_kva': gain((A, MLA_KV_RANK)),
        'mla_w_kv_up': nrm((A, MLA_KV_RANK, MLA_HEADS * (MLA_NOPE + MLA_V)), MLA_KV_RANK ** -0.5),
        'mla_g_q': gain((A, MLA_QK)),
        'mla_g_k': gain((A, MLA_QK)),
        'gqa_w_in': nrm((Cn, D, GQA_IN), D ** -0.5),
        'gqa_w_out': nrm((Cn, GQA_HEADS * GQA_HEAD_DIM, D), (GQA_HEADS * GQA_HEAD_DIM) ** -0.5),
        'gqa_g_q': gain((Cn, GQA_HEAD_DIM)),
        'gqa_g_k': gain((Cn, GQA_HEAD_DIM)),
        'router_w': nrm((D, N_EXPERTS), D ** -0.5),
        'router_b': nrm((N_EXPERTS,), 0.01),
        'moe_w_gate': nrm((DEPTH_2, N_EXPERTS, D, EXPERT_FF), D ** -0.5),
        'moe_w_up': nrm((DEPTH_2, N_EXPERTS, D, EXPERT_FF), D ** -0.5),
        'moe_w_down': nrm((DEPTH_2, N_EXPERTS, EXPERT_FF, D), EXPERT_FF ** -0.5),
        'shared_w_gate': nrm((DEPTH_2, D, SHARED_FF), D ** -0.5),
        'shared_w_up': nrm((DEPTH_2, D, SHARED_FF), D ** -0.5),
        'shared_w_down': nrm((DEPTH_2, SHARED_FF, D), SHARED_FF ** -0.5),
    }

def second_block(x, c, ctx, c_ctx, ada_w, ada_b, norm1_g, norm2_g, ab_w_in, ab_w_out, rw_mu, rw_w0,
              rw_w2, rw_a0, rw_a2, rw_k_k, rw_k_a, rw_r_k, rw_g2, rw_ln_w, rw_ln_b, mla_g_qa,
              mla_w_q_up, mla_g_kva, mla_w_kv_up, mla_g_q, mla_g_k, gqa_w_in, gqa_w_out, gqa_g_q,
              gqa_g_k, router_w, router_b, moe_w_gate, moe_w_up, moe_w_down, shared_w_gate,
              shared_w_up, shared_w_down):
    seq = x.shape[1]
    rows = seq // GRID_W
    row = jnp.repeat(jnp.arange(rows, dtype=jnp.float32), GRID_W)
    col = jnp.tile(jnp.arange(GRID_W, dtype=jnp.float32), rows)
    xl, xc = x, ctx
    for l in range(DEPTH_2):
        need_ctx = l < DEPTH_2 - 1
        i = l // 2
        sh1_l, sc1_l, ga1_l, sh2_l, sc2_l, ga2_l = ada_mods(c, ada_w[l], ada_b[l])
        sh1_c, sc1_c, ga1_c, sh2_c, sc2_c, ga2_c = ada_mods(c_ctx[None, :], ada_w[l], ada_b[l])
        hl = modulate(rmsnorm(xl, norm1_g[l]), sh1_l, sc1_l)
        hc = modulate(rmsnorm(xc, norm1_g[l]), sh1_c, sc1_c)
        if l % 2 == 0:
            prm = dict(w_in=ab_w_in[i], w_out=ab_w_out[i], mu=rw_mu[i], w0=rw_w0[i], w2=rw_w2[i],
                       a0=rw_a0[i], a2=rw_a2[i], k_k=rw_k_k[i], k_a=rw_k_a[i], r_k=rw_r_k[i],
                       g2=rw_g2[i], ln_w=rw_ln_w[i], ln_b=rw_ln_b[i], g_qa=mla_g_qa[i],
                       w_q_up=mla_w_q_up[i], g_kva=mla_g_kva[i], w_kv_up=mla_w_kv_up[i],
                       g_q=mla_g_q[i], g_k=mla_g_k[i])
            oc, ol = mixer_ab(hc, hl, row, col, need_ctx, prm)
        else:
            prm = dict(w_in=gqa_w_in[i], w_out=gqa_w_out[i], g_q=gqa_g_q[i], g_k=gqa_g_k[i])
            oc, ol = mixer_gqa(hc, hl, row, col, need_ctx, prm)
        moe_prm = dict(router_w=router_w, router_b=router_b, w_gate=moe_w_gate[l], w_up=moe_w_up[l],
                       w_down=moe_w_down[l], sh_gate=shared_w_gate[l], sh_up=shared_w_up[l],
                       sh_down=shared_w_down[l])
        xl = xl + ga1_l * ol
        hl = modulate(rmsnorm(xl, norm2_g[l]), sh2_l, sc2_l)
        xl = xl + ga2_l * moe_ffn(hl, moe_prm)
        if need_ctx:
            xc = xc + ga1_c * oc
            hc = modulate(rmsnorm(xc, norm2_g[l]), sh2_c, sc2_c)
            xc = xc + ga2_c * moe_ffn(hc, moe_prm)
    return xl


def setup_inputs(seed=0):
    out = dict(first_inputs(seed))
    for name, value in second_inputs(seed + 1).items():
        if name != "x":
            out[name + "_2"] = value
    return out


def reference(
    x, norm_mix, w_in, lru_conv_w, lru_conv_b, lru_w_gates, lru_b_gates, lru_lambda, sc_conv_w,
    fox_f_bias, fox_qk_norm, nsa_qk_norm, nsa_cmp_pos, nsa_cmp_w1, nsa_cmp_w2, nsa_gate_bias,
    rel_bias, out_norm, w_out, norm_ffn, w_gate_up, w_down, c_2, ctx_2, c_ctx_2, ada_w_2,
    ada_b_2, norm1_g_2, norm2_g_2, ab_w_in_2, ab_w_out_2, rw_mu_2, rw_w0_2, rw_w2_2, rw_a0_2,
    rw_a2_2, rw_k_k_2, rw_k_a_2, rw_r_k_2, rw_g2_2, rw_ln_w_2, rw_ln_b_2, mla_g_qa_2,
    mla_w_q_up_2, mla_g_kva_2, mla_w_kv_up_2, mla_g_q_2, mla_g_k_2, gqa_w_in_2, gqa_w_out_2,
    gqa_g_q_2, gqa_g_k_2, router_w_2, router_b_2, moe_w_gate_2, moe_w_up_2, moe_w_down_2,
    shared_w_gate_2, shared_w_up_2, shared_w_down_2,
):
    x = first_block(
        x, norm_mix, w_in, lru_conv_w, lru_conv_b, lru_w_gates, lru_b_gates, lru_lambda,
        sc_conv_w, fox_f_bias, fox_qk_norm, nsa_qk_norm, nsa_cmp_pos, nsa_cmp_w1, nsa_cmp_w2,
        nsa_gate_bias, rel_bias, out_norm, w_out, norm_ffn, w_gate_up, w_down,
    )
    return second_block(
        x, c_2, ctx_2, c_ctx_2, ada_w_2, ada_b_2, norm1_g_2, norm2_g_2, ab_w_in_2, ab_w_out_2,
        rw_mu_2, rw_w0_2, rw_w2_2, rw_a0_2, rw_a2_2, rw_k_k_2, rw_k_a_2, rw_r_k_2, rw_g2_2,
        rw_ln_w_2, rw_ln_b_2, mla_g_qa_2, mla_w_q_up_2, mla_g_kva_2, mla_w_kv_up_2, mla_g_q_2,
        mla_g_k_2, gqa_w_in_2, gqa_w_out_2, gqa_g_q_2, gqa_g_k_2, router_w_2, router_b_2,
        moe_w_gate_2, moe_w_up_2, moe_w_down_2, shared_w_gate_2, shared_w_up_2, shared_w_down_2,
    )


_drawn_inputs = setup_inputs


def setup_inputs(seed=0):
    import zlib

    import numpy as np

    out = dict(_drawn_inputs(seed))
    spreads = {}
    factors = {'lru_b_gates': 5.811,
     'fox_qk_norm': 3.736,
     'nsa_qk_norm': 3.867,
     'nsa_gate_bias': 8.0,
     'norm_ffn': 3.215,
     'norm1_g_2': 3.195,
     'rw_w2_2': 5.145,
     'rw_ln_w_2': 24.126,
     'rw_ln_b_2': 55.111,
     'mla_g_qa_2': 8.0,
     'mla_w_q_up_2': 2.976,
     'mla_g_kva_2': 6.112,
     'mla_g_q_2': 8.0,
     'mla_g_k_2': 8.0,
     'gqa_g_q_2': 8.0,
     'gqa_g_k_2': 8.0,
     'norm2_g_2': 3.938,
     'rw_k_k_2': 4.29,
     'router_b_2': 4.476}
    for name, (base, spread) in spreads.items():
        noise = np.random.default_rng([zlib.crc32(name.encode()), seed]).standard_normal(out[name].shape)
        drawn = base * np.exp(spread * noise) if base else spread * noise
        out[name] = jnp.asarray(drawn.astype(out[name].dtype))
    for name, factor in factors.items():
        out[name] = (out[name] * factor).astype(out[name].dtype)
    return out
```

```python
from contextlib import ExitStack, nullcontext

import numpy as np
import concourse.bass as bass
from concourse import mybir

P = 128
F32 = mybir.dt.float32
ALU = mybir.AluOpType
ACT = mybir.ActivationFunctionType
AX_X = mybir.AxisListType.X

D = 1024
KT = D // P
SEQ = 512
CTX = 256
ALLTOK = CTX + SEQ
HD = 64
GROUP = 256
D_FF = ((8 * D // 3 + 255) // 256) * 256
FF_CHUNK = 256
SLOTS = 6
SLOT_COLS = KT * 256
EPS = 1e-6
NEG = -1e30
CMP_LEN, CMP_STRIDE, CMP_HID = 32, 16, 128
N_CMP = (SEQ - CMP_LEN) // CMP_STRIDE + 1
REL_BUCKETS, REL_MAX = 32, 128
N_EXP = 16
MLA_H, MLA_QK, MLA_NOPE, MLA_ROPE, MLA_V = 8, 96, 64, 32, 64
Q_RANK, KV_RANK = 384, 256
RW_DIM = 512
GQA_H, GQA_KV = 16, 4
CH = 128
N_CH = ALLTOK // CH


class Tally:

    def __init__(self, nc, ctx):
        self.nc, self.ctx, self.sems, self.total = nc, ctx, {}, {}

    def sem(self, name):
        if name not in self.sems:
            self.sems[name] = self.ctx.enter_context(self.nc.semaphore(name))
            self.total[name] = 0
        return self.sems[name]

    def claim(self, name, n):
        self.sem(name)
        base = self.total[name]
        self.total[name] += n
        return base


class Stage:

    def __init__(self, k):
        self.k, self.nc, self.tally = len(k.stages), k.nc, k.tally
        self.kern = k
        k.stages.append(self)

    def count(self, name, n):
        return self.tally.sem(name), self.tally.claim(name, n)

    def tensor(self, pe):
        pass

    def scalar(self, act):
        pass

    def vector(self, dve):
        pass

    def gpsimd(self, pool):
        pass



def enter(stage, eng, me):
    if stage.k:
        for other in ("tensor", "scalar", "vector", "gpsimd"):
            if other != me:
                eng.wait_ge(stage.tally.sem(other + "_stage_done"), stage.k)


def leave(stage, eng, me):
    eng.drain().then_inc(stage.tally.sem(me + "_stage_done"), 1)


class Ring:

    def __init__(self):
        self.n = 0

    def take(self, n):
        first = self.n
        self.n += n
        return first


def segments(tokens):
    return [(0, CTX), (CTX, ALLTOK)] if tokens == ALLTOK else [(CTX, ALLTOK)]


class Norm(Stage):

    def __init__(self, k, src, dst, tiles, group, segs, gain, ones, shift=None):
        super().__init__(k)
        self.src, self.dst, self.tiles, self.group = src, dst, tiles, group
        self.segs, self.gain, self.ones, self.shift = segs, gain, ones, shift
        self.units = [(g, s) for s in segs for g in range(tiles // group)]
        self.squares = self.count("norm_squares", len(segs))
        self.sums = self.count("norm_sums", len(self.units))
        self.roots = self.count("norm_roots", len(self.units))
        self.scaled = self.count("norm_scaled", len(self.units))

    def bank(self, n):
        a, b = self.units[n][1]
        return self.kern.ps[n % 4][:, 0:b - a]

    def root(self, n):
        a, b = self.units[n][1]
        return self.kern.rstd[:, n % 4, 0:b - a]

    def scalar(self, act):
        nc = self.nc
        for a, b in self.segs:
            nc.scalar.activation(self.dst[:, 0:self.tiles, a:b], self.src[:, 0:self.tiles, a:b],
                                 ACT.Square).then_inc(self.squares[0], 1)
        for n in range(len(self.units)):
            act.wait_ge(self.sums[0], self.sums[1] + n + 1)
            if n >= 4:
                act.wait_ge(self.scaled[0], self.scaled[1] + n - 3)
            nc.scalar.activation(self.root(n), self.bank(n), ACT.Sqrt,
                                 bias=self.kern.eps[:, 0:1]).then_inc(self.roots[0], 1)
        if self.shift is not None:
            for n, (g, (a, b)) in enumerate(self.units):
                act.wait_ge(self.scaled[0], self.scaled[1] + n + 1)
                for t in range(g * self.group, (g + 1) * self.group):
                    nc.scalar.activation(self.dst[:, t, a:b], self.dst[:, t, a:b], ACT.Identity,
                                         bias=self.shift(t, a))

    def tensor(self, pe):
        for n, (g, (a, b)) in enumerate(self.units):
            pe.wait_ge(self.squares[0], self.squares[1] + self.segs.index((a, b)) + 1)
            if n >= 4:
                pe.wait_ge(self.roots[0], self.roots[1] + n - 3)
            for i in range(self.group):
                last = self.nc.tensor.matmul(self.bank(n), self.ones, self.dst[:, g * self.group + i, a:b],
                                             start=(i == 0), stop=(i == self.group - 1))
            last.then_inc(self.sums[0], 1)

    def vector(self, dve):
        nc = self.nc
        for n, (g, (a, b)) in enumerate(self.units):
            dve.wait_ge(self.roots[0], self.roots[1] + n + 1)
            nc.vector.reciprocal(self.root(n), self.root(n))
            dve.drain()
            for t in range(g * self.group, (g + 1) * self.group):
                last = nc.vector.scalar_tensor_tensor(
                    out=self.dst[:, t, a:b], in0=self.src[:, t, a:b], scalar=self.gain(t, a),
                    in1=self.root(n), op0=ALU.mult, op1=ALU.mult)
            last.then_inc(self.scaled[0], 1)


class Project(Stage):

    def __init__(self, k, src, segs, tiles, width, out, gate=None):
        super().__init__(k)
        self.src, self.segs, self.tiles, self.width, self.out, self.gate = src, segs, tiles, width, out, gate
        self.per = 256 // width
        self.items = -(-tiles // self.per)
        self.first = k.ring.take(self.items)
        self.used = k.tally.claim("weights_used", self.items)
        self.groups = [(t, s) for t in range(tiles) for s in segs]
        self.summed = self.count("tile_summed", len(self.groups))
        self.moved = [self.count(f"tile_moved_{e}", (len(self.groups) + 1 - e) // 2) for e in (0, 1)]

    def bank(self, n):
        a, b = self.groups[n][1]
        return self.kern.ps[n % 8][0:self.width, 0:b - a]

    def tensor(self, pe):
        n = 0
        for i in range(self.items):
            slot = self.kern.slot_ready(pe, self.first + i)
            w = slot.rearrange("p (k c) -> p k c", k=KT)
            for t in range(i * self.per, min((i + 1) * self.per, self.tiles)):
                c = (t % self.per) * self.width
                for a, b in self.segs:
                    if n >= 8:
                        s, base = self.moved[n % 2]
                        pe.wait_ge(s, base + (n - 8) // 2 + 1)
                    for kt in range(KT):
                        last = self.nc.tensor.matmul(self.bank(n), w[:, kt, c:c + self.width], self.src[:, kt, a:b],
                                                     start=(kt == 0), stop=(kt == KT - 1))
                    last.then_inc(self.summed[0], 1)
                    n += 1
            pe.drain().then_inc(self.tally.sem("weights_used"), 1)

    def move(self, eng, which):
        for n, (t, (a, b)) in enumerate(self.groups):
            if n % 2 != which:
                continue
            eng.wait_ge(self.summed[0], self.summed[1] + n + 1)
            dst = self.out(t, a, b)
            if self.gate is not None:
                g = self.gate(t, a)
                e = self.nc.vector
                ins = e.scalar_tensor_tensor(out=dst, in0=self.bank(n), scalar=g, in1=dst, op0=ALU.mult, op1=ALU.add)
            elif which:
                ins = self.nc.vector.tensor_copy(dst, self.bank(n))
            else:
                ins = self.nc.scalar.activation(dst, self.bank(n), ACT.Copy)
            ins.then_inc(self.moved[which][0], 1)

    def scalar(self, act):
        if self.gate is None:
            self.move(act, 0)

    def vector(self, dve):
        if self.gate is None:
            self.move(dve, 1)
            return
        for n in range(len(self.groups)):
            t, (a, b) = self.groups[n]
            dve.wait_ge(self.summed[0], self.summed[1] + n + 1)
            dst = self.out(t, a, b)
            self.nc.vector.scalar_tensor_tensor(out=dst, in0=self.bank(n), scalar=self.gate(t, a), in1=dst,
                                                op0=ALU.mult, op1=ALU.add).then_inc(self.moved[n % 2][0], 1)


class TokenProject(Stage):

    def __init__(self, k, src, token_tiles, cols, out):
        super().__init__(k)
        self.src, self.token_tiles, self.cols, self.out = src, token_tiles, cols, out
        self.first = k.ring.take(len(cols))
        k.tally.claim("weights_used", len(cols))
        self.groups = [(i, t) for i in range(len(cols)) for t in token_tiles]
        self.summed = self.count("rows_summed", len(self.groups))
        self.moved = self.count("rows_moved", len(self.groups))

    def bank(self, n):
        return self.kern.ps[n % 4][:, 0:self.cols[self.groups[n][0]]]

    def tensor(self, pe):
        n = 0
        for i, cols in enumerate(self.cols):
            w = self.kern.slot_ready(pe, self.first + i).rearrange("p (k c) -> p k c", k=KT)
            for t in self.token_tiles:
                if n >= 4:
                    pe.wait_ge(self.moved[0], self.moved[1] + n - 3)
                for kt in range(KT):
                    last = self.nc.tensor.matmul(self.bank(n), self.src[:, kt, t * P:(t + 1) * P], w[:, kt, 0:cols],
                                                 start=(kt == 0), stop=(kt == KT - 1))
                last.then_inc(self.summed[0], 1)
                n += 1
            pe.drain().then_inc(self.tally.sem("weights_used"), 1)

    def vector(self, dve):
        for n, (i, t) in enumerate(self.groups):
            dve.wait_ge(self.summed[0], self.summed[1] + n + 1)
            self.nc.vector.tensor_copy(self.out(t, i), self.bank(n)).then_inc(self.moved[0], 1)


class Experts(Stage):

    def __init__(self, k, src, dst, segs, chunks, gate, comb=None):
        super().__init__(k)
        self.src, self.dst, self.segs, self.chunks, self.gate, self.comb = src, dst, segs, chunks, gate, comb
        self.first = k.ring.take(3 * chunks)
        k.tally.claim("weights_used", 3 * chunks)
        u = chunks * len(segs)
        self.ns = len(segs)
        self.gu = self.count("gate_up_summed", 2 * u)
        self.sig = self.count("gate_sigmoid", 2 * u)
        self.hid = self.count("hidden_ready", 2 * u)
        self.down = self.count("down_summed", 8 * u)
        self.added = self.count("down_added", 8 * u)
        if comb is not None:
            self.sel = self.count("expert_selected", chunks)
            self.cb = self.count("combine_spread", u)

    def item(self, chunks, c, kind):
        if self.ns == 1 and chunks == 2:
            return self.first + (2 * c + kind if kind < 2 else 4 + c)
        return self.first + 3 * c + kind

    def turns(self, eng, body):
        if self.chunks > 1:
            with eng.Fori(0, self.chunks // 2) as i:
                body(i, 2)
        if self.chunks % 2:
            body(self.chunks // 2, 1)

    def gu_bank(self, which, ft):
        return self.kern.ps[2 * ft + which]

    def tensor(self, pe):
        nc, kern, ns = self.nc, self.kern, self.ns

        def body(i, chunks):
            units = [(c, s) for c in range(chunks) for s in range(ns)]

            def gate_up(v):
                c, s = units[v]
                a, b = self.segs[s]
                u = i * (2 * ns) + v
                if s == 0:
                    kern.slot_ready(pe, self.item(chunks, c, 0), turn=i)
                    kern.slot_ready(pe, self.item(chunks, c, 1), turn=i)
                    if self.comb is not None:
                        pe.wait_ge(self.sel[0], self.sel[1] + 1 + c + i * 2)
                wg = kern.slot(self.item(chunks, c, 0)).rearrange("p (k c) -> p k c", k=KT)
                wu = kern.slot(self.item(chunks, c, 1)).rearrange("p (k c) -> p k c", k=KT)
                for ft in (0, 1):
                    pe.wait_ge(self.hid[0], u * 2 + (self.hid[1] + ft - 1))
                    if ft == 1 and self.comb is not None:
                        nc.tensor.matmul(kern.ps[4][:, 0:b - a], kern.sel_buf[0:self.chunks, c, :],
                                         self.comb[0:self.chunks, a:b], start=True, stop=True).then_inc(self.cb[0], 1)
                    for which, w in ((0, wg), (1, wu)):
                        for kt in range(KT):
                            last = nc.tensor.matmul(self.gu_bank(which, ft)[:, 0:b - a], w[:, kt, ft * P:(ft + 1) * P],
                                                    self.src[:, kt, a:b], start=(kt == 0), stop=(kt == KT - 1))
                    last.then_inc(self.gu[0], 1)
                if s == ns - 1:
                    pe.drain().then_inc(self.tally.sem("weights_used"), 2)

            def down(v):
                c, s = units[v]
                a, b = self.segs[s]
                u = i * (2 * ns) + v
                if s == 0:
                    kern.slot_ready(pe, self.item(chunks, c, 2), turn=i)
                wd = kern.slot(self.item(chunks, c, 2)).rearrange("p (f n) -> p f n", f=2)
                pe.wait_ge(self.hid[0], u * 2 + (self.hid[1] + 2))
                for n in range(KT):
                    pe.wait_ge(self.added[0], u * 8 + (self.added[1] + n - (1 if n < 2 else 2)))
                    for ft in (0, 1):
                        last = nc.tensor.matmul(kern.ps[5 + n % 3][:, 0:b - a], wd[:, ft, n * P:(n + 1) * P],
                                                kern.hidden[:, v % 2, ft, 0:b - a], start=(ft == 0), stop=(ft == 1))
                    last.then_inc(self.down[0], 1)
                if s == ns - 1:
                    pe.drain().then_inc(self.tally.sem("weights_used"), 1)

            gate_up(0)
            for v in range(1, len(units)):
                gate_up(v)
                down(v - 1)
            down(len(units) - 1)

        self.turns(pe, body)

    def scalar(self, act):
        nc, kern, ns = self.nc, self.kern, self.ns

        def body(i, chunks):
            for v in range(chunks * ns):
                c, s = divmod(v, ns)
                a, b = self.segs[s]
                u = i * (2 * ns) + v
                if s == 0 and self.comb is not None:
                    act.wait_ge(self.cb[0], u + (self.cb[1] - ns))
                    nc.scalar.activation(kern.sel_buf[0:self.chunks, c, :],
                                         kern.sel_rows[0:self.chunks, bass.ds((i * 2 + c) * P, P)],
                                         ACT.Copy).then_inc(self.sel[0], 1)
                for ft in (0, 1):
                    act.wait_ge(self.gu[0], u * 2 + (self.gu[1] + ft + 1))
                    act.wait_ge(self.hid[0], u * 2 + (self.hid[1] + ft - 1))
                    nc.scalar.activation(kern.sigm[:, ft, 0:b - a], self.gu_bank(0, ft)[:, 0:b - a],
                                         ACT.Sigmoid).then_inc(self.sig[0], 1)

        self.turns(act, body)

    def vector(self, dve):
        nc, kern, ns = self.nc, self.kern, self.ns

        def body(i, chunks):
            units = [(c, s) for c in range(chunks) for s in range(ns)]

            def hidden(v):
                a, b = self.segs[units[v][1]]
                u = i * (2 * ns) + v
                for ft in (0, 1):
                    dve.wait_ge(self.sig[0], u * 2 + (self.sig[1] + ft + 1))
                    h, n = kern.hidden[:, v % 2, ft, 0:b - a], b - a
                    nc.vector.tensor_tensor(out=kern.sigm[:, ft, 0:n], in0=kern.sigm[:, ft, 0:n],
                                            in1=self.gu_bank(0, ft)[:, 0:n], op=ALU.mult)
                    dve.drain()
                    if self.comb is None:
                        nc.vector.tensor_tensor(out=h, in0=kern.sigm[:, ft, 0:n], in1=self.gu_bank(1, ft)[:, 0:n],
                                                op=ALU.mult).then_inc(self.hid[0], 1)
                        continue
                    nc.vector.tensor_tensor(out=kern.sigm[:, ft, 0:n], in0=kern.sigm[:, ft, 0:n],
                                            in1=self.gu_bank(1, ft)[:, 0:n], op=ALU.mult)
                    dve.drain()
                    dve.wait_ge(self.cb[0], u + (self.cb[1] + 1))
                    nc.vector.tensor_tensor(out=h, in0=kern.sigm[:, ft, 0:n], in1=kern.ps[4][:, 0:n],
                                            op=ALU.mult).then_inc(self.hid[0], 1)

            def add(v):
                a, b = self.segs[units[v][1]]
                u = i * (2 * ns) + v
                for n in range(KT):
                    dve.wait_ge(self.down[0], u * 8 + (self.down[1] + n + 1))
                    nc.vector.scalar_tensor_tensor(
                        out=self.dst[:, n, a:b], in0=kern.ps[5 + n % 3][:, 0:b - a], scalar=self.gate(n, a),
                        in1=self.dst[:, n, a:b], op0=ALU.mult, op1=ALU.add).then_inc(self.added[0], 1)

            hidden(0)
            for v in range(1, len(units)):
                hidden(v)
                add(v - 1)
            add(len(units) - 1)

        self.turns(dve, body)


class HeadNorm(Stage):

    def __init__(self, k, units, ones, d, eps=None):
        super().__init__(k)
        self.units, self.ones, self.d = units, ones, d
        self.eps = k.eps if eps is None else eps
        n = len(units)
        self.sq = self.count("head_squares", n)
        self.sum = self.count("head_sums", n)
        self.root = self.count("head_roots", n)
        self.done = self.count("head_normed", n)

    def scalar(self, act):
        nc, kern, d = self.nc, self.kern, self.d
        for n in range(len(self.units) + 1):
            if n < len(self.units):
                x = self.units[n][0]
                if n >= 2:
                    act.wait_ge(self.sum[0], self.sum[1] + n - 1)
                nc.scalar.activation(kern.scratch[0:d, n % 2, 0:x.shape[-1]], x, ACT.Square).then_inc(self.sq[0], 1)
            if n >= 1:
                m = n - 1
                w = self.units[m][0].shape[-1]
                act.wait_ge(self.sum[0], self.sum[1] + m + 1)
                if m >= 2:
                    act.wait_ge(self.done[0], self.done[1] + m - 1)
                nc.scalar.activation(kern.scratch[0:d, 2 + m % 2, 0:w], kern.ps[m % 4][0:d, 0:w], ACT.Sqrt,
                                     bias=self.eps[0:d, 0:1]).then_inc(self.root[0], 1)

    def tensor(self, pe):
        kern, d = self.kern, self.d
        for n, (x, _) in enumerate(self.units):
            w = x.shape[-1]
            pe.wait_ge(self.sq[0], self.sq[1] + n + 1)
            if n >= 4:
                pe.wait_ge(self.root[0], self.root[1] + n - 3)
            self.nc.tensor.matmul(kern.ps[n % 4][0:d, 0:w], self.ones, kern.scratch[0:d, n % 2, 0:w],
                                  start=True, stop=True).then_inc(self.sum[0], 1)

    def vector(self, dve):
        kern, d = self.kern, self.d
        for n, (x, gain) in enumerate(self.units):
            r = kern.scratch[0:d, 2 + n % 2, 0:x.shape[-1]]
            dve.wait_ge(self.root[0], self.root[1] + n + 1)
            self.nc.vector.reciprocal(r, r)
            dve.drain()
            self.nc.vector.scalar_tensor_tensor(out=x, in0=x, scalar=gain, in1=r, op0=ALU.mult,
                                                op1=ALU.mult).then_inc(self.done[0], 1)


class Rope(Stage):

    def __init__(self, k, units, rot_t, cos, sin, d):
        super().__init__(k)
        self.units, self.rot_t, self.cos, self.sin, self.d = units, rot_t, cos, sin, d
        self.rot = self.count("rope_rotated", len(units))
        self.done = self.count("rope_done", len(units))

    def tensor(self, pe):
        for n, x in enumerate(self.units):
            if n >= 4:
                pe.wait_ge(self.done[0], self.done[1] + n - 3)
            self.nc.tensor.matmul(self.kern.ps[n % 4][0:self.d, :], self.rot_t, x, start=True,
                                  stop=True).then_inc(self.rot[0], 1)

    def vector(self, dve):
        v, d = self.nc.vector, self.d
        for n, x in enumerate(self.units):
            t = self.kern.scratch[0:d, n % 2, :]
            dve.wait_ge(self.rot[0], self.rot[1] + n + 1)
            v.tensor_tensor(out=t, in0=self.kern.ps[n % 4][0:d, :], in1=self.sin, op=ALU.mult)
            v.tensor_tensor(out=x, in0=x, in1=self.cos, op=ALU.mult)
            dve.drain()
            v.tensor_tensor(out=x, in0=x, in1=t, op=ALU.add).then_inc(self.done[0], 1)


class Attention(Stage):

    def __init__(self, k, d, keys, kv_heads, per_kv, q_tiles, q, key, value, out, bias=None, factor=None, add=False):
        super().__init__(k)
        self.d, self.keys, self.hk, self.g, self.nt = d, keys, kv_heads, per_kv, q_tiles
        self.q, self.key, self.value, self.out, self.bias, self.factor, self.add = q, key, value, out, bias, factor, add
        self.biased, self.probs, self.probs_t = k.biased, k.probs, k.probs_t
        self.per = per_kv * q_tiles
        n = kv_heads * self.per
        names = ("q_staged", "scores_summed", "max_ready", "exp_done", "probs_turned", "probs_copied", "pv_summed",
                 "head_out")
        (self.staged, self.scores, self.maxed, self.exped, self.turned, self.copied, self.pv,
         self.outed) = (self.count(x, n) for x in names)
        self.kts = [(i, min(P, keys - i * P)) for i in range(-(-keys // P))]

    def units(self, hk):
        for v in range(self.per):
            yield hk * self.g + v // self.nt, v % self.nt, hk * self.per + v, v % 2

    def s_psum(self, par):
        return self.kern.psum[:, 2 * par:2 * par + 2, :].rearrange("p a b -> p (a b)")[:, 0:self.keys]

    def tensor(self, pe):
        nc, kern = self.nc, self.kern
        pt = kern.psum[:, 4:6, :].rearrange("p a b -> p (a b)")

        def scores(hk, u, par):
            pe.wait_ge(self.staged[0], u + (self.staged[1] + 1))
            s = self.s_psum(par)
            for a in range(0, self.keys, 512):
                b = min(a + 512, self.keys)
                last = nc.tensor.matmul(s[:, a:b], kern.q_stage[0:self.d, par, :], self.key(hk, a, b),
                                        start=True, stop=True)
            last.then_inc(self.scores[0], 1)

        def turn(hk, ahead):
            for v, (h, t, u, par) in enumerate(self.units(hk)):
                pe.wait_ge(self.exped[0], u + (self.exped[1] + 1))
                pe.wait_ge(self.copied[0], u + self.copied[1])
                for i, n in self.kts:
                    last = nc.tensor.transpose(pt[0:n, i * P:i * P + P], self.probs[:, par, i * P:i * P + n],
                                               kern.ident)
                last.then_inc(self.turned[0], 1)
                if ahead or v + 2 < self.per:
                    scores(hk + (v + 2) // self.per, u + 2, par)
                pe.wait_ge(self.copied[0], u + (self.copied[1] + 1))
                pe.wait_ge(self.outed[0], u + (self.outed[1] - 1))
                for i, n in self.kts:
                    last = nc.tensor.matmul(kern.ps[6 + par][:, 0:HD], self.probs_t[0:n, par, i * P:(i + 1) * P],
                                            self.value(i, n, hk), start=(i == 0), stop=(i == len(self.kts) - 1))
                last.then_inc(self.pv[0], 1)

        scores(0, 0, 0)
        scores(0, 1, 1)
        with pe.Fori(0, self.hk - 1) as hk:
            turn(hk, True)
        turn(self.hk - 1, False)

    def gpsimd(self, pool):
        with pool.Fori(0, self.hk) as hk:
            for h, t, u, par in self.units(hk):
                pool.wait_ge(self.scores[0], u + (self.scores[1] - 1))
                self.nc.gpsimd.tensor_copy(self.kern.q_stage[0:self.d, par, :], self.q(h, t)).then_inc(self.staged[0], 1)

    def scalar(self, act):
        nc, kern = self.nc, self.kern
        pt = kern.psum[:, 4:6, :].rearrange("p a b -> p (a b)")

        def exponentials(u, par):
            act.wait_ge(self.maxed[0], u + (self.maxed[1] + 1))
            act.wait_ge(self.outed[0], u + (self.outed[1] - 1))
            src = self.s_psum(par) if self.bias is None else self.biased[:, par, 0:self.keys]
            nc.scalar.activation(self.probs[:, par, 0:self.keys], src, ACT.Exp, bias=kern.neg_max[:, par:par + 1],
                                 accum_out=kern.row_sum[:, par:par + 1]).then_inc(self.exped[0], 1)

        def copy(u, par):
            act.wait_ge(self.turned[0], u + (self.turned[1] + 1))
            act.wait_ge(self.pv[0], u + (self.pv[1] - 1))
            n = self.kts[0][1]
            w = len(self.kts) * P
            nc.scalar.activation(self.probs_t[0:n, par, 0:w], pt[0:n, 0:w], ACT.Copy).then_inc(self.copied[0], 1)

        def turn(hk, ahead):
            for v, (h, t, u, par) in enumerate(self.units(hk)):
                copy(u, par)
                if ahead or v + 1 < self.per:
                    exponentials(u + 1, 1 - par)

        exponentials(0, 0)
        with act.Fori(0, self.hk - 1) as hk:
            turn(hk, True)
        turn(self.hk - 1, False)

    def vector(self, dve):
        nc, kern = self.nc, self.kern

        def maximum(h, t, u, par):
            dve.wait_ge(self.scores[0], u + (self.scores[1] + 1))
            src = self.s_psum(par)
            if self.bias is not None:
                nc.vector.tensor_tensor(out=self.biased[:, par, 0:self.keys], in0=src, in1=self.bias(h, t), op=ALU.add)
                dve.drain()
                src = self.biased[:, par, 0:self.keys]
            nc.vector.reduce_max(kern.row_max[:, par:par + 1], src, AX_X)
            dve.drain()
            nc.vector.tensor_scalar(kern.neg_max[:, par:par + 1], kern.row_max[:, par:par + 1], -1.0, None,
                                    ALU.mult).then_inc(self.maxed[0], 1)

        def output(h, t, u, par):
            dve.wait_ge(self.pv[0], u + (self.pv[1] + 1))
            r, o = kern.row_inv[:, par:par + 1], kern.ps[6 + par][:, 0:HD]
            nc.vector.reciprocal(r, kern.row_sum[:, par:par + 1])
            dve.drain()
            if self.factor is not None:
                nc.vector.tensor_tensor(out=r, in0=r, in1=self.factor(h, t), op=ALU.mult)
                dve.drain()
            dst = self.out(h, t)
            if self.add:
                ins = nc.vector.scalar_tensor_tensor(out=dst, in0=o, scalar=r, in1=dst, op0=ALU.mult, op1=ALU.add)
            else:
                ins = nc.vector.tensor_scalar(dst, o, r, None, ALU.mult)
            ins.then_inc(self.outed[0], 1)

        def turn(hk, ahead):
            units = list(self.units(hk)) + (list(self.units(hk + 1))[0:2] if ahead else [])
            for v in range(self.per):
                if v + 2 < len(units):
                    maximum(*units[v + 2])
                output(*units[v])

        first = list(self.units(0))
        maximum(*first[0])
        maximum(*first[1])
        with dve.Fori(0, self.hk - 1) as hk:
            turn(hk, True)
        turn(self.hk - 1, False)


class Turn(Stage):

    def __init__(self, k, groups):
        super().__init__(k)
        self.groups = groups
        self.turned = self.count("blocks_turned", len(groups))
        self.moved = self.count("blocks_moved", len(groups))

    def tensor(self, pe):
        for n, (blocks, _) in enumerate(self.groups):
            if n >= 4:
                pe.wait_ge(self.moved[0], self.moved[1] + n - 3)
            for i, x in enumerate(blocks):
                last = self.nc.tensor.transpose(self.kern.ps[n % 4][:, i * P:(i + 1) * P], x, self.kern.ident)
            last.then_inc(self.turned[0], 1)

    def scalar(self, act):
        for n, (blocks, dst) in enumerate(self.groups):
            act.wait_ge(self.turned[0], self.turned[1] + n + 1)
            self.nc.scalar.activation(dst, self.kern.ps[n % 4][:, 0:P * len(blocks)],
                                      ACT.Copy).then_inc(self.moved[0], 1)


class FromHbm(Stage):

    def __init__(self, k, pairs):
        super().__init__(k)
        self.pairs = pairs
        self.arrived = self.count("extra_arrived", 16 * len(pairs))

    def gpsimd(self, pool):
        for dst, src in self.pairs:
            pool.dma_start(dst, src).then_inc(self.arrived[0], 16)
        pool.wait_ge(self.arrived[0], self.arrived[1] + 16 * len(self.pairs))


class ConvMixers(Stage):

    def __init__(self, k, z, y, work):
        super().__init__(k)
        self.z, self.y = z, y
        self.xc, self.r, self.i, self.b, self.t, self.g = (work[:, n * 1024:(n + 1) * 1024].rearrange(
            "p (c t) -> p c t", c=2) for n in range(6))
        self.v = self.count("mixer_vector", 5)
        self.a = self.count("mixer_scalar", 5)
        self.p = self.count("mixer_gates", 1)

    def conv(self, dve, out, x, taps, w, lo):
        for sh in range(lo, taps):
            self.nc.vector.scalar_tensor_tensor(out=out[:, sh:SEQ], in0=x[:, 0:SEQ - sh], scalar=w(taps - 1 - sh),
                                                in1=out[:, sh:SEQ], op0=ALU.mult, op1=ALU.add)
            dve.drain()

    def vector(self, dve):
        v, C, z, sm = self.nc.vector, self.kern.const, self.z, self.kern.small
        for c in (0, 1):
            v.tensor_scalar(self.xc[:, c, :], z[:, c, :], C("lru_cw", c * 4 + 3), C("lru_cb", c), ALU.mult, ALU.add)
            dve.drain()
            self.conv(dve, self.xc[:, c, :], z[:, c, :], 4, lambda i, c=c: C("lru_cw", c * 4 + i), 1)
        lam = C("lru_lam", 0, 2)
        v.tensor_scalar(sm[:, 0:2], lam, -1.0, None, ALU.mult)
        dve.drain()
        v.tensor_tensor(out=sm[:, 2:4], in0=sm[:, 0:2], in1=lam, op=ALU.max)
        v.tensor_scalar(sm[:, 4:6], sm[:, 0:2], 0.0, None, ALU.max)
        dve.drain().then_inc(self.v[0], 1)
        for c in (0, 1):
            u = self.t[:, c, :]
            v.tensor_tensor(out=u, in0=z[:, 6 + c, :], in1=z[:, 8 + c, :], op=ALU.mult)
            dve.drain()
            s = self.g[:, c, :]
            v.tensor_scalar(s, u, C("sc_w", c * 3 + 2), None, ALU.mult)
            dve.drain()
            self.conv(dve, s, u, 3, lambda i, c=c: C("sc_w", c * 3 + i), 1)
            v.tensor_tensor(out=self.y[:, 2 + c, :], in0=s, in1=z[:, 4 + c, :], op=ALU.mult)
            dve.drain()
        dve.wait_ge(self.a[0], self.a[1] + 1)
        v.tensor_tensor(out=sm[:, 8:10], in0=sm[:, 4:6], in1=sm[:, 6:8], op=ALU.add)
        dve.drain()
        v.tensor_scalar(sm[:, 8:10], sm[:, 8:10], -8.0, None, ALU.mult)
        dve.drain()
        dve.wait_ge(self.a[0], self.a[1] + 2)
        for c in (0, 1):
            v.tensor_scalar(self.r[:, c, :], self.r[:, c, :], sm[:, 8 + c:9 + c], None, ALU.mult)
            v.tensor_tensor(out=self.i[:, c, :], in0=self.i[:, c, :], in1=self.xc[:, c, :], op=ALU.mult)
        dve.drain().then_inc(self.v[0], 1)
        dve.wait_ge(self.a[0], self.a[1] + 3)
        v.tensor_scalar(self.b[:, :, :], self.t[:, :, :], 1.0, None, ALU.add)
        dve.drain()
        v.reciprocal(self.b[:, :, :], self.b[:, :, :])
        dve.drain()
        v.tensor_tensor(out=self.b[:, :, :], in0=self.b[:, :, :], in1=self.t[:, :, :], op=ALU.mult)
        dve.drain().then_inc(self.v[0], 1)
        dve.wait_ge(self.a[0], self.a[1] + 4)
        v.tensor_tensor(out=self.b[:, :, :], in0=self.b[:, :, :], in1=self.i[:, :, :], op=ALU.mult)
        dve.drain()
        for c in (0, 1):
            v.tensor_tensor_scan(self.t[:, c, :], self.xc[:, c, :], self.b[:, c, :], 0.0, ALU.mult, ALU.add)
        dve.drain()
        dve.wait_ge(self.a[0], self.a[1] + 5)
        for c in (0, 1):
            v.tensor_tensor(out=self.y[:, c, :], in0=self.t[:, c, :], in1=self.g[:, c, :], op=ALU.mult)

    def tensor(self, pe):
        pe.wait_ge(self.v[0], self.v[1] + 1)
        for n in range(4):
            last = self.nc.tensor.matmul(self.kern.ps[n][:, :], self.kern.const("lru_wg", n * P, P),
                                         self.xc[:, n % 2, :], start=True, stop=True)
        last.then_inc(self.p[0], 1)

    def scalar(self, act):
        s, C, sm = self.nc.scalar, self.kern.const, self.kern.small
        act.wait_ge(self.v[0], self.v[1] + 1)
        s.activation(sm[:, 6:8], sm[:, 2:4], ACT.Exp, scale=-1.0)
        act.drain()
        s.activation(sm[:, 6:8], sm[:, 6:8], ACT.Ln, bias=self.kern.one[:, 0:1])
        act.drain().then_inc(self.a[0], 1)
        act.wait_ge(self.p[0], self.p[1] + 1)
        for n in range(4):
            dst = (self.r if n < 2 else self.i)[:, n % 2, :]
            s.activation(dst, self.kern.ps[n][:, :], ACT.Sigmoid, bias=C("lru_gb", n))
        act.drain().then_inc(self.a[0], 1)
        act.wait_ge(self.v[0], self.v[1] + 2)
        s.activation(self.xc[:, :, :], self.r[:, :, :], ACT.Exp)
        s.activation(self.t[:, :, :], self.r[:, :, :], ACT.Tanh, scale=-1.0)
        act.drain().then_inc(self.a[0], 1)
        act.wait_ge(self.v[0], self.v[1] + 3)
        s.activation(self.b[:, :, :], self.b[:, :, :], ACT.Sqrt, scale=2.0)
        act.drain().then_inc(self.a[0], 1)
        s.activation(self.g[:, :, :], self.z[:, 2:4, :], ACT.Gelu_apprx_tanh)
        act.drain().then_inc(self.a[0], 1)


class FoxRows(Stage):

    def __init__(self, k, toks, rows):
        super().__init__(k)
        self.toks, self.rows = toks, rows
        self.turned = self.count("fox_turned", 1)

    def tensor(self, pe):
        for t in range(SEQ // P):
            last = self.nc.tensor.transpose(self.kern.ps[0][0:4, t * P:(t + 1) * P], self.toks[:, t, 396:400],
                                            self.kern.ident)
        last.then_inc(self.turned[0], 1)

    def scalar(self, act):
        act.wait_ge(self.turned[0], self.turned[1] + 1)
        self.nc.scalar.activation(self.rows, self.kern.ps[0][0:4, :], ACT.Copy)


class Clear(Stage):

    def __init__(self, k, parts):
        super().__init__(k)
        self.parts = parts

    def gpsimd(self, pool):
        for x in self.parts:
            self.nc.gpsimd.memset(x, 0.0)


class Scale(Stage):

    def __init__(self, k, items):
        super().__init__(k)
        self.items = items

    def vector(self, dve):
        for dst, src, factor in self.items:
            self.nc.vector.tensor_scalar(dst, src, factor, None, ALU.mult)


class FoxGates(Stage):

    def __init__(self, k, f, q_rows, k_rows, work):
        super().__init__(k)
        self.f, self.q_rows, self.k_rows = f, q_rows, k_rows
        self.x, self.e, self.c = (work[0:4, n * SEQ:(n + 1) * SEQ] for n in range(3))
        self.one = work[0:4, 3 * SEQ:4 * SEQ]
        self.v = self.count("fox_vector", 2)
        self.a = self.count("fox_scalar", 1)
        self.stored = self.count("fox_rows_stored", 64)

    def vector(self, dve):
        v = self.nc.vector
        v.memset(self.one, 1.0)
        v.tensor_scalar(self.f, self.f, self.kern.const("fox_fb", 0)[0:4, :], None, ALU.add)
        dve.drain()
        v.tensor_scalar(self.x, self.f, -1.0, None, ALU.mult)
        dve.drain()
        v.tensor_tensor(out=self.x, in0=self.x, in1=self.f, op=ALU.max)
        v.tensor_scalar(self.f, self.f, 0.0, None, ALU.min)
        dve.drain().then_inc(self.v[0], 1)
        dve.wait_ge(self.a[0], self.a[1] + 1)
        v.tensor_tensor(out=self.f, in0=self.f, in1=self.e, op=ALU.subtract)
        dve.drain()
        v.tensor_tensor_scan(self.c, self.one, self.f, 0.0, ALU.mult, ALU.add)
        dve.drain()
        v.tensor_scalar(self.x, self.c, -1.0, None, ALU.mult)
        dve.drain().then_inc(self.v[0], 1)

    def scalar(self, act):
        s = self.nc.scalar
        act.wait_ge(self.v[0], self.v[1] + 1)
        s.activation(self.e, self.x, ACT.Exp, scale=-1.0)
        act.drain()
        s.activation(self.e, self.e, ACT.Ln, bias=self.kern.one[0:4, 0:1])
        act.drain().then_inc(self.a[0], 1)

    def gpsimd(self, pool):
        pool.wait_ge(self.v[0], self.v[1] + 2)
        for dst, src in ((self.q_rows[0], self.c), (self.q_rows[1], self.one), (self.k_rows[0], self.one),
                         (self.k_rows[1], self.x)):
            pool.dma_start(dst, src).then_inc(self.stored[0], 16)
        pool.wait_ge(self.stored[0], self.stored[1] + 64)


class Compress(Stage):

    def __init__(self, k, xk, xv, w1, w2, pos, kc, vc, work):
        super().__init__(k)
        self.x, self.w1, self.w2, self.pos, self.kc, self.vc = (xk, xv), w1, w2, pos, kc, vc
        n = CMP_LEN * 32
        self.blocks = [work[0:HD, j * n:(j + 1) * n].rearrange("p (l n) -> p l n", n=32) for j in (0, 1)]
        self.hid = [work[:, 2 * n + j * 32:2 * n + (j + 1) * 32] for j in (0, 1)]
        self.v = self.count("compress_blocks", 2)
        self.p = self.count("compress_summed", 4)
        self.a = self.count("compress_hidden", 2)

    def vector(self, dve):
        v = self.nc.vector
        for j in (0, 1):
            for l in range(CMP_LEN):
                x = self.x[j][:, l:l + CMP_STRIDE * (N_CMP - 1) + 1:CMP_STRIDE]
                last = v.tensor_scalar(self.blocks[j][:, l, 0:N_CMP], x, self.pos[:, j * CMP_LEN + l:j * CMP_LEN + l + 1],
                                       None, ALU.add)
            last.then_inc(self.v[0], 1)
        dve.wait_ge(self.p[0], self.p[1] + 4)
        v.tensor_copy(self.kc, self.kern.ps[2][0:HD, 0:N_CMP])
        v.tensor_copy(self.vc, self.kern.ps[3][0:N_CMP, 0:HD])

    def tensor(self, pe):
        t = self.nc.tensor
        for j in (0, 1):
            pe.wait_ge(self.v[0], self.v[1] + j + 1)
            for l in range(CMP_LEN):
                last = t.matmul(self.kern.ps[j][:, 0:N_CMP], self.w1[j][:, l, :], self.blocks[j][:, l, 0:N_CMP],
                                start=(l == 0), stop=(l == CMP_LEN - 1))
            last.then_inc(self.p[0], 1)
        pe.wait_ge(self.a[0], self.a[1] + 1)
        t.matmul(self.kern.ps[2][0:HD, 0:N_CMP], self.w2[:, 0, :], self.hid[0][:, 0:N_CMP], start=True,
                 stop=True).then_inc(self.p[0], 1)
        pe.wait_ge(self.a[0], self.a[1] + 2)
        t.matmul(self.kern.ps[3][0:N_CMP, 0:HD], self.hid[1][:, 0:N_CMP], self.w2[:, 1, :], start=True,
                 stop=True).then_inc(self.p[0], 1)

    def scalar(self, act):
        for j in (0, 1):
            act.wait_ge(self.p[0], self.p[1] + j + 1)
            self.nc.scalar.activation(self.hid[j][:, 0:N_CMP], self.kern.ps[j][:, 0:N_CMP],
                                      ACT.Gelu_apprx_tanh).then_inc(self.a[0], 1)


class NsaGates(Stage):

    def __init__(self, k, gates):
        super().__init__(k)
        self.gates = gates
        self.v = self.count("nsa_biased", 1)
        self.a = self.count("nsa_gates", 1)

    def vector(self, dve):
        for t in range(SEQ // P):
            last = self.nc.vector.tensor_tensor(out=self.gates[:, t, :], in0=self.gates[:, t, :],
                                                in1=self.kern.const("nsa_gb", 0, 12), op=ALU.add)
        last.then_inc(self.v[0], 1)
        dve.wait_ge(self.a[0], self.a[1] + 1)
        self.nc.vector.tensor_scalar(self.gates[:, 0, 0:4], self.gates[:, 0, 0:4], self.kern.const("cmp_valid", 0),
                                     None, ALU.mult)

    def scalar(self, act):
        act.wait_ge(self.v[0], self.v[1] + 1)
        self.nc.scalar.activation(self.gates, self.gates, ACT.Sigmoid).then_inc(self.a[0], 1)


class RelBias(Stage):

    def __init__(self, k, onehot, onehot_fwd, rel, r, line, toe, cmp_bias):
        super().__init__(k)
        self.onehot, self.fwd, self.rel, self.r, self.line, self.toe, self.cmp_bias = (
            onehot, onehot_fwd, rel, r, line, toe, cmp_bias)
        self.p = self.count("bias_summed", 2)
        self.a = self.count("bias_rows", 1)
        self.moved = self.count("bias_moved", 128)

    def tensor(self, pe):
        t = self.nc.tensor
        for c in (0, 1):
            last = t.matmul(self.kern.ps[c][0:4, :], self.rel, self.onehot[:, c * 512:(c + 1) * 512], start=True, stop=True)
        last.then_inc(self.p[0], 1)
        for tile in range(SEQ // P):
            for n in range(N_CMP):
                at = P * tile - CMP_STRIDE * n - (CMP_LEN - 1) + (SEQ - 1)
                last = t.matmul(self.kern.ps[2 + tile][:, n * 4:n * 4 + 4], self.fwd[:, at:at + P], self.rel,
                                start=True, stop=True)
        last.then_inc(self.p[0], 1)

    def scalar(self, act):
        act.wait_ge(self.p[0], self.p[1] + 1)
        for c in (0, 1):
            self.nc.scalar.activation(self.r[:, c * 512:(c + 1) * 512], self.kern.ps[c][0:4, :], ACT.Copy)
        act.drain().then_inc(self.a[0], 1)

    def vector(self, dve):
        dve.wait_ge(self.p[0], self.p[1] + 2)
        for tile in range(SEQ // P):
            for h in range(4):
                self.nc.vector.tensor_copy(self.cmp_bias[:, tile, h, 0:N_CMP],
                                           self.kern.ps[2 + tile][:, h:4 * N_CMP:4])

    def gpsimd(self, pool):
        pool.wait_ge(self.a[0], self.a[1] + 1)
        for h in range(4):
            src = self.r[h:h + 1, :].rearrange("h (a x) -> h a x", a=1).broadcast_to([1, P, 1024])
            pool.dma_start(self.line[h:h + 1, :, :], src).then_inc(self.moved[0], 16)
        pool.wait_ge(self.moved[0], self.moved[1] + 64)
        for h in range(4):
            src = bass.AP(tensor=self.line.tensor, offset=h * P * 1024 + P - 1, ap=[[1023, P], [1, 896]])
            pool.dma_start(self.toe[:, h, :], src).then_inc(self.moved[0], 16)
        pool.wait_ge(self.moved[0], self.moved[1] + 128)


class Ada(Stage):

    def __init__(self, k, c_t, mod, bias):
        super().__init__(k)
        self.c_t, self.mod, self.bias = c_t, mod, bias
        self.tiles = 6 * D // P
        self.items = self.tiles // 2
        self.first = k.ring.take(self.items)
        k.tally.claim("weights_used", self.items)
        self.summed = self.count("ada_summed", 1)

    def tensor(self, pe):
        kern = self.kern
        with pe.Fori(0, self.items // SLOTS) as i:
            for j in range(SLOTS):
                w = kern.slot_ready(pe, self.first + j, turn=i).rearrange("p (k c) -> p k c", k=KT)
                for m in (0, 1):
                    out = kern.ps[0][:, bass.ds(i * (4 * SLOTS) + (4 * j + 2 * m), 2)]
                    for kt in range(KT):
                        self.nc.tensor.matmul(out, w[:, kt, m * P:(m + 1) * P], self.c_t[:, kt, :], start=(kt == 0),
                                              stop=(kt == KT - 1))
                pe.drain().then_inc(self.tally.sem("weights_used"), 1)
        pe.drain().then_inc(self.summed[0], 1)

    def vector(self, dve):
        dve.wait_ge(self.summed[0], self.summed[1] + 1)
        for s in (0, 1):
            self.nc.vector.tensor_tensor(out=self.mod[:, :, s], in0=self.kern.ps[0][:, s:2 * self.tiles:2],
                                         in1=self.bias, op=ALU.add)


class Silu(Stage):

    def __init__(self, k, x, tmp):
        super().__init__(k)
        self.x, self.tmp = x, tmp
        self.a = self.count("silu_sigmoid", 1)

    def scalar(self, act):
        self.nc.scalar.activation(self.tmp, self.x, ACT.Sigmoid).then_inc(self.a[0], 1)

    def vector(self, dve):
        dve.wait_ge(self.a[0], self.a[1] + 1)
        self.nc.vector.tensor_tensor(out=self.x, in0=self.x, in1=self.tmp, op=ALU.mult)


class ModGains(Stage):

    def __init__(self, k, items):
        super().__init__(k)
        self.items = items

    def vector(self, dve):
        for dst, scale, g in self.items:
            for s in (0, 1):
                self.nc.vector.scalar_tensor_tensor(out=dst[:, :, s], in0=scale[:, :, s], scalar=1.0, in1=g,
                                                    op0=ALU.add, op1=ALU.mult)


class LocalProject(Stage):

    def __init__(self, k, groups):
        super().__init__(k)
        self.groups = groups
        self.summed = self.count("local_summed", len(groups))
        self.moved = [self.count(f"local_moved_{e}", (len(groups) + 1 - e) // 2) for e in (0, 1)]

    def bank(self, n):
        dst = self.groups[n][1]
        return self.kern.ps[n % 8][0:dst.shape[0], 0:dst.shape[-1]]

    def tensor(self, pe):
        for n, (pairs, _) in enumerate(self.groups):
            if n >= 8:
                s, base = self.moved[n % 2]
                pe.wait_ge(s, base + (n - 8) // 2 + 1)
            for i, (w, x) in enumerate(pairs):
                last = self.nc.tensor.matmul(self.bank(n), w, x, start=(i == 0), stop=(i == len(pairs) - 1))
            last.then_inc(self.summed[0], 1)

    def move(self, eng, which):
        for n in range(which, len(self.groups), 2):
            eng.wait_ge(self.summed[0], self.summed[1] + n + 1)
            dst = self.groups[n][1]
            if which:
                ins = self.nc.vector.tensor_copy(dst, self.bank(n))
            else:
                ins = self.nc.scalar.activation(dst, self.bank(n), ACT.Copy)
            ins.then_inc(self.moved[which][0], 1)

    def scalar(self, act):
        self.move(act, 0)

    def vector(self, dve):
        self.move(dve, 1)


class ShiftMix(Stage):

    def __init__(self, k, p, tiles, mu, tmp, tanh, sigm):
        super().__init__(k)
        self.p, self.tiles, self.mu, self.tmp, self.tanh, self.sigm = p, tiles, mu, tmp, tanh, sigm
        self.v = self.count("shift_mixed", 1)

    def vector(self, dve):
        v = self.nc.vector
        for j in range(self.tiles):
            x, t = self.p[:, j, :], self.tmp[:, j % 2, :]
            for a, b in segments(ALLTOK):
                v.tensor_tensor(out=t[:, a + 1:b - 1], in0=x[:, a:b - 2], in1=x[:, a + 2:b], op=ALU.add)
                v.tensor_copy(t[:, a:a + 1], x[:, a + 1:a + 2])
                v.tensor_copy(t[:, b - 1:b], x[:, b - 2:b - 1])
            dve.drain()
            v.scalar_tensor_tensor(out=t, in0=t, scalar=0.5, in1=x, op0=ALU.mult, op1=ALU.subtract)
            dve.drain()
            v.scalar_tensor_tensor(out=x, in0=t, scalar=self.mu[:, j:j + 1], in1=x, op0=ALU.mult, op1=ALU.add)
        dve.drain().then_inc(self.v[0], 1)

    def scalar(self, act):
        act.wait_ge(self.v[0], self.v[1] + 1)
        self.nc.scalar.activation(self.tanh, self.tanh, ACT.Tanh)
        self.nc.scalar.activation(self.sigm, self.sigm, ACT.Sigmoid)


class Wkv(Stage):

    LEVELS = 6

    def __init__(self, k, w, y, ksum):
        super().__init__(k)
        self.w, self.y, self.ksum = w, y, ksum
        n = 4 * N_CH
        self.steps = {}
        for name, per in (("operands", 1), ("logits", 1), ("sigmoids", 1), ("key_squares", 1), ("key_sums", 1),
                          ("key_roots", 1), ("logs", 1), ("exps", 1), ("factors", 1), ("tokens", 1), ("token_rows", 1),
                          ("grams", 1), ("more_grams", 1), ("last_grams", 1), ("low_masked", 2), ("masked", 2), ("more_masked", 1),
                          ("level_blocks", 2 * self.LEVELS), ("level_half", 2 * self.LEVELS),
                          ("level_half_copied", 2 * self.LEVELS), ("level_summed", 2 * self.LEVELS),
                          ("level_added", 2 * self.LEVELS), ("w_summed", 1), ("w_copied", 1), ("u_summed", 2),
                          ("u_copied", 2), ("outputs", 1)):
            self.steps[name] = (*self.count("wkv_" + name, per * n), per)
        self.staged = self.count("wkv_tile_staged", 4)

    def at(self, name, u, i=0):
        s, base, per = self.steps[name]
        return s, u * per + (base + i + 1)

    def turns(self, eng, tile, chunk):
        with eng.Fori(0, 4) as c:
            tile(c)
            for lo, hi in ((0, CTX // CH), (CTX // CH, N_CH)):
                with eng.Fori(lo, hi) as ch:
                    chunk(c, c * N_CH + ch, (ch * CH, (lo + hi - 1) * CH - ch * CH))

    def gram(self, n, e):
        bank, half = 3 * e + (1 if n in (2, 3) else 0), n % 2
        return self.kern.ps[bank][:, half * 2 * CH:(half + 1) * 2 * CH]

    def half_bank(self, g):
        return self.kern.ps[(5, 2)[g]]

    def level_bank(self, g):
        x = self.kern.ps[6 + g].rearrange("p (a t) -> p a t", a=4)
        return x[:, 0:2, :], x[:, 2:4, :]

    def nat(self, x, c, off, d):
        return x[:, bass.ds(c * ALLTOK + off[d], CH)]

    @staticmethod
    def ordered(x, d):
        return x[:, ::-1] if d else x

    def tensor(self, pe):
        t, w, ps = self.nc.tensor, self.w, self.kern.ps
        ident = self.kern.ident

        def chunk(c, u, off):
            pe.wait_ge(self.staged[0], c + (self.staged[1] + 1))
            pe.wait_ge(*self.at("operands", u))
            for i in range(4):
                d, x = i % 2, (w.w1c if i < 2 else w.a1c)
                ws = w.w2s if i < 2 else w.a2s
                last = t.matmul(ps[d][:, i // 2 * CH:(i // 2 + 1) * CH], ws[64 * d:64 * d + 64, :], x[64 * d:64 * d + 64, :],
                                start=True, stop=True)
            last.then_inc(self.steps["logits"][0], 1)
            pe.wait_ge(*self.at("key_squares", u))
            t.matmul(ps[2][:, 0:2 * CH], w.head_ones, w.sq, start=True, stop=True).then_inc(self.steps["key_sums"][0], 1)
            pe.wait_ge(*self.at("factors", u))

            def grams(n, qs):
                lhs, rhs = ((w.bt, w.at), (w.at, w.bt), (w.kt, w.at), (w.bt, w.rt), (w.kt, w.rt))[n]
                for q in qs:
                    d, e = q % 2, slice(64 * (q // 2), 64 * (q // 2) + 64)
                    last = t.matmul(self.gram(n, q // 2)[:, d * CH:(d + 1) * CH], lhs[e, d, :], rhs[e, d, :],
                                    start=True, stop=True)
                return last

            grams(0, (0, 2, 1, 3))
            grams(1, (0, 2, 1, 3)).then_inc(self.steps["grams"][0], 1)
            for d in (0, 1):
                t.transpose(ps[5][:, d * CH:(d + 1) * CH], w.bt[:, d, :], ident)
                t.transpose(ps[5][:, (2 + d) * CH:(3 + d) * CH], w.kt[:, d, :], ident)
                last = t.transpose(ps[6][:, d * CH:(d + 1) * CH], w.vc[:, d, :], ident)
            last.then_inc(self.steps["tokens"][0], 1)
            grams(2, (0, 2, 1, 3))
            grams(3, (0, 2, 1, 3)).then_inc(self.steps["more_grams"][0], 1)

            def half(lv, g):
                if lv:
                    pe.wait_ge(*self.at("level_added", u, 2 * lv - 2 + g))
                else:
                    pe.wait_ge(*self.at("masked", u, g))
                pe.wait_ge(*self.at("level_blocks", u, 2 * lv + g))
                for q in (2 * g, 2 * g + 1):
                    last = t.matmul(self.half_bank(g)[:, q % 2 * CH:(q % 2 + 1) * CH], w.lo[:, lv % 2, q, :], w.x[:, q, :], start=True, stop=True)
                last.then_inc(self.steps["level_half"][0], 1)

            def whole(lv, g):
                pe.wait_ge(*self.at("level_half_copied", u, 2 * lv + g))
                x, xt = self.level_bank(g)
                for q in (2 * g, 2 * g + 1):
                    last = t.matmul(xt[:, q % 2, :], w.t1[:, q, :], w.xt[:, q, :], start=True, stop=True)
                    if lv < self.LEVELS - 1:
                        last = t.matmul(x[:, q % 2, :], w.xt[:, q, :], w.t1[:, q, :], start=True, stop=True)
                last.then_inc(self.steps["level_summed"][0], 1)

            def right_side():
                pe.wait_ge(*self.at("more_masked", u))
                for q in range(4):
                    d, e = q % 2, slice(64 * (q // 2), 64 * (q // 2) + 64)
                    o = ps[q // 2][:, d * HD:(d + 1) * HD]
                    t.matmul(o, w.at[e, d, :], w.s[e, d, :], start=True, stop=False)
                    last = t.matmul(o, w.lkt[:, q, :], w.vr[:, d, e], start=False, stop=True)
                last.then_inc(self.steps["w_summed"][0], 1)

            pe.wait_ge(*self.at("token_rows", u))
            for lv in range(self.LEVELS):
                half(lv, 0)
                half(lv, 1)
                whole(lv, 0)
                whole(lv, 1)
                if lv == 0:
                    grams(4, (0, 2, 1, 3)).then_inc(self.steps["last_grams"][0], 1)
                if lv == self.LEVELS - 2:
                    right_side()
            pe.wait_ge(*self.at("w_copied", u))
            for g in (0, 1):
                pe.wait_ge(*self.at("level_added", u, 2 * self.LEVELS - 2 + g))
                for q in (2 * g, 2 * g + 1):
                    last = t.matmul(self.half_bank(g)[:, q % 2 * HD:(q % 2 + 1) * HD], w.xt[:, q, :], w.wv[:, q, :], start=True, stop=True)
                last.then_inc(self.steps["u_summed"][0], 1)
            for g in (0, 1):
                pe.wait_ge(*self.at("u_copied", u, g))
                for q in (2 * g, 2 * g + 1):
                    d, e = q % 2, slice(64 * g, 64 * g + 64)
                    o = ps[3][e, d * CH:(d + 1) * CH]
                    t.matmul(o, w.uv[:, q, :], w.rbt[:, q, :], start=True, stop=False)
                    t.matmul(o, w.s[e, d, :], w.rt[e, d, :], start=False, stop=False)
                    t.matmul(o, w.vr[:, d, e], w.rkt[:, q, :], start=False, stop=True)
                    o = ps[4][e, d * HD:(d + 1) * HD]
                    t.matmul(o, w.br[:, d, e], w.uv[:, q, :], start=True, stop=False)
                    last = t.matmul(o, w.kr[:, d, e], w.vr[:, d, e], start=False, stop=True)
            last.then_inc(self.steps["outputs"][0], 1)

        self.turns(pe, lambda c: None, chunk)

    def scalar(self, act):
        s, w, ps = self.nc.scalar, self.w, self.kern.ps

        def tile(c):
            act.wait_ge(self.staged[0], c + (self.staged[1] + 1))

        def chunk(c, u, off):
            act.wait_ge(*self.at("logits", u))
            for d in (0, 1):
                s.activation(w.lw[:, d, :], ps[d][:, 0:CH], ACT.Sigmoid, bias=w.cst[:, d:d + 1])
                s.activation(w.a[:, d, :], ps[d][:, CH:2 * CH], ACT.Sigmoid, bias=w.cst[:, 2 + d:3 + d])
            act.drain().then_inc(self.steps["sigmoids"][0], 1)
            act.wait_ge(*self.at("key_sums", u))
            s.activation(w.root, ps[2][:, 0:2 * CH], ACT.Sqrt, bias=w.tiny).then_inc(self.steps["key_roots"][0], 1)
            act.wait_ge(*self.at("logs", u))
            s.activation(w.en, w.e1, ACT.Exp, scale=-1.0)
            s.activation(w.half, w.half, ACT.Exp)
            s.activation(w.ea, w.ea, ACT.Exp)
            act.drain()
            s.activation(w.e1, w.e1, ACT.Exp)
            act.drain().then_inc(self.steps["exps"][0], 1)
            act.wait_ge(*self.at("tokens", u))
            s.activation(w.br, ps[5][:, 0:2 * CH].rearrange("p (d t) -> p d t", d=2), ACT.Copy)
            s.activation(w.kr, ps[5][:, 2 * CH:4 * CH].rearrange("p (d t) -> p d t", d=2), ACT.Copy)
            s.activation(w.vr, ps[6][:, 0:2 * CH].rearrange("p (d t) -> p d t", d=2), ACT.Copy)
            act.drain().then_inc(self.steps["token_rows"][0], 1)
            for lv in range(self.LEVELS):
                for g in (0, 1):
                    act.wait_ge(*self.at("level_half", u, 2 * lv + g))
                    half = slice(2 * g * CH, (2 * g + 2) * CH)
                    s.activation(w.t1_flat[:, half], self.half_bank(g)[:, 0:2 * CH], ACT.Copy).then_inc(self.steps["level_half_copied"][0], 1)
            act.wait_ge(*self.at("w_summed", u))
            for e in (0, 1):
                s.activation(w.wv_flat[:, e * P:(e + 1) * P], ps[e][:, 0:P], ACT.Copy)
            act.drain().then_inc(self.steps["w_copied"][0], 1)
            for g in (0, 1):
                act.wait_ge(*self.at("u_summed", u, g))
                half = slice(2 * g * HD, (2 * g + 2) * HD)
                s.activation(w.uv_flat[:, half], self.half_bank(g)[:, 0:2 * HD], ACT.Copy).then_inc(self.steps["u_copied"][0], 1)

        self.turns(act, tile, chunk)

    def vector(self, dve):
        v, w, ps = self.nc.vector, self.w, self.kern.ps

        def mask2(m):
            return m.rearrange("p (a t) -> p a t", a=1).broadcast_to([P, 2, CH])

        def tile(c):
            dve.drain()
            v.tensor_copy(w.w2s, w.w2[:, bass.ds(c * P, P)])
            v.tensor_copy(w.a2s, w.a2[:, bass.ds(c * P, P)])
            v.tensor_copy(w.cst, w.csts[:, bass.ds(c * 8, 8)])
            v.memset(w.s_flat, 0.0)
            dve.drain().then_inc(self.staged[0], 1)

        def chunk(c, u, off):
            for d in (0, 1):
                e = slice(64 * d, 64 * d + 64)
                for dst, src in ((w.w1c, w.w1), (w.a1c, w.a1)):
                    v.tensor_copy(self.ordered(dst[e, :], d), src[e, bass.ds(off[d], CH)])
                v.tensor_copy(self.ordered(w.kc[:, d, :], d), self.nat(w.k, c, off, d))
                v.tensor_copy(self.ordered(w.vc[:, d, :], d), self.nat(w.v, c, off, d))
            dve.drain().then_inc(self.steps["operands"][0], 1)
            v.tensor_scalar(w.kk, w.kc_flat, w.cst[:, 4:5], None, ALU.mult)
            dve.drain()
            v.tensor_tensor(out=w.sq, in0=w.kk, in1=w.kk, op=ALU.mult)
            dve.drain().then_inc(self.steps["key_squares"][0], 1)
            dve.wait_ge(*self.at("sigmoids", u))
            v.tensor_scalar(w.lw_flat, w.lw_flat, -float(np.exp(-0.5)), None, ALU.mult)
            v.tensor_scalar(w.kd_flat, w.a_flat, w.cst[:, 5:6], w.cst[:, 7:8], ALU.mult, ALU.add)
            dve.drain()
            v.tensor_tensor(out=w.kd_flat, in0=w.kd_flat, in1=w.kc_flat, op=ALU.mult)
            for d in (0, 1):
                v.tensor_tensor_scan(w.e1d[:, d, :], w.ones_row, w.lw[:, d, :], 0.0, ALU.mult, ALU.add)
            dve.drain()
            v.tensor_scalar(w.half, w.e1d[:, :, CH - 1], 0.5, None, ALU.mult)
            for d in (0, 1):
                ks = self.nat(self.ksum, c, off, d)
                v.tensor_tensor(out=ks, in0=ks, in1=self.ordered(w.kd[:, d, :], d), op=ALU.add)
                dve.drain()
            for d in (0, 1):
                v.tensor_scalar(w.e1d[:, d, :], w.e1d[:, d, :], w.half[:, d:d + 1], None, ALU.subtract)
            dve.drain()
            v.tensor_tensor(out=w.ea, in0=w.e1, in1=w.lw_flat, op=ALU.subtract)
            dve.drain().then_inc(self.steps["logs"][0], 1)
            dve.wait_ge(*self.at("key_roots", u))
            v.reciprocal(w.root, w.root)
            dve.drain()
            v.tensor_tensor(out=w.kk, in0=w.kk, in1=w.root, op=ALU.mult)
            dve.drain()
            dve.wait_ge(*self.at("exps", u))
            v.tensor_tensor(out=w.bt_flat, in0=w.kk, in1=w.a_flat, op=ALU.mult)
            v.scalar_tensor_tensor(out=w.at_flat, in0=w.kk, scalar=-1.0, in1=w.ea, op0=ALU.mult, op1=ALU.mult)
            v.tensor_tensor(out=w.kt_flat, in0=w.kd_flat, in1=w.en, op=ALU.mult)
            for d in (0, 1):
                v.tensor_tensor(out=self.ordered(w.rt[:, d, :], d), in0=self.nat(w.r, c, off, d),
                                in1=self.ordered(w.e1d[:, d, :], d), op=ALU.mult)
                v.tensor_scalar(w.s[:, d, :], w.s[:, d, :], w.half[:, d:d + 1], None, ALU.mult)
            dve.drain()
            v.tensor_tensor(out=w.bt_flat, in0=w.bt_flat, in1=w.en, op=ALU.mult)
            dve.drain().then_inc(self.steps["factors"][0], 1)
            def mask(n, dst, m, e):
                v.tensor_tensor(out=dst[:, 2 * e:2 * e + 2, :], op=ALU.mult,
                                in0=self.gram(n, e).rearrange("p (a t) -> p a t", a=2), in1=mask2(m))

            dve.wait_ge(*self.at("grams", u))
            for g in (0, 1):
                pair = slice(2 * g, 2 * g + 2)
                mask(0, w.lt, w.strict, g)
                dve.drain().then_inc(self.steps["low_masked"][0], 1)
                mask(1, w.x, w.first_low, g)
                v.tensor_tensor(out=w.xt[:, pair, :], in0=w.lt[:, pair, :], in1=mask2(w.first_up), op=ALU.mult)
                dve.drain()
                v.tensor_tensor(out=w.x[:, pair, :], in0=w.x[:, pair, :], in1=mask2(self.kern.ident), op=ALU.add)
                v.tensor_tensor(out=w.xt[:, pair, :], in0=w.xt[:, pair, :], in1=mask2(self.kern.ident), op=ALU.add)
                dve.drain().then_inc(self.steps["masked"][0], 1)
            more = ((2, w.lkt, w.strict), (3, w.rbt, w.incl), (4, w.rkt, w.incl))
            for lv in range(self.LEVELS):
                for g in (0, 1):
                    pair = slice(2 * g, 2 * g + 2)
                    dve.wait_ge(*self.at("level_summed", u, 2 * lv + g))
                    x, xt = self.level_bank(g)
                    if lv < self.LEVELS - 1:
                        v.tensor_tensor(out=w.x[:, pair, :], in0=w.x[:, pair, :], in1=x, op=ALU.add)
                    v.tensor_tensor(out=w.xt[:, pair, :], in0=w.xt[:, pair, :], in1=xt, op=ALU.add)
                    dve.drain().then_inc(self.steps["level_added"][0], 1)
                    if lv < len(more):
                        dve.wait_ge(*self.at("last_grams" if lv == 2 else "more_grams", u))
                        mask(*more[lv], g)
                if lv == len(more) - 1:
                    dve.drain().then_inc(self.steps["more_masked"][0], 1)
            dve.wait_ge(*self.at("outputs", u))
            v.tensor_tensor(out=w.s_flat, in0=w.s_flat, in1=ps[4][:, 0:2 * HD], op=ALU.add)
            for d in (0, 1):
                yv = self.nat(self.y, c, off, d)
                v.tensor_tensor(out=yv, in0=yv, in1=self.ordered(ps[3][:, d * CH:(d + 1) * CH], d), op=ALU.add)
                dve.drain()
            for d in (0, 1):
                v.tensor_scalar(w.s[:, d, :], w.s[:, d, :], w.half[:, d:d + 1], None, ALU.mult)
            dve.drain()

        v.memset(w.ones_row, 1.0)
        v.memset(self.y, 0.0)
        v.memset(self.ksum, 0.0)
        for c in range(4):
            v.tensor_scalar(w.csts[:, c * 8 + 7:c * 8 + 8], w.csts[:, c * 8 + 5:c * 8 + 6], -1.0, 1.0, ALU.mult, ALU.add)
        self.turns(dve, tile, chunk)

    def gpsimd(self, pool):
        w = self.w

        def chunk(c, u, off):
            for lv in range(self.LEVELS):
                m = w.joins[:, lv * CH:(lv + 1) * CH].rearrange("p (a t) -> p a t", a=1).broadcast_to([P, 2, CH])
                for g in (0, 1):
                    if lv == 0:
                        pool.wait_ge(*self.at("low_masked", u, g))
                    elif lv >= 2:
                        pool.wait_ge(*self.at("level_half", u, 2 * lv - 4 + g))
                    pair = slice(2 * g, 2 * g + 2)
                    self.nc.gpsimd.tensor_tensor(out=w.lo[:, lv % 2, pair], in0=w.lt[:, pair], in1=m,
                                                 op=ALU.mult).then_inc(self.steps["level_blocks"][0], 1)

        self.turns(pool, lambda c: None, chunk)


class RwkvOut(Stage):

    def __init__(self, k, y, ksum, r, v, g, mean_ones, sum_ones, vecs, eps, tmp):
        super().__init__(k)
        self.y, self.ks, self.r, self.v_, self.g = y, ksum, r, v, g
        self.mean_ones, self.sum_ones, self.vecs, self.eps, self.tmp = mean_ones, sum_ones, vecs, eps, tmp
        self.units = [(c, s) for c in range(4) for s in segments(ALLTOK)]
        n = len(self.units)
        self.p = self.count("rwout_summed", 2 * n)
        self.d = self.count("rwout_vector", 3 * n)
        self.a = self.count("rwout_scalar", n)

    def parts(self, c, s):
        a, b = s
        return tuple(x[:, c, a:b] for x in (self.y, self.ks, self.r, self.v_, self.g)) + (self.tmp[:, 0, 0:b - a],)

    def tensor(self, pe):
        t, ps = self.nc.tensor, self.kern.ps
        for n, (c, s) in enumerate(self.units):
            y, ks, r, v, g, tmp = self.parts(c, s)
            w = s[1] - s[0]
            pe.wait_ge(self.d[0], self.d[1] + 3 * n + 1)
            t.matmul(ps[0][:, 0:w], self.mean_ones, y, start=True, stop=True)
            t.matmul(ps[1][:, 0:w], self.sum_ones, ks, start=True, stop=True).then_inc(self.p[0], 1)
            pe.wait_ge(self.d[0], self.d[1] + 3 * n + 2)
            t.matmul(ps[2][:, 0:w], self.mean_ones, tmp, start=True, stop=True).then_inc(self.p[0], 1)

    def scalar(self, act):
        for n, (c, s) in enumerate(self.units):
            tmp = self.parts(c, s)[5]
            act.wait_ge(self.p[0], self.p[1] + 2 * n + 2)
            self.nc.scalar.activation(tmp, self.kern.ps[2][:, 0:s[1] - s[0]], ACT.Sqrt, bias=self.eps).then_inc(self.a[0], 1)

    def vector(self, dve):
        e, ps = self.nc.vector, self.kern.ps
        for n, (c, s) in enumerate(self.units):
            y, ks, r, v, g, tmp = self.parts(c, s)
            w = s[1] - s[0]
            e.scalar_tensor_tensor(out=ks, in0=ks, scalar=self.vecs[:, 8 + c:9 + c], in1=r, op0=ALU.mult, op1=ALU.mult)
            dve.drain().then_inc(self.d[0], 1)
            dve.wait_ge(self.p[0], self.p[1] + 2 * n + 1)
            e.tensor_tensor(out=y, in0=y, in1=ps[0][:, 0:w], op=ALU.subtract)
            e.tensor_tensor(out=ks, in0=v, in1=ps[1][:, 0:w], op=ALU.mult)
            dve.drain()
            e.tensor_tensor(out=tmp, in0=y, in1=y, op=ALU.mult)
            dve.drain().then_inc(self.d[0], 1)
            dve.wait_ge(self.a[0], self.a[1] + n + 1)
            e.reciprocal(tmp, tmp)
            dve.drain()
            e.tensor_tensor(out=y, in0=y, in1=tmp, op=ALU.mult)
            dve.drain()
            e.tensor_scalar(y, y, self.vecs[:, c:c + 1], self.vecs[:, 4 + c:5 + c], ALU.mult, ALU.add)
            dve.drain()
            e.tensor_tensor(out=y, in0=y, in1=ks, op=ALU.add)
            dve.drain()
            e.tensor_tensor(out=y, in0=y, in1=g, op=ALU.mult)
            dve.drain().then_inc(self.d[0], 1)


class Copy(Stage):
    def __init__(self, k, pairs):
        super().__init__(k)
        self.pairs = pairs

    def scalar(self, act):
        for dst, src in self.pairs:
            self.nc.scalar.activation(dst, src, ACT.Copy)


class Router(Stage):

    def __init__(self, k, h, tiles, rw, rb, work, rows):
        super().__init__(k)
        self.h, self.tiles, self.rw, self.rb, self.rows = h, tiles, rw, rb, rows
        n = self.n = len(tiles)
        e, g = n * N_EXP, n * 4
        at = [0]

        def take(cols):
            at[0] += cols
            return work[:, at[0] - cols:at[0]]

        self.scores, self.biased, self.lost, self.cmp = take(e), take(e), take(e), take(g)
        self.sums, self.best, self.glost, self.den = take(g), take(g), take(g), take(n)
        self.comb = take(n * 17).rearrange("p (t e) -> p t e", e=17)
        self.summed = self.count("router_summed", 1)
        self.sig = self.count("router_scores", 1)
        self.done = self.count("router_combined", 1)
        self.turned = self.count("router_turned", 1)

    def tensor(self, pe):
        t, ps = self.nc.tensor, self.kern.ps
        for i, tile in enumerate(self.tiles):
            for kt in range(KT):
                last = t.matmul(ps[0][:, i * N_EXP:(i + 1) * N_EXP], self.h[:, kt, tile * P:(tile + 1) * P],
                                self.rw[:, kt * N_EXP:(kt + 1) * N_EXP], start=(kt == 0), stop=(kt == KT - 1))
        last.then_inc(self.summed[0], 1)
        pe.wait_ge(self.done[0], self.done[1] + 1)
        for i in range(self.n):
            last = t.transpose(self.kern.ps[1 + i // 4][0:17, (i % 4) * P:(i % 4 + 1) * P], self.comb[:, i, :], self.kern.ident)
        last.then_inc(self.turned[0], 1)

    def scalar(self, act):
        act.wait_ge(self.summed[0], self.summed[1] + 1)
        self.nc.scalar.activation(self.scores, self.kern.ps[0][:, 0:self.n * N_EXP], ACT.Sigmoid).then_inc(self.sig[0], 1)
        act.wait_ge(self.turned[0], self.turned[1] + 1)
        for i, tile in enumerate(self.tiles):
            self.nc.scalar.activation(self.rows[0:17, tile * P:(tile + 1) * P],
                                      self.kern.ps[1 + i // 4][0:17, (i % 4) * P:(i % 4 + 1) * P], ACT.Copy)

    def vector(self, dve):
        v, n = self.nc.vector, self.n

        def tt(out, a, b, op):
            v.tensor_tensor(out=out, in0=a, in1=b, op=op)
            dve.drain()

        def member(x, i):
            return x[:, i:n * N_EXP:4]

        def group(x, i):
            return x[:, i:n * 4:4]

        dve.wait_ge(self.sig[0], self.sig[1] + 1)
        for i in range(n):
            v.tensor_tensor(out=self.biased[:, i * N_EXP:(i + 1) * N_EXP], in0=self.scores[:, i * N_EXP:(i + 1) * N_EXP],
                            in1=self.rb, op=ALU.add)
        v.memset(self.lost, 0.0)
        v.memset(self.glost, 0.0)
        v.memset(self.sums, NEG)
        v.memset(self.comb, 1.0)
        dve.drain()
        for i in range(4):
            for j in range(i + 1, 4):
                a, b = member(self.biased, i), member(self.biased, j)
                tt(self.cmp, a, b, ALU.add)
                tt(self.sums, self.sums, self.cmp, ALU.max)
                tt(self.cmp, a, b, ALU.is_ge)
                tt(member(self.lost, j), member(self.lost, j), self.cmp, ALU.add)
                tt(self.cmp, a, b, ALU.is_lt)
                tt(member(self.lost, i), member(self.lost, i), self.cmp, ALU.add)
        for i in range(4):
            for j in range(i + 1, 4):
                a, b, c = group(self.sums, i), group(self.sums, j), self.cmp[:, 0:n]
                tt(c, a, b, ALU.is_ge)
                tt(group(self.glost, j), group(self.glost, j), c, ALU.add)
                tt(c, a, b, ALU.is_lt)
                tt(group(self.glost, i), group(self.glost, i), c, ALU.add)
        v.tensor_scalar(self.lost, self.lost, 2.0, None, ALU.is_lt)
        v.tensor_scalar(self.best, self.glost, 1.0, None, ALU.is_lt)
        dve.drain()
        for i in range(4):
            tt(member(self.lost, i), member(self.lost, i), self.best, ALU.mult)
        tt(self.scores, self.scores, self.lost, ALU.mult)
        v.reduce_sum(self.den, self.scores.rearrange("p (t e) -> p t e", e=N_EXP), AX_X)
        dve.drain()
        v.reciprocal(self.den, self.den)
        dve.drain()
        for i in range(n):
            v.tensor_scalar(self.comb[:, i, 0:N_EXP], self.scores[:, i * N_EXP:(i + 1) * N_EXP], self.den[:, i:i + 1],
                            None, ALU.mult)
        dve.drain().then_inc(self.done[0], 1)


ARENA = 24000


class Kernel:

    def __init__(self, nc, ctx, A):
        self.nc, self.A = nc, A
        self.tally = Tally(nc, ctx)
        self.stages = []
        self.ring = Ring()

        def sb(name, shape):
            return ctx.enter_context(nc.sbuf_tensor(name, shape, F32))

        self.psum = ctx.enter_context(nc.psum_tensor("psum", [P, 8, 512], F32))
        self.ps = [self.psum[:, i, :] for i in range(8)]
        self.slots = sb("weight_slots", [P, SLOTS, SLOT_COLS])
        self.x_t = sb("x_t", [P, KT, ALLTOK])
        self.h_t = sb("h_t", [P, KT, ALLTOK])
        self.consts = sb("consts", [P, A["consts"].shape[1]])
        self.arena = sb("arena", [P, ARENA])
        self.rstd = sb("rstd", [P, 4, 512])
        self.scratch = self.rstd
        self.small = sb("small", [P, 24])
        self.mod_all = sb("mod_all", [P, 256])
        self.h_flat = self.h_t[:, :, :].rearrange("p a b -> p (a b)")
        self.stat = sb("stat", [P, 16])
        self.row_max, self.neg_max = self.stat[:, 0:2], self.stat[:, 2:4]
        self.row_sum, self.row_inv = self.stat[:, 4:6], self.stat[:, 6:8]
        self.q_stage = sb("q_stage", [P, 2, P])
        c = self.const
        self.ident, self.eps, self.one = c("ident", 0, P), c("eps", 0), c("one", 0)

    def const(self, name, at, n=1):
        off = CONST_AT[name]
        return self.consts[:, off + at:off + at + n]

    def slot(self, item):
        return self.slots[:, item % SLOTS, :]

    def slot_ready(self, pe, item, turn=0):
        pe.wait_ge(self.tally.sem(f"slot_{item % SLOTS}_loaded"), turn * 16 + 16 * (item // SLOTS + 1))
        return self.slot(item)

    def part(self, at, *dims, parts=P):
        n = int(np.prod(dims))
        assert at + n <= ARENA, (at, dims)
        v = self.arena[0:parts, at:at + n]
        if len(dims) == 1:
            return v
        names = "abc"[:len(dims)]
        return v.rearrange(f"p ({' '.join(names)}) -> p {' '.join(names)}", **{x: d for x, d in zip(names[1:], dims[1:])})

    def attention_buffers(self, at, keys):
        self.biased = self.part(at, 2, keys)
        self.probs = self.part(at + 2 * keys, 2, keys)
        self.probs_t = self.part(at + 4 * keys, 2, max(keys, P))
        return at + 4 * keys + 2 * max(keys, P)

    def block_one(self):
        A, c = self.A, self.const
        x, h = self.x_t, self.h_t
        lat = slice(CTX, ALLTOK)
        segs = segments(SEQ)
        FromHbm(self, [(self.consts[:, :], A["consts"]), (x[:, :, lat], A["x"])])
        Norm(self, x, h, KT, KT, segs, lambda t, a: c("norm_mix", t), c("ones_1024", 0, P))
        z = self.part(0, 10, SEQ)
        toks = self.part(5120, 4, 400)
        o_tok = self.part(6720, 4, 512)
        heads = self.part(8768, 16, SEQ, parts=66)
        work_at = 16960
        f4 = self.part(work_at, SEQ, parts=4)
        y = h[:, :, lat]
        Project(self, h, segs, 10, P, lambda t, a, b: z[:, t, :])
        Project(self, h, segs, 16, HD, lambda t, a, b: heads[0:HD, t, :])
        TokenProject(self, h, [2, 3, 4, 5], [256, 144], lambda t, i: toks[:, t - 2, i * 256:i * 256 + (256, 144)[i]])
        FoxRows(self, toks, f4)
        ConvMixers(self, z, y, self.part(work_at + 512, 6144))
        sm = self.small
        Scale(self, [(sm[:, 16:17], c("fox_gq", 0), HD ** -0.5), (sm[:, 17:18], c("nsa_gq", 0), HD ** -0.5)])
        gains = [sm[0:HD, 16:17]] * 4 + [c("fox_gk", 0)[0:HD, :]] * 4 + [sm[0:HD, 17:18]] * 4
        units = [(heads[0:HD, i, :], g) for i, g in enumerate(gains)]
        units += [(heads[0:HD, 14, :], c("nsa_gks", 0)[0:HD, :]), (heads[0:HD, 15, :], c("nsa_gkw", 0)[0:HD, :])]
        HeadNorm(self, units, c("ones_64", 0, HD)[0:HD, :], HD)
        FoxGates(self, f4, (heads[64:65, 0:4, :], heads[65:66, 0:4, :]), (heads[64:65, 4:8, :], heads[65:66, 4:8, :]),
                 self.part(work_at + 512, 4 * SEQ))
        w1 = [self.part(0, 32, P, parts=HD), self.part(work_at, 32, P, parts=HD)]
        kc, vc = self.part(4096, 32, parts=HD), self.part(4160, HD, parts=32)
        FromHbm(self, [(w1[0], A["cmp_w1"][:, 0]), (w1[1], A["cmp_w1"][:, 1])])
        Compress(self, heads[0:HD, 12, :], heads[0:HD, 13, :], w1, c("cmp_w2", 0, 2 * HD).rearrange("p (a b) -> p a b", a=2),
                 c("cmp_pos", 0, 2 * CMP_LEN)[0:HD, :], kc[:, 0:N_CMP], vc[0:N_CMP, :], self.part(work_at + 4096, 2112))
        HeadNorm(self, [(kc[:, 0:N_CMP], c("nsa_gkc", 0)[0:HD, :])], c("ones_64", 0, HD)[0:HD, :], HD)
        toe = self.part(0, 4, 896)
        cmp_bias = self.part(3584, 4, 4, 32)
        onehots = self.part(work_at, 2, 1024, parts=33)
        rel = self.part(work_at + 2048, 4, parts=33)
        FromHbm(self, [(onehots, A["onehots"]), (rel, A["rel"])])
        RelBias(self, onehots[:, 0, :], onehots[:, 1, :], rel, self.part(work_at, 1024, parts=4), A["bias_line"], toe, cmp_bias)
        gates = toks[:, :, 384:396]
        NsaGates(self, gates)
        FromHbm(self, [(self.part(work_at + 3072, 896), A["causal"])])
        self.attention_buffers(work_at, SEQ)
        mask = self.part(work_at + 3072, 896)
        Attention(self, 66, SEQ, 4, 1, 4, lambda hh, t: heads[0:66, hh, bass.ds(t * P, P)],
                  lambda hk, a, b: heads[0:66, 4 + hk, a:b], lambda kt, n, hk: toks[:, kt, bass.ds(hk * HD, HD)],
                  lambda hh, t: o_tok[:, t, bass.ds(hh * HD, HD)], bias=lambda hh, t: mask[:, bass.ds(384 - t * P, SEQ)])
        gate = lambda br: (lambda hh, t: gates[:, t, bass.ds(br * 4 + hh, 1)])
        q = lambda hh, t: heads[0:HD, 8 + hh, bass.ds(t * P, P)]
        o = lambda hh, t: o_tok[:, t, bass.ds(hh * HD + 256, HD)]
        Attention(self, HD, N_CMP, 4, 1, 4, q, lambda hk, a, b: kc[:, a:b], lambda kt, n, hk: vc[0:N_CMP, :], o,
                  bias=lambda hh, t: cmp_bias[:, t, hh, 0:N_CMP], factor=gate(0))
        for br, key, v in ((1, 14, 256), (2, 15, 320)):
            Attention(self, HD, SEQ, 4, 1, 4, q, lambda hk, a, b, key=key: heads[0:HD, key, a:b],
                      lambda kt, n, hk, v=v: toks[:, kt, v:v + HD], o,
                      bias=lambda hh, t: toe[:, hh, bass.ds(384 - t * P, SEQ)], factor=gate(br), add=True)
        Turn(self, [([o_tok[:, t, f * P:(f + 1) * P] for t in range(4)], y[:, 4 + f, :]) for f in range(4)])
        mixed = self.part(0, KT, SEQ)
        mixed_all = self.part(0, KT, ALLTOK)
        Norm(self, h, mixed_all, KT, 2, segs, lambda t, a: c("out_norm", t), c("ones_256", 0, P))
        Project(self, mixed_all, segs, KT, P, lambda t, a, b: x[:, t, a:b], gate=lambda t, a: self.one)
        Norm(self, x, h, KT, KT, segs, lambda t, a: c("norm_ffn", t), c("ones_1024", 0, P))
        self.experts_buffers()
        Experts(self, h, x, segs, D_FF // FF_CHUNK, lambda t, a: self.one)

    def experts_buffers(self):
        self.hidden = self.part(0, 2, 2, 512)
        self.sigm = self.part(2048, 2, 512)
        self.sel_buf = self.part(3072, 2, P, parts=17)
        self.sel_rows = self.part(3328, 17 * P, parts=17)

    def mods(self, layer):
        return [self.mod[layer][:, i * KT:(i + 1) * KT, :] for i in range(6)]

    def by_stream(self, x):
        return lambda t, a: x[:, t, (1 if a == 0 else 0):(1 if a == 0 else 0) + 1]

    def block_two(self):
        A, c, x, h = self.A, self.const, self.x_t, self.h_t
        every, lat = segments(ALLTOK), segments(SEQ)
        vec = self.mod_all
        self.mod = [vec[:, i * 96:(i + 1) * 96].rearrange("p (m s) -> p m s", s=2) for i in (0, 1)]
        gains = [vec[:, 192 + i * 16:208 + i * 16].rearrange("p (m s) -> p m s", s=2) for i in range(4)]
        c_t = self.part(0, KT, 2)
        FromHbm(self, [(x[:, :, 0:CTX], A["ctx"]), (self.part(0, 16), A["c"])])
        Silu(self, self.part(0, 16), self.part(16, 16))
        for layer in (0, 1):
            Ada(self, c_t, self.mod[layer], c("ada_b", layer * 48, 48))
        m = [self.mods(0), self.mods(1)]
        ModGains(self, [(gains[2 * l + j], m[l][3 * j + 1], c("norm12", (2 * l + j) * KT, KT)) for l in (0, 1) for j in (0, 1)])

        Norm(self, x, h, KT, KT, every, self.by_stream(gains[0]), c("ones_1024", 0, P), shift=self.by_stream(m[0][0]))
        p = self.part(0, 6, ALLTOK)
        q = self.part(4608, 8, ALLTOK)
        kk = self.part(10752, 8, ALLTOK)
        v = self.part(16896, 6, 512)
        wq = self.part(19968, 3, 768)
        wk, wv = self.part(19968, 2, 8, 96), self.part(21504, 2, 512)
        cos, sin = self.part(22528, 512, parts=96), self.part(23040, 512, parts=96)
        Project(self, h, every, 6, P, lambda t, a, b: p[:, t, a:b])
        FromHbm(self, [(wq, A["mla_q_up"]), (self.part(22528, 1024, parts=96), A["mla_rope"])])
        qn = self.part(10752, 3, ALLTOK)
        Norm(self, p, qn, 3, 3, every, lambda t, a: c("g_qa", t), c("ones_384", 0, P))
        LocalProject(self, [([(wq[:, kt, hh * 96:(hh + 1) * 96], qn[:, kt, a:b]) for kt in range(3)], q[0:96, hh, a:b])
                            for hh in range(8) for a, b in every])
        kvn = self.part(0, 2, ALLTOK)
        Norm(self, p[:, 3:5, :], kvn, 2, 2, every, lambda t, a: c("g_kva", t), c("ones_256", 0, P))
        FromHbm(self, [(self.part(19968, 2560), A["mla_kv_up"])])
        LocalProject(self, [([(wk[:, kt, hh, :], kvn[:, kt, a:b]) for kt in range(2)]
                             + [(c("place", 0, 96)[0:32, :], p[0:32, 5, a:b])], kk[0:96, hh, a:b])
                            for hh in range(8) for a, b in every]
                     + [([(kvn[:, kt, t * P:(t + 1) * P], wv[:, kt, :]) for kt in range(2)], v[:, t, :]) for t in range(6)])
        Scale(self, [(self.small[:, 16:17], c("mla_gq", 0), MLA_QK ** -0.5), (self.small[:, 17:18], c("gqa_gq", 0), HD ** -0.5)])
        HeadNorm(self, [(y[0:96, hh, a:b], g) for y, g in ((q, self.small[0:96, 16:17]), (kk, c("mla_gk", 0)[0:96, :]))
                        for hh in range(8) for a, b in every], c("ones_96", 0, 96)[0:96, :], 96)
        Rope(self, [y[0:96, hh, CTX:ALLTOK] for y in (q, kk) for hh in range(8)], c("mla_rot", 0, 96)[0:96, :], cos, sin, 96)
        self.attention_buffers(0, ALLTOK)
        o_tok = self.part(19968, 6, 512)
        q_all = self.part(4608, 8 * ALLTOK)
        for tile0, tiles, keys in ((0, 2, CTX), (2, 4, ALLTOK)):
            Attention(self, 96, keys, 8, 1, tiles,
                      lambda hh, t, t0=tile0: q_all[0:96, bass.ds(hh * ALLTOK + (t * P + t0 * P), P)],
                      lambda hk, a, b: kk[0:96, hk, a:b], lambda kt, n, hk: v[:, kt, bass.ds(hk * HD, HD)],
                      lambda hh, t, t0=tile0: self.part(19968, 3072)[:, bass.ds(t * 512 + (t0 * 512) + hh * HD, HD)])
        mla_t = self.part(0, 4, ALLTOK)
        Turn(self, [([o_tok[:, t, f * P:(f + 1) * P] for t in ts], mla_t[:, f, ts[0] * P:(ts[-1] + 1) * P])
                    for f in range(4) for ts in ([0, 1], [2, 3, 4, 5])])

        rw = self.part(3072, 15, ALLTOK)
        Project(self, h, every, 15, P, lambda t, a, b: rw[:, t, a:b])
        work = 3072 + 15 * ALLTOK
        at = [work]

        def take(n, *dims):
            at[0] += n
            return self.part(at[0] - n, *(dims or (n,)))

        mu = take(16)
        FromHbm(self, [(mu[:, 0:15], A["rw_mu"])])
        ShiftMix(self, rw, 15, mu, self.part(at[0], 2, ALLTOK), rw[:, 12, :], rw[:, 14, :])
        w = Views()
        flat = lambda t0: self.part(3072 + t0 * ALLTOK, 4 * ALLTOK)
        w.r, w.k, w.v = flat(0), flat(4), flat(8)
        w.w1, w.a1 = rw[:, 12, :], rw[:, 13, :]
        y, ksum = self.h_flat[:, 0:3072], self.h_flat[:, 3072:6144]
        rwc = take(RWC_COLS)
        FromHbm(self, [(rwc, A["rw_consts"])])
        w.w2, w.a2 = rwc[:, 0:512], rwc[:, 512:1024]
        w.csts = rwc[:, 1024:1056]
        w.strict, w.incl, w.first_low, w.first_up = (rwc[:, 1056 + i * P:1056 + (i + 1) * P] for i in range(4))
        w.joins = rwc[:, 1568:1568 + 6 * P]
        w.head_ones = rwc[:, 2336:2464]
        head_mean = rwc[:, 2464:2592]
        out_vecs = rwc[:, 2592:2606]
        w.tiny, gn_eps = rwc[:, 2604:2605], rwc[:, 2605:2606]
        pair = lambda f: f.rearrange("p (d t) -> p d t", d=2)
        quad = lambda f: f.rearrange("p (q t) -> p q t", q=4)
        w.w2s, w.a2s, w.cst = take(P), take(P), take(8)
        w.kc_flat, w.kk = take(256), take(256)
        w.e1, w.ea, w.en = take(256), take(256), take(256)
        w.at_flat, w.rt_flat, w.bt_flat, w.kt_flat = (take(256) for _ in range(4))
        w.at, w.rt, w.bt, w.kt, w.kc, w.e1d = (pair(f) for f in (w.at_flat, w.rt_flat, w.bt_flat, w.kt_flat, w.kc_flat, w.e1))
        w.br, w.kr, w.vr = (pair(take(256)) for _ in range(3))
        lt = take(512)
        lkt, rbt, rkt = (self.rstd[:, i, :] for i in range(3))
        w.lt, w.lkt, w.rbt, w.rkt = quad(lt), quad(lkt), quad(rbt), quad(rkt)
        w.sq, w.root = lt[:, 0:256], lt[:, 256:512]
        w.lw_flat, w.a_flat, w.kd_flat = lkt[:, 0:256], rbt[:, 0:256], rkt[:, 0:256]
        w.lw, w.a, w.kd = pair(w.lw_flat), pair(w.a_flat), pair(w.kd_flat)
        w.lo = take(1024).rearrange("p (l q t) -> p l q t", l=2, q=4)
        xf, xtf, t1f = take(512), take(512), take(512)
        w.x, w.xt, w.t1, w.t1_flat = quad(xf), quad(xtf), quad(t1f), t1f
        w.w1c, w.a1c, w.vc = xf[:, 0:P], xf[:, P:2 * P], pair(t1f[:, 0:256])
        w.wv_flat, w.uv_flat = w.en, w.ea
        w.wv, w.uv = quad(w.wv_flat), quad(w.uv_flat)
        w.s_flat, w.half, w.ones_row = take(128), take(2), take(P)
        w.s = pair(w.s_flat)
        Wkv(self, w, y, ksum)
        g2, g = self.part(work + 16, 512), self.part(at[0] - 3072, 4, ALLTOK)
        assert at[0] - 3072 > work + 16 + RWC_COLS + 512
        g2 = self.part(work + 16 + RWC_COLS, 512)
        FromHbm(self, [(g2, A["rw_g2"])])
        LocalProject(self, [([(g2[:, f * P:(f + 1) * P], rw[:, 14, a:b])], g[:, f, a:b]) for f in range(4) for a, b in every])
        y4, ks4 = h[:, 0:4, :], h[:, 4:8, :]
        RwkvOut(self, y4, ks4, rw[:, 0:4, :], rw[:, 8:12, :], g, head_mean, w.head_ones, out_vecs, gn_eps, self.rstd)
        Copy(self, [(h[:, 4 + f, :], mla_t[:, f, :]) for f in range(4)])
        Project(self, h, every, KT, P, lambda t, a, b: x[:, t, a:b], gate=self.by_stream(m[0][2]))
        self.moe(every, gains[1], m[0][3], m[0][5], 0)

        Norm(self, x, h, KT, KT, every, self.by_stream(gains[2]), c("ones_1024", 0, P), shift=self.by_stream(m[1][0]))
        q1 = self.part(0, 16, SEQ)
        k1 = self.part(8192, 4, ALLTOK)
        v1 = self.part(11264, 6, 256)
        o1 = self.part(17408, 4, D)
        cos, sin = self.part(21504, 512, parts=HD), self.part(22016, 512, parts=HD)
        Project(self, h, lat, 16, HD, lambda t, a, b: q1[0:HD, t, :])
        Project(self, h, every, 4, HD, lambda t, a, b: k1[0:HD, t, a:b])
        TokenProject(self, h, list(range(6)), [256], lambda t, i: v1[:, t, :])
        FromHbm(self, [(self.part(21504, 1024, parts=HD), A["gqa_rope"])])
        units = [(q1[0:HD, i, :], self.small[0:HD, 17:18]) for i in range(16)]
        units += [(k1[0:HD, i, a:b], c("gqa_gk", 0)[0:HD, :]) for i in range(4) for a, b in every]
        HeadNorm(self, units, c("ones_64", 0, HD)[0:HD, :], HD)
        Rope(self, [q1[0:HD, i, :] for i in range(16)] + [k1[0:HD, i, CTX:ALLTOK] for i in range(4)],
             c("gqa_rot", 0, HD)[0:HD, :], cos, sin, HD)
        Clear(self, [self.part(0, 11264)[HD:96, :]])
        self.attention_buffers(12800, ALLTOK)
        q_rows, o_all = self.part(0, 16 * SEQ), self.part(17408, 4 * D)
        Attention(self, 96, ALLTOK, GQA_KV, GQA_H // GQA_KV, 4, lambda hh, t: q_rows[0:96, bass.ds(hh * SEQ + t * P, P)],
                  lambda hk, a, b: k1[0:96, hk, a:b], lambda kt, n, hk: v1[:, kt, bass.ds(hk * HD, HD)],
                  lambda hh, t: o_all[:, bass.ds(t * D + hh * HD, HD)])
        Turn(self, [([o1[:, t, f * P:(f + 1) * P] for t in range(4)], h[:, f, CTX:ALLTOK]) for f in range(8)])
        Project(self, h, lat, KT, P, lambda t, a, b: x[:, t, a:b], gate=self.by_stream(m[1][2]))
        self.moe(lat, gains[3], m[1][3], m[1][5], 1)

    def moe(self, segs, gain, shift, gate, layer):
        c = self.const
        Norm(self, self.x_t, self.h_t, KT, KT, segs, self.by_stream(gain), c("ones_1024", 0, P), shift=self.by_stream(shift))
        self.experts_buffers()
        rows = self.part(6144, ALLTOK, parts=17)
        tiles = list(range(segs[0][0] // P, ALLTOK // P))
        FromHbm(self, [(self.sel_rows, self.A["sel_rows"])])
        Router(self, self.h_t, tiles, c("router_w", 0, KT * N_EXP), c("router_b", 0, N_EXP), self.part(7168, 1024), rows)
        Experts(self, self.h_t, self.x_t, segs, N_EXP + 1, self.by_stream(gate), comb=rows)


ENGINE_NAMES = ("tensor", "scalar", "vector", "gpsimd")
PRIMED = ("hidden_ready", "down_added", "combine_spread", "scores_summed", "exp_done", "probs_copied", "pv_summed",
          "head_out")
PRIME = 16


def build(nc, A, out):
    with ExitStack() as ctx:
        k = Kernel(nc, ctx, A)
        for name in PRIMED:
            k.tally.claim(name, PRIME)
        k.block_one()
        if not A.get("stop"):
            k.block_two()
        items = k.ring.n
        stored = k.tally.sem("output_stored")
        loaded = [k.tally.sem(f"slot_{i}_loaded") for i in range(SLOTS)]
        used = k.tally.sem("weights_used")
        done = {n: k.tally.sem(n + "_stage_done") for n in ENGINE_NAMES}
        block = ctx.enter_context(nc.Block())

        @block.sync
        def _(sp):
            def load(item, slot):
                sp.dma_start(k.slots[:, slot, :], A["weights"][bass.ds(item, 1), :, :].rearrange("a p c -> p (a c)")
                             ).then_inc(loaded[slot], 16)

            for slot in range(SLOTS):
                load(slot, slot)
            with sp.Fori(1, items // SLOTS) as i:
                for slot in range(SLOTS):
                    sp.wait_ge(used, i * SLOTS + (slot - SLOTS + 1))
                    load(i * SLOTS + slot, slot)
            for item in range(items // SLOTS * SLOTS, items):
                sp.wait_ge(used, item - SLOTS + 1)
                load(item, item % SLOTS)
            for name in ENGINE_NAMES:
                sp.wait_ge(done[name], len(k.stages))
            sp.dma_start(out, k.x_t[:, :, CTX:ALLTOK]).then_inc(stored, 16)
            sp.wait_ge(stored, 16)

        @block.tensor
        def _(pe):
            for s in k.stages:
                enter(s, pe, "tensor")
                s.tensor(pe)
                leave(s, pe, "tensor")

        @block.scalar
        def _(act):
            for s in k.stages:
                enter(s, act, "scalar")
                s.scalar(act)
                leave(s, act, "scalar")

        @block.vector
        def _(dve):
            for s in k.stages:
                enter(s, dve, "vector")
                s.vector(dve)
                leave(s, dve, "vector")

        @block.gpsimd
        def _(pool):
            for name in PRIMED:
                pool.drain().then_inc(k.tally.sem(name), PRIME)
            for s in k.stages:
                enter(s, pool, "gpsimd")
                s.gpsimd(pool)
                leave(s, pool, "gpsimd")


def fmaj(v, tiles=None):
    v = np.asarray(v)
    v = v.reshape(v.shape[0], -1)
    return v.reshape(-1, P, v.shape[1]).transpose(1, 0, 2).reshape(P, -1)


def rows(v):
    v = np.asarray(v)
    v = v.reshape(v.shape[0], -1)
    o = np.zeros((P, v.shape[1]), np.float32)
    o[:v.shape[0]] = v
    return o


def bucket(d):
    exact = REL_BUCKETS // 2
    big = exact + (np.log(np.maximum(d, 1).astype(np.float32) / np.float32(exact)) / np.float32(np.log(REL_MAX / exact))
                   * np.float32(REL_BUCKETS - exact)).astype(np.int32)
    return np.where(d < exact, np.maximum(d, 0), np.minimum(big, REL_BUCKETS - 1))


def block_diag(blocks):
    n = len(blocks)
    o = np.zeros((P, P), np.float32)
    for i, b in enumerate(blocks):
        o[i * P // n:(i + 1) * P // n, i * P // n:(i + 1) * P // n] = b
    return o


CONST_AT = {}


def pack_consts(parts):
    at, cols = 0, []
    for name, v in parts:
        CONST_AT[name] = at
        at += v.shape[1]
        cols.append(np.asarray(v, np.float32))
    return np.ascontiguousarray(np.concatenate(cols, axis=1))


def pack_items(w):
    n = -(-w.shape[1] // 256) * 256
    o = np.zeros((D, n), np.float32)
    o[:, :w.shape[1]] = w
    return o.reshape(KT, P, n // 256, 256).transpose(2, 1, 0, 3).reshape(n // 256, P, SLOT_COLS)


def pack_down(w):
    return w.reshape(2, P, D).transpose(1, 0, 2).reshape(1, P, SLOT_COLS)


def expert_items(chunks, paired):
    out, n = [], len(chunks)
    for i in range(0, n, 2):
        pair = [(pack_items(g), pack_items(u), pack_down(d)) for g, u, d in chunks[i:i + 2]]
        if paired and len(pair) == 2:
            out += [pair[0][0], pair[0][1], pair[1][0], pair[1][1], pair[0][2], pair[1][2]]
        else:
            out += [x for p in pair for x in p]
    return out


def host_block_one(i):
    w = np.asarray(i["w_in"])[0]
    g = GROUP
    fox = 5 * g
    q, k_, v, f = (w[:, fox:fox + g], w[:, fox + g:fox + 2 * g], w[:, fox + 2 * g:fox + 3 * g],
                   w[:, fox + 3 * g:fox + 3 * g + 4])
    nq = fox + 3 * g + 4
    kv = [w[:, nq + g + j * HD:nq + g + (j + 1) * HD] for j in range(6)]
    gate = w[:, nq + g + 6 * HD:nq + g + 6 * HD + 12]
    items = [pack_items(w[:, 0:fox]),
             pack_items(np.concatenate([q, k_, w[:, nq:nq + g], kv[0], kv[1], kv[2], kv[4]], axis=1)),
             pack_items(v), pack_items(np.concatenate([kv[3], kv[5], gate, f], axis=1)),
             pack_items(np.asarray(i["w_out"])[0])]
    gu, dn = np.asarray(i["w_gate_up"])[0], np.asarray(i["w_down"])[0]
    items += expert_items([(gu[:, c:c + 256], gu[:, D_FF + c:D_FF + c + 256], dn[c:c + 256])
                           for c in range(0, D_FF, 256)], True)
    y = np.arange(896)[None, :]
    p = np.arange(P)[:, None]
    lw = np.asarray(i["lru_w_gates"])[0]
    lb = np.asarray(i["lru_b_gates"])[0]
    consts = [
        ("ident", np.eye(P)), ("eps", np.full((P, 1), EPS)), ("one", np.ones((P, 1))),
        ("ones_1024", np.full((P, P), 1 / D)), ("ones_256", np.full((P, P), 1 / 256)),
        ("ones_64", np.full((P, HD), 1 / HD)),
        ("norm_mix", fmaj(i["norm_mix"][0])), ("norm_ffn", fmaj(i["norm_ffn"][0])),
        ("lru_cw", fmaj(np.asarray(i["lru_conv_w"])[0].T)), ("lru_cb", fmaj(i["lru_conv_b"][0])),
        ("lru_wg", np.concatenate([block_diag(lw[a, 2 * c:2 * c + 2]) for a in (0, 1) for c in (0, 1)], axis=1)),
        ("lru_gb", np.concatenate([fmaj(lb[0]), fmaj(lb[1])], axis=1)), ("lru_lam", fmaj(i["lru_lambda"][0])),
        ("sc_w", fmaj(np.asarray(i["sc_conv_w"])[0].T)),
        ("fox_fb", rows(np.asarray(i["fox_f_bias"])[0])),
        ("fox_gq", rows(np.asarray(i["fox_qk_norm"])[0, 0])), ("fox_gk", rows(np.asarray(i["fox_qk_norm"])[0, 1])),
        ("nsa_gq", rows(np.asarray(i["nsa_qk_norm"])[0, 0])), ("nsa_gkc", rows(np.asarray(i["nsa_qk_norm"])[0, 1])),
        ("nsa_gks", rows(np.asarray(i["nsa_qk_norm"])[0, 2])), ("nsa_gkw", rows(np.asarray(i["nsa_qk_norm"])[0, 3])),
        ("cmp_w2", np.concatenate([np.asarray(i["nsa_cmp_w2"])[0, 0], np.asarray(i["nsa_cmp_w2"])[0, 1]], axis=1)),
        ("cmp_pos", rows(np.concatenate([np.asarray(i["nsa_cmp_pos"])[0, 0].T, np.asarray(i["nsa_cmp_pos"])[0, 1].T], axis=1))),
        ("nsa_gb", np.tile(np.asarray(i["nsa_gate_bias"])[0][None, :], (P, 1))),
        ("cmp_valid", (np.arange(P) >= CMP_LEN - 1).astype(np.float32)[:, None]),
        ("out_norm", fmaj(np.asarray(i["out_norm"])[0].reshape(-1))),
    ]
    dist = np.arange(1024) - (SEQ - 1)
    fwd = np.zeros((33, 1024), np.float32)
    fwd[np.where(dist >= 0, bucket(dist), 32), np.arange(1024)] = 1.0
    fwd[32] *= NEG
    rel = np.concatenate([np.asarray(i["rel_bias"]), np.ones((1, 4), np.float32)])
    back = np.zeros_like(fwd)
    back[:, 0:1023] = fwd[:, 0:1023][:, ::-1]
    extra = {
        "causal": np.where(y - 384 <= p, 0.0, NEG).astype(np.float32),
        "x": np.asarray(i["x"])[0].T.reshape(KT, P, SEQ).transpose(1, 0, 2),
        "onehots": np.stack([back, fwd], axis=1), "rel": rel,
        "cmp_w1": np.asarray(i["nsa_cmp_w1"])[0].transpose(2, 0, 1, 3),
    }
    return items, consts, extra


class Views:
    pass


def rope_tables(lead, half, repeat_cos=True):
    inv = (np.float32(ROPE_THETA) ** (-np.arange(half, dtype=np.float32) / half)).astype(np.float32)
    pos = np.arange(SEQ)
    axes = [(pos // GRID_W).astype(np.float32), (pos % GRID_W).astype(np.float32)]
    d = lead + 4 * half
    cos, sin, rot = np.ones((d, SEQ), np.float32), np.zeros((d, SEQ), np.float32), np.zeros((d, d), np.float32)
    for i, axis in enumerate(axes):
        ang = inv[:, None] * axis[None, :]
        for part in (0, 1):
            at = lead + 2 * half * i + half * part
            cos[at:at + half], sin[at:at + half] = np.cos(ang), np.sin(ang)
        for j in range(half):
            a = lead + 2 * half * i + j
            rot[a, a + half], rot[a + half, a] = -1.0, 1.0
    return np.concatenate([cos, sin], axis=1), np.ascontiguousarray(rot.T)


ROPE_THETA, GRID_W = 10000.0, 64
RWC_COLS = 2606


def host_block_two(i):
    n = lambda name: np.asarray(i[name + "_2"])
    items = []
    for layer in (0, 1):
        items.append(pack_items(n("ada_w")[layer]))
    w = n("ab_w_in")[0]
    rwc = 3 * RW_DIM + 384
    items += [pack_items(w[:, rwc:rwc + 672]), pack_items(w[:, 0:rwc]), pack_items(n("ab_w_out")[0])]

    def moe(layer):
        g, u, d = n("moe_w_gate")[layer], n("moe_w_up")[layer], n("moe_w_down")[layer]
        chunks = [(g[e], u[e], d[e]) for e in range(N_EXP)]
        chunks.append((n("shared_w_gate")[layer], n("shared_w_up")[layer], n("shared_w_down")[layer]))
        return expert_items(chunks, paired=layer == 1)

    items += moe(0)
    w = n("gqa_w_in")[0]
    items += [pack_items(w[:, 0:1024]), pack_items(w[:, 1024:1280]), pack_items(w[:, 1280:1536]),
              pack_items(n("gqa_w_out")[0])]
    items += moe(1)

    mla_rope, mla_rot = rope_tables(MLA_NOPE, MLA_ROPE // 4)
    gqa_rope, gqa_rot = rope_tables(0, HD // 4)
    place = np.zeros((32, 96), np.float32)
    place[np.arange(32), 64 + np.arange(32)] = 1.0
    consts = [
        ("ada_b", np.concatenate([fmaj(n("ada_b")[0]), fmaj(n("ada_b")[1])], axis=1)),
        ("norm12", np.concatenate([fmaj(n(f"norm{j}_g")[l]) for l in (0, 1) for j in (1, 2)], axis=1)),
        ("g_qa", fmaj(n("mla_g_qa")[0])), ("g_kva", fmaj(n("mla_g_kva")[0])),
        ("ones_384", np.full((P, P), 1 / 384)), ("ones_96", np.full((P, 96), 1 / 96)),
        ("mla_gq", rows(n("mla_g_q")[0])), ("mla_gk", rows(n("mla_g_k")[0])),
        ("gqa_gq", rows(n("gqa_g_q")[0])), ("gqa_gk", rows(n("gqa_g_k")[0])),
        ("mla_rot", rows(mla_rot)), ("gqa_rot", rows(gqa_rot)), ("place", rows(place)),
        ("router_w", fmaj(n("router_w"))), ("router_b", np.tile(n("router_b")[None, :], (P, 1))),
    ]
    kv = n("mla_w_kv_up")[0].reshape(2, P, MLA_H, 128)
    wk = np.zeros((P, 2, MLA_H, 96), np.float32)
    wk[..., 0:64] = kv[..., 0:64].transpose(1, 0, 2, 3)
    wv = kv[..., 64:128].transpose(1, 0, 2, 3)
    s, t = np.arange(P)[:, None], np.arange(P)[None, :]

    def joins(m):
        return ((s // (2 * m) == t // (2 * m)) & (s % (2 * m) < m) & (t % (2 * m) >= m)).astype(np.float32)

    csts = np.zeros((P, 4, 8), np.float32)
    vecs = [n("rw_w0")[0, 0], n("rw_w0")[0, 1], n("rw_a0")[0, 0], n("rw_a0")[0, 1], n("rw_k_k")[0], n("rw_k_a")[0]]
    for j, x in enumerate(vecs):
        csts[:, :, j] = fmaj(x)
    same = (s // 64 == t // 64).astype(np.float32)
    rw_consts = np.concatenate(
        [n("rw_w2")[0].reshape(P, RW_DIM), n("rw_a2")[0].reshape(P, RW_DIM), csts.reshape(P, 32),
         (s < t).astype(np.float32), (s <= t).astype(np.float32), joins(1).T, joins(1)]
        + [joins(2 ** l) for l in range(1, 7)]
        + [same, same / 64, fmaj(n("rw_ln_w")[0]), fmaj(n("rw_ln_b")[0]), fmaj(n("rw_r_k")[0].reshape(-1)),
           np.full((P, 1), 1e-12), np.full((P, 1), 64e-5)], axis=1).astype(np.float32)
    sel = np.zeros((17, 17, P), np.float32)
    sel[np.arange(17), np.arange(17), :] = 1.0
    c2 = np.stack([n("c")[0], n("c_ctx")], axis=1)
    extra = {
        "ctx": n("ctx")[0].T.reshape(KT, P, CTX).transpose(1, 0, 2), "c": fmaj(c2),
        "mla_q_up": n("mla_w_q_up")[0].reshape(3, P, 768).transpose(1, 0, 2), "mla_rope": mla_rope, "gqa_rope": gqa_rope,
        "mla_kv_up": np.concatenate([wk.reshape(P, -1), wv.reshape(P, -1)], axis=1),
        "rw_mu": fmaj(n("rw_mu")[0]), "rw_consts": rw_consts, "rw_g2": n("rw_g2")[0], "sel_rows": sel.reshape(17, 17 * P),
    }
    return items, consts, extra


def kernel(**inputs):
    import concourse.bacc as bacc
    from concourse.bass_utils import run_bass_kernel_spmd

    items1, consts1, extra1 = host_block_one(inputs)
    items2, consts2, extra2 = host_block_two(inputs)
    arrays = {"weights": np.concatenate(items1 + items2), "consts": pack_consts(consts1 + consts2), **extra1, **extra2}
    nc = bacc.Bacc("TRN2", target_bir_lowering=False, num_devices=1)
    A, feed = {}, {}
    for name, a in arrays.items():
        a = np.ascontiguousarray(a, dtype=np.float32)
        feed[f"in_{name}"] = a
        A[name] = nc.dram_tensor(f"in_{name}", a.shape, F32, kind="ExternalInput").ap()
    A["bias_line"] = nc.dram_tensor("bias_line", [4, P, 1024], F32, kind="Internal").ap()
    out = nc.dram_tensor("out_x", [P, KT, SEQ], F32, kind="ExternalOutput").ap()
    build(nc, A, out)
    r = run_bass_kernel_spmd(nc, [feed], core_ids=[0])
    return np.ascontiguousarray(r.results[0]["out_x"].transpose(1, 0, 2).reshape(D, SEQ).T)[None]
```

```python
from contextlib import ExitStack, nullcontext

import numpy as np
import concourse.bass as bass
from concourse import mybir

P = 128
F32 = mybir.dt.float32
F32R = mybir.dt.float32r
ALU = mybir.AluOpType
ACT = mybir.ActivationFunctionType
AX_X = mybir.AxisListType.X

D = 1024
KT = D // P
SEQ = 512
CTX = 256
ALLTOK = CTX + SEQ
HD = 64
GROUP = 256
D_FF = ((8 * D // 3 + 255) // 256) * 256
FF_CHUNK = 256
SLOTS = 6
SLOT_COLS = KT * 256
EPS = 1e-6
NEG = -1e30
CMP_LEN, CMP_STRIDE, CMP_HID = 32, 16, 128
N_CMP = (SEQ - CMP_LEN) // CMP_STRIDE + 1
REL_BUCKETS, REL_MAX = 32, 128
N_EXP = 16
MLA_H, MLA_QK, MLA_NOPE, MLA_ROPE, MLA_V = 8, 96, 64, 32, 64
Q_RANK, KV_RANK = 384, 256
RW_DIM = 512
GQA_H, GQA_KV = 16, 4
CH = 128
N_CH = ALLTOK // CH


class Tally:

    def __init__(self, nc, ctx):
        self.nc, self.ctx, self.sems, self.total = nc, ctx, {}, {}

    def sem(self, name):
        if name not in self.sems:
            self.sems[name] = self.ctx.enter_context(self.nc.semaphore(name))
            self.total[name] = 0
        return self.sems[name]

    def claim(self, name, n):
        self.sem(name)
        base = self.total[name]
        self.total[name] += n
        return base


class Stage:

    def __init__(self, k):
        self.k, self.nc, self.tally = len(k.stages), k.nc, k.tally
        self.kern = k
        self.loads, self.zeros = [], []
        k.stages.append(self)

    def count(self, name, n):
        return self.tally.sem(name), self.tally.claim(name, n)

    def beside(self, loads=(), zeros=()):
        self.loads, self.zeros = list(loads), list(zeros)
        self.arrived = self.count("extra_arrived", 16 * len(self.loads))

    def start_beside(self, pool):
        for dst, src in self.loads:
            pool.dma_start(dst, src).then_inc(self.arrived[0], 16)
        for x in self.zeros:
            self.nc.gpsimd.memset(x, 0.0)

    def end_beside(self, pool):
        if self.loads:
            pool.wait_ge(self.arrived[0], self.arrived[1] + 16 * len(self.loads))

    def tensor(self, pe):
        pass

    def scalar(self, act):
        pass

    def vector(self, dve):
        pass

    def gpsimd(self, pool):
        pass



def enter(stage, eng, me):
    if stage.k:
        for other in ("tensor", "scalar", "vector", "gpsimd"):
            if other != me:
                eng.wait_ge(stage.tally.sem(other + "_stage_done"), stage.k)


def leave(stage, eng, me):
    eng.drain().then_inc(stage.tally.sem(me + "_stage_done"), 1)


class Ring:

    def __init__(self):
        self.n = 0

    def take(self, n):
        first = self.n
        self.n += n
        return first


def segments(tokens):
    return [(0, CTX), (CTX, ALLTOK)] if tokens == ALLTOK else [(CTX, ALLTOK)]


class Norm(Stage):

    def __init__(self, k, src, dst, tiles, group, segs, gain, ones, shift=None):
        super().__init__(k)
        self.src, self.dst, self.tiles, self.group = src, dst, tiles, group
        self.segs, self.gain, self.ones, self.shift = segs, gain, ones, shift
        self.units = [(g, s) for s in segs for g in range(tiles // group)]
        self.squares = self.count("norm_squares", len(segs))
        self.sums = self.count("norm_sums", len(self.units))
        self.roots = self.count("norm_roots", len(self.units))
        self.scaled = self.count("norm_scaled", len(self.units))

    def bank(self, n):
        a, b = self.units[n][1]
        return self.kern.ps[n % 4][:, 0:b - a]

    def root(self, n):
        a, b = self.units[n][1]
        return self.kern.rstd[:, n % 4, 0:b - a]

    def scalar(self, act):
        nc = self.nc
        for a, b in self.segs:
            nc.scalar.activation(self.dst[:, 0:self.tiles, a:b], self.src[:, 0:self.tiles, a:b],
                                 ACT.Square).then_inc(self.squares[0], 1)
        for n in range(len(self.units)):
            act.wait_ge(self.sums[0], self.sums[1] + n + 1)
            if n >= 4:
                act.wait_ge(self.scaled[0], self.scaled[1] + n - 3)
            nc.scalar.activation(self.root(n), self.bank(n), ACT.Sqrt,
                                 bias=self.kern.eps[:, 0:1]).then_inc(self.roots[0], 1)
        if self.shift is not None:
            for n, (g, (a, b)) in enumerate(self.units):
                act.wait_ge(self.scaled[0], self.scaled[1] + n + 1)
                for t in range(g * self.group, (g + 1) * self.group):
                    nc.scalar.activation(self.dst[:, t, a:b], self.dst[:, t, a:b], ACT.Identity,
                                         bias=self.shift(t, a))

    def tensor(self, pe):
        for n, (g, (a, b)) in enumerate(self.units):
            pe.wait_ge(self.squares[0], self.squares[1] + self.segs.index((a, b)) + 1)
            if n >= 4:
                pe.wait_ge(self.roots[0], self.roots[1] + n - 3)
            for i in range(self.group):
                last = self.nc.tensor.matmul(self.bank(n), self.ones, self.dst[:, g * self.group + i, a:b],
                                             start=(i == 0), stop=(i == self.group - 1))
            last.then_inc(self.sums[0], 1)

    def vector(self, dve):
        nc = self.nc
        for n, (g, (a, b)) in enumerate(self.units):
            dve.wait_ge(self.roots[0], self.roots[1] + n + 1)
            nc.vector.reciprocal(self.root(n), self.root(n))
            dve.drain()
            for t in range(g * self.group, (g + 1) * self.group):
                last = nc.vector.scalar_tensor_tensor(
                    out=self.dst[:, t, a:b], in0=self.src[:, t, a:b], scalar=self.gain(t, a),
                    in1=self.root(n), op0=ALU.mult, op1=ALU.mult)
            last.then_inc(self.scaled[0], 1)


class Split(Stage):

    def __init__(self, k, src, hi, lo, tiles=KT):
        super().__init__(k)
        self.src, self.hi, self.lo, self.tiles = src, hi, lo, tiles
        self.rounded = self.count("operand_rounded", tiles)

    def scalar(self, act):
        for t in range(self.tiles):
            self.nc.scalar.activation(self.hi[:, t, :], self.src[:, t, :], ACT.Copy).then_inc(self.rounded[0], 1)

    def vector(self, dve):
        for t in range(self.tiles):
            dve.wait_ge(self.rounded[0], self.rounded[1] + t + 1)
            self.nc.vector.tensor_tensor(out=self.lo[:, t, :], in0=self.src[:, t, :], in1=self.hi[:, t, :].bitcast(F32),
                                         op=ALU.subtract)


class Project(Stage):

    def __init__(self, k, src, segs, tiles, out, at, gate=None, heads=False):
        super().__init__(k)
        self.src, self.segs, self.tiles, self.out, self.gate, self.heads = src, segs, tiles, out, gate, heads
        self.items = -(-tiles // 2)
        self.first = k.ring.take(self.items)
        self.w_hi = k.part_r(at, 2, KT, P)
        k.tally.claim("weights_used", self.items)
        self.groups = [(t, s) for t in range(tiles) for s in segs]
        self.rounded, self.split = self.count("tile_rounded", tiles), self.count("tile_split", tiles)
        self.summed = self.count("tile_summed", len(self.groups))
        self.moved = [self.count(f"tile_moved_{e}", (len(self.groups) + 1 - e) // 2) for e in (0, 1)]

    def bank(self, n):
        a, b = self.groups[n][1]
        return self.kern.ps[n % 8][:, 0:b - a]

    def tile_weights(self, slots, t):
        w = slots[:, (self.first + t // 2) % SLOTS, :].rearrange("p (k c) -> p k c", k=KT)
        return w[:, :, t % 2 * P:(t % 2 + 1) * P]

    def gpsimd(self, pool):
        for t in range(self.tiles):
            pool.wait_ge(self.rounded[0], self.rounded[1] + t + 1)
            self.nc.gpsimd.tensor_tensor(out=self.tile_weights(self.kern.slots_r, t), in0=self.tile_weights(self.kern.slots, t),
                                         in1=self.w_hi[:, t % 2].bitcast(F32), op=ALU.subtract).then_inc(self.split[0], 1)

    def tensor(self, pe):
        hi, lo = self.src
        for n, (t, (a, b)) in enumerate(self.groups):
            if n % len(self.segs) == 0:
                pe.wait_ge(self.split[0], self.split[1] + t + 1)
            if n >= 8:
                s, base = self.moved[n % 2]
                pe.wait_ge(s, base + (n - 8) // 2 + 1)
            w_hi, w_lo = self.w_hi[:, t % 2], self.tile_weights(self.kern.slots_r, t)
            passes = [(w, x, kt) for kt in range(KT) for w, x in ((w_hi, hi), (w_hi, lo), (w_lo, hi))]
            for i, (w, x, kt) in enumerate(passes):
                last = self.nc.tensor.matmul(self.bank(n), w[:, kt, :], x[:, kt, a:b], start=(i == 0),
                                             stop=(i == len(passes) - 1))
            last.then_inc(self.summed[0], 1)
            if n % len(self.segs) == len(self.segs) - 1 and (t % 2 or t == self.tiles - 1):
                pe.drain().then_inc(self.tally.sem("weights_used"), 1)

    def pieces(self, n):
        t, (a, b) = self.groups[n]
        if not self.heads:
            return [(self.bank(n), self.out(t, a, b))]
        return [(self.bank(n)[i * HD:(i + 1) * HD, :], self.out(2 * t + i, a, b)) for i in (0, 1)]

    def scalar(self, act):
        ns = len(self.segs)
        for t in range(self.tiles + 2):
            if t < self.tiles:
                if t % 2 == 0:
                    self.kern.slot_ready(act, self.first + t // 2)
                if t >= 2:
                    act.wait_ge(self.summed[0], self.summed[1] + (t - 1) * ns)
                self.nc.scalar.activation(self.w_hi[:, t % 2], self.tile_weights(self.kern.slots, t),
                                          ACT.Copy).then_inc(self.rounded[0], 1)
            for n in range((t - 2) * ns, (t - 1) * ns):
                if self.gate is not None or t < 2 or n % 2:
                    continue
                act.wait_ge(self.summed[0], self.summed[1] + n + 1)
                for x, dst in self.pieces(n):
                    last = self.nc.scalar.activation(dst, x, ACT.Copy)
                last.then_inc(self.moved[0][0], 1)

    def vector(self, dve):
        for n, (t, (a, b)) in enumerate(self.groups):
            if self.gate is None and n % 2 == 0:
                continue
            dve.wait_ge(self.summed[0], self.summed[1] + n + 1)
            for x, dst in self.pieces(n):
                if self.gate is None:
                    last = self.nc.vector.tensor_copy(dst, x)
                else:
                    last = self.nc.vector.scalar_tensor_tensor(out=dst, in0=x, scalar=self.gate(t, a), in1=dst,
                                                               op0=ALU.mult, op1=ALU.add)
            last.then_inc(self.moved[n % 2][0], 1)


class TokenProject(Stage):

    def __init__(self, k, src, token_tiles, cols, out):
        super().__init__(k)
        self.src, self.token_tiles, self.cols, self.out = src, token_tiles, cols, out
        self.first = k.ring.take(len(cols))
        k.tally.claim("weights_used", len(cols))
        self.groups = [(i, t) for i in range(len(cols)) for t in token_tiles]
        self.summed = self.count("rows_summed", len(self.groups))
        self.moved = self.count("rows_moved", len(self.groups))

    def bank(self, n):
        return self.kern.ps[n % 4][:, 0:self.cols[self.groups[n][0]]]

    def tensor(self, pe):
        n = 0
        for i, cols in enumerate(self.cols):
            w = self.kern.slot_ready(pe, self.first + i).rearrange("p (k c) -> p k c", k=KT)
            for t in self.token_tiles:
                if n >= 4:
                    pe.wait_ge(self.moved[0], self.moved[1] + n - 3)
                for kt in range(KT):
                    last = self.nc.tensor.matmul(self.bank(n), self.src[:, kt, t * P:(t + 1) * P], w[:, kt, 0:cols],
                                                 start=(kt == 0), stop=(kt == KT - 1))
                last.then_inc(self.summed[0], 1)
                n += 1
            pe.drain().then_inc(self.tally.sem("weights_used"), 1)

    def vector(self, dve):
        for n, (i, t) in enumerate(self.groups):
            dve.wait_ge(self.summed[0], self.summed[1] + n + 1)
            self.nc.vector.tensor_copy(self.out(t, i), self.bank(n)).then_inc(self.moved[0], 1)


class Experts(Stage):

    def __init__(self, k, src, dst, segs, chunks, gate, comb=None):
        super().__init__(k)
        self.src, self.dst, self.segs, self.chunks, self.gate, self.comb = src, dst, segs, chunks, gate, comb
        self.first = k.ring.take(3 * chunks)
        k.tally.claim("weights_used", 3 * chunks)
        self.rounded, self.split = self.count("weights_rounded", 3 * chunks), self.count("weights_split", 3 * chunks)
        u = chunks * len(segs)
        self.ns = len(segs)
        self.gu = self.count("gate_up_summed", 2 * u)
        self.sig = self.count("gate_sigmoid", 2 * u)
        self.raw = self.count("hidden_made", 2 * u)
        self.hid_hi = self.count("hidden_rounded", 2 * u)
        self.hid = self.count("hidden_ready", 2 * u)
        self.down = self.count("down_summed", 8 * u)
        self.added = self.count("down_added", 8 * u)
        if comb is not None:
            self.sel = self.count("expert_selected", chunks)
            self.cb = self.count("combine_spread", u)

    def item(self, chunks, c, kind):
        if self.ns == 1 and chunks == 2:
            return self.first + (2 * c + kind if kind < 2 else 4 + c)
        return self.first + 3 * c + kind

    def turns(self, eng, body):
        if self.chunks > 1:
            with eng.Fori(0, self.chunks // 2) as i:
                body(i, 2)
        if self.chunks % 2:
            body(self.chunks // 2, 1)

    def gu_bank(self, which, ft):
        return self.kern.ps[2 * ft + which]

    def tensor(self, pe):
        nc, kern, ns = self.nc, self.kern, self.ns

        def body(i, chunks):
            units = [(c, s) for c in range(chunks) for s in range(ns)]

            def weights(item, **shape):
                pe.wait_ge(self.split[0], i * 6 + (self.split[1] + item - self.first + 1))
                return [w.rearrange("p (k c) -> p k c", **shape) for w in
                        (kern.w_hi[:, item % 3, :], kern.slots_r[:, item % SLOTS, :])]

            def products(bank, w, x, n):
                for k in range(n):
                    for j, (p, q) in enumerate(((0, 0), (0, 1), (1, 0))):
                        last = nc.tensor.matmul(bank, w(p, k), x(q, k), start=(k == j == 0), stop=(k == n - 1 and j == 2))
                return last

            def gate_up(v):
                c, s = units[v]
                a, b = self.segs[s]
                u = i * (2 * ns) + v
                for which in (0, 1):
                    w = weights(self.item(chunks, c, which), k=KT)
                    for ft in (0, 1):
                        if which == 0:
                            pe.wait_ge(self.raw[0], u * 2 + (self.raw[1] + ft - 1))
                        last = products(self.gu_bank(which, ft)[:, 0:b - a], lambda p, k: w[p][:, k, ft * P:(ft + 1) * P],
                                        lambda q, k: self.src[q][:, k, a:b], KT)
                        if which:
                            last.then_inc(self.gu[0], 1)
                    if which == 0 and self.comb is not None:
                        if s == 0:
                            pe.wait_ge(self.sel[0], self.sel[1] + 1 + c + i * 2)
                        nc.tensor.matmul(kern.ps[4][:, 0:b - a], kern.sel_buf[0:self.chunks, c, :],
                                         self.comb[0:self.chunks, a:b], start=True, stop=True).then_inc(self.cb[0], 1)
                if s == ns - 1:
                    pe.drain().then_inc(self.tally.sem("weights_used"), 2)

            def down(v):
                c, s = units[v]
                a, b = self.segs[s]
                u = i * (2 * ns) + v
                w = weights(self.item(chunks, c, 2), k=2)
                pe.wait_ge(self.hid[0], u * 2 + (self.hid[1] + 2))
                for n in range(KT):
                    pe.wait_ge(self.added[0], u * 8 + (self.added[1] + n - (1 if n < 2 else 2)))
                    products(kern.ps[5 + n % 3][:, 0:b - a], lambda p, k: w[p][:, k, n * P:(n + 1) * P],
                             lambda q, k: kern.hidden[q][:, v % 2, k, 0:b - a], 2).then_inc(self.down[0], 1)
                if s == ns - 1:
                    pe.drain().then_inc(self.tally.sem("weights_used"), 1)

            gate_up(0)
            for v in range(1, len(units)):
                gate_up(v)
                down(v - 1)
            down(len(units) - 1)

        self.turns(pe, body)

    def scalar(self, act):
        nc, kern, ns = self.nc, self.kern, self.ns

        def body(i, chunks):
            def rounding(*items):
                for j in items:
                    item = self.first + j
                    kern.slot_ready(act, item, turn=i)
                    act.wait_ge(self.tally.sem("weights_used"), i * 6 + (item - 2))
                    nc.scalar.activation(kern.w_hi[:, item % 3, :], kern.slot(item), ACT.Copy).then_inc(self.rounded[0], 1)

            rounding(0, 1, 2)
            for v in range(chunks * ns):
                c, s = divmod(v, ns)
                if chunks == ns == 2 and v == 3:
                    rounding(5)
                a, b = self.segs[s]
                u = i * (2 * ns) + v
                if s == 0 and self.comb is not None:
                    act.wait_ge(self.cb[0], u + (self.cb[1] - ns))
                    nc.scalar.activation(kern.sel_buf[0:self.chunks, c, :],
                                         kern.sel_rows[0:self.chunks, bass.ds((i * 2 + c) * P, P)],
                                         ACT.Copy).then_inc(self.sel[0], 1)
                for ft in (0, 1):
                    act.wait_ge(self.gu[0], u * 2 + (self.gu[1] + ft + 1))
                    act.wait_ge(self.hid[0], u * 2 + (self.hid[1] + ft - 1))
                    nc.scalar.activation(kern.sigm[:, ft, 0:b - a], self.gu_bank(0, ft)[:, 0:b - a],
                                         ACT.Sigmoid).then_inc(self.sig[0], 1)
                if chunks == 2 and v == ns - 1:
                    rounding(3, 4)
                if chunks == 2 and ns == 1 and v == 1:
                    rounding(5)
                for ft in (0, 1):
                    act.wait_ge(self.raw[0], u * 2 + (self.raw[1] + ft + 1))
                    nc.scalar.activation(kern.hidden[0][:, v % 2, ft, 0:b - a], kern.sigm[:, ft, 0:b - a],
                                         ACT.Copy).then_inc(self.hid_hi[0], 1)

        self.turns(act, body)

    def vector(self, dve):
        nc, kern, ns = self.nc, self.kern, self.ns

        def body(i, chunks):
            units = [(c, s) for c in range(chunks) for s in range(ns)]

            def hidden(v):
                a, b = self.segs[units[v][1]]
                u = i * (2 * ns) + v
                n = b - a
                for ft in (0, 1):
                    dve.wait_ge(self.sig[0], u * 2 + (self.sig[1] + ft + 1))
                    x = kern.sigm[:, ft, 0:n]
                    nc.vector.tensor_tensor(out=x, in0=x, in1=self.gu_bank(0, ft)[:, 0:n], op=ALU.mult)
                    dve.drain()
                    last = nc.vector.tensor_tensor(out=x, in0=x, in1=self.gu_bank(1, ft)[:, 0:n], op=ALU.mult)
                    if self.comb is not None:
                        dve.drain()
                        dve.wait_ge(self.cb[0], u + (self.cb[1] + 1))
                        last = nc.vector.tensor_tensor(out=x, in0=x, in1=kern.ps[4][:, 0:n], op=ALU.mult)
                    last.then_inc(self.raw[0], 1)

            def remainder(v):
                a, b = self.segs[units[v][1]]
                u, n = i * (2 * ns) + v, b - a
                for ft in (0, 1):
                    dve.wait_ge(self.hid_hi[0], u * 2 + (self.hid_hi[1] + ft + 1))
                    hi, lo = (x[:, v % 2, ft, 0:n] for x in kern.hidden)
                    nc.vector.tensor_tensor(out=lo, in0=kern.sigm[:, ft, 0:n], in1=hi.bitcast(F32),
                                            op=ALU.subtract).then_inc(self.hid[0], 1)

            def add(v, tiles=range(KT)):
                a, b = self.segs[units[v][1]]
                u = i * (2 * ns) + v
                for n in tiles:
                    dve.wait_ge(self.down[0], u * 8 + (self.down[1] + n + 1))
                    nc.vector.scalar_tensor_tensor(
                        out=self.dst[:, n, a:b], in0=kern.ps[5 + n % 3][:, 0:b - a], scalar=self.gate(n, a),
                        in1=self.dst[:, n, a:b], op0=ALU.mult, op1=ALU.add).then_inc(self.added[0], 1)

            hidden(0)
            remainder(0)
            for v in range(1, len(units)):
                hidden(v)
                add(v - 1, range(0, 4))
                remainder(v)
                add(v - 1, range(4, KT))
            add(len(units) - 1)

        self.turns(dve, body)

    def gpsimd(self, pool):
        def body(i, chunks):
            for j in range(3 * chunks):
                item = self.first + j
                pool.wait_ge(self.rounded[0], i * 6 + (self.rounded[1] + j + 1))
                self.nc.gpsimd.tensor_tensor(out=self.kern.slots_r[:, item % SLOTS, :], in0=self.kern.slot(item),
                                             in1=self.kern.w_hi[:, item % 3, :].bitcast(F32),
                                             op=ALU.subtract).then_inc(self.split[0], 1)

        self.turns(pool, body)




class HeadNorm(Stage):

    def __init__(self, k, units, ones, d, eps=None):
        super().__init__(k)
        self.units, self.ones, self.d = units, ones, d
        self.eps = k.eps if eps is None else eps
        n = len(units)
        self.sq = self.count("head_squares", n)
        self.sum = self.count("head_sums", n)
        self.root = self.count("head_roots", n)
        self.done = self.count("head_normed", n)

    def scalar(self, act):
        nc, kern, d = self.nc, self.kern, self.d
        for n in range(len(self.units) + 1):
            if n < len(self.units):
                x = self.units[n][0]
                if n >= 2:
                    act.wait_ge(self.sum[0], self.sum[1] + n - 1)
                nc.scalar.activation(kern.scratch[0:d, n % 2, 0:x.shape[-1]], x, ACT.Square).then_inc(self.sq[0], 1)
            if n >= 1:
                m = n - 1
                w = self.units[m][0].shape[-1]
                act.wait_ge(self.sum[0], self.sum[1] + m + 1)
                if m >= 2:
                    act.wait_ge(self.done[0], self.done[1] + m - 1)
                nc.scalar.activation(kern.scratch[0:d, 2 + m % 2, 0:w], kern.ps[m % 4][0:d, 0:w], ACT.Sqrt,
                                     bias=self.eps[0:d, 0:1]).then_inc(self.root[0], 1)

    def tensor(self, pe):
        kern, d = self.kern, self.d
        for n, (x, _) in enumerate(self.units):
            w = x.shape[-1]
            pe.wait_ge(self.sq[0], self.sq[1] + n + 1)
            if n >= 4:
                pe.wait_ge(self.root[0], self.root[1] + n - 3)
            self.nc.tensor.matmul(kern.ps[n % 4][0:d, 0:w], self.ones, kern.scratch[0:d, n % 2, 0:w],
                                  start=True, stop=True).then_inc(self.sum[0], 1)

    def vector(self, dve):
        kern, d = self.kern, self.d
        for n, (x, gain) in enumerate(self.units):
            r = kern.scratch[0:d, 2 + n % 2, 0:x.shape[-1]]
            dve.wait_ge(self.root[0], self.root[1] + n + 1)
            self.nc.vector.reciprocal(r, r)
            dve.drain()
            self.nc.vector.scalar_tensor_tensor(out=x, in0=x, scalar=gain, in1=r, op0=ALU.mult,
                                                op1=ALU.mult).then_inc(self.done[0], 1)


class Rope(Stage):

    def __init__(self, k, units, rot_t, cos, sin, d):
        super().__init__(k)
        self.units, self.rot_t, self.cos, self.sin, self.d = units, rot_t, cos, sin, d
        self.rot = self.count("rope_rotated", len(units))
        self.done = self.count("rope_done", len(units))

    def tensor(self, pe):
        for n, x in enumerate(self.units):
            if n >= 4:
                pe.wait_ge(self.done[0], self.done[1] + n - 3)
            self.nc.tensor.matmul(self.kern.ps[n % 4][0:self.d, :], self.rot_t, x, start=True,
                                  stop=True).then_inc(self.rot[0], 1)

    def vector(self, dve):
        v, d = self.nc.vector, self.d
        for n, x in enumerate(self.units):
            t = self.kern.scratch[0:d, n % 2, :]
            dve.wait_ge(self.rot[0], self.rot[1] + n + 1)
            v.tensor_tensor(out=t, in0=self.kern.ps[n % 4][0:d, :], in1=self.sin, op=ALU.mult)
            v.tensor_tensor(out=x, in0=x, in1=self.cos, op=ALU.mult)
            dve.drain()
            v.tensor_tensor(out=x, in0=x, in1=t, op=ALU.add).then_inc(self.done[0], 1)


class Attention(Stage):

    def __init__(self, k, d, keys, kv_heads, per_kv, q_tiles, q, key, value, out, bias=None, factor=None, add=False):
        super().__init__(k)
        self.d, self.keys, self.hk, self.g, self.nt = d, keys, kv_heads, per_kv, q_tiles
        self.q, self.key, self.value, self.out, self.bias, self.factor, self.add = q, key, value, out, bias, factor, add
        self.biased, self.probs, self.probs_t = k.biased, k.probs, k.probs_t
        self.per = per_kv * q_tiles
        n = kv_heads * self.per
        names = ("q_staged", "scores_summed", "max_ready", "exp_done", "probs_turned", "probs_copied", "pv_summed",
                 "head_out")
        (self.staged, self.scores, self.maxed, self.exped, self.turned, self.copied, self.pv,
         self.outed) = (self.count(x, n) for x in names)
        self.kts = [(i, min(P, keys - i * P)) for i in range(-(-keys // P))]

    def units(self, hk):
        for v in range(self.per):
            yield hk * self.g + v // self.nt, v % self.nt, hk * self.per + v, v % 2

    def s_psum(self, par):
        return self.kern.psum[:, 2 * par:2 * par + 2, :].rearrange("p a b -> p (a b)")[:, 0:self.keys]

    def tensor(self, pe):
        nc, kern = self.nc, self.kern
        pt = kern.psum[:, 4:6, :].rearrange("p a b -> p (a b)")

        def scores(hk, u, par):
            pe.wait_ge(self.staged[0], u + (self.staged[1] + 1))
            s = self.s_psum(par)
            for a in range(0, self.keys, 512):
                b = min(a + 512, self.keys)
                last = nc.tensor.matmul(s[:, a:b], kern.q_stage[0:self.d, par, :], self.key(hk, a, b),
                                        start=True, stop=True)
            last.then_inc(self.scores[0], 1)

        def turn(hk, ahead):
            for v, (h, t, u, par) in enumerate(self.units(hk)):
                pe.wait_ge(self.exped[0], u + (self.exped[1] + 1))
                pe.wait_ge(self.copied[0], u + self.copied[1])
                for i, n in self.kts:
                    last = nc.tensor.transpose(pt[0:n, i * P:i * P + P], self.probs[:, par, i * P:i * P + n],
                                               kern.ident)
                last.then_inc(self.turned[0], 1)
                if ahead or v + 2 < self.per:
                    scores(hk + (v + 2) // self.per, u + 2, par)
                pe.wait_ge(self.copied[0], u + (self.copied[1] + 1))
                pe.wait_ge(self.outed[0], u + (self.outed[1] - 1))
                for i, n in self.kts:
                    last = nc.tensor.matmul(kern.ps[6 + par][:, 0:HD], self.probs_t[0:n, par, i * P:(i + 1) * P],
                                            self.value(i, n, hk), start=(i == 0), stop=(i == len(self.kts) - 1))
                last.then_inc(self.pv[0], 1)

        scores(0, 0, 0)
        scores(0, 1, 1)
        with pe.Fori(0, self.hk - 1) as hk:
            turn(hk, True)
        turn(self.hk - 1, False)

    def gpsimd(self, pool):
        with pool.Fori(0, self.hk) as hk:
            for h, t, u, par in self.units(hk):
                pool.wait_ge(self.scores[0], u + (self.scores[1] - 1))
                self.nc.gpsimd.tensor_copy(self.kern.q_stage[0:self.d, par, :], self.q(h, t)).then_inc(self.staged[0], 1)

    def scalar(self, act):
        nc, kern = self.nc, self.kern
        pt = kern.psum[:, 4:6, :].rearrange("p a b -> p (a b)")

        def exponentials(u, par):
            act.wait_ge(self.maxed[0], u + (self.maxed[1] + 1))
            act.wait_ge(self.outed[0], u + (self.outed[1] - 1))
            src = self.s_psum(par) if self.bias is None else self.biased[:, par, 0:self.keys]
            nc.scalar.activation(self.probs[:, par, 0:self.keys], src, ACT.Exp, bias=kern.neg_max[:, par:par + 1],
                                 accum_out=kern.row_sum[:, par:par + 1]).then_inc(self.exped[0], 1)

        def copy(u, par):
            act.wait_ge(self.turned[0], u + (self.turned[1] + 1))
            act.wait_ge(self.pv[0], u + (self.pv[1] - 1))
            n = self.kts[0][1]
            w = len(self.kts) * P
            nc.scalar.activation(self.probs_t[0:n, par, 0:w], pt[0:n, 0:w], ACT.Copy).then_inc(self.copied[0], 1)

        def turn(hk, ahead):
            for v, (h, t, u, par) in enumerate(self.units(hk)):
                copy(u, par)
                if ahead or v + 1 < self.per:
                    exponentials(u + 1, 1 - par)

        exponentials(0, 0)
        with act.Fori(0, self.hk - 1) as hk:
            turn(hk, True)
        turn(self.hk - 1, False)

    def vector(self, dve):
        nc, kern = self.nc, self.kern

        def maximum(h, t, u, par):
            dve.wait_ge(self.scores[0], u + (self.scores[1] + 1))
            src = self.s_psum(par)
            if self.bias is not None:
                nc.vector.tensor_tensor(out=self.biased[:, par, 0:self.keys], in0=src, in1=self.bias(h, t), op=ALU.add)
                dve.drain()
                src = self.biased[:, par, 0:self.keys]
            nc.vector.reduce_max(kern.row_max[:, par:par + 1], src, AX_X)
            dve.drain()
            nc.vector.tensor_scalar(kern.neg_max[:, par:par + 1], kern.row_max[:, par:par + 1], -1.0, None,
                                    ALU.mult).then_inc(self.maxed[0], 1)

        def output(h, t, u, par):
            dve.wait_ge(self.pv[0], u + (self.pv[1] + 1))
            r, o = kern.row_inv[:, par:par + 1], kern.ps[6 + par][:, 0:HD]
            nc.vector.reciprocal(r, kern.row_sum[:, par:par + 1])
            dve.drain()
            if self.factor is not None:
                nc.vector.tensor_tensor(out=r, in0=r, in1=self.factor(h, t), op=ALU.mult)
                dve.drain()
            dst = self.out(h, t)
            if self.add:
                ins = nc.vector.scalar_tensor_tensor(out=dst, in0=o, scalar=r, in1=dst, op0=ALU.mult, op1=ALU.add)
            else:
                ins = nc.vector.tensor_scalar(dst, o, r, None, ALU.mult)
            ins.then_inc(self.outed[0], 1)

        def turn(hk, ahead):
            units = list(self.units(hk)) + (list(self.units(hk + 1))[0:2] if ahead else [])
            for v in range(self.per):
                if v + 2 < len(units):
                    maximum(*units[v + 2])
                output(*units[v])

        first = list(self.units(0))
        maximum(*first[0])
        maximum(*first[1])
        with dve.Fori(0, self.hk - 1) as hk:
            turn(hk, True)
        turn(self.hk - 1, False)


class Turn(Stage):

    def __init__(self, k, groups):
        super().__init__(k)
        self.groups = groups
        self.turned = self.count("blocks_turned", len(groups))
        self.moved = self.count("blocks_moved", len(groups))

    def tensor(self, pe):
        for n, (blocks, _) in enumerate(self.groups):
            if n >= 4:
                pe.wait_ge(self.moved[0], self.moved[1] + n - 3)
            for i, x in enumerate(blocks):
                last = self.nc.tensor.transpose(self.kern.ps[n % 4][:, i * P:(i + 1) * P], x, self.kern.ident)
            last.then_inc(self.turned[0], 1)

    def scalar(self, act):
        for n, (blocks, dst) in enumerate(self.groups):
            act.wait_ge(self.turned[0], self.turned[1] + n + 1)
            self.nc.scalar.activation(dst, self.kern.ps[n % 4][:, 0:P * len(blocks)],
                                      ACT.Copy).then_inc(self.moved[0], 1)


class FromHbm(Stage):

    def __init__(self, k, pairs):
        super().__init__(k)
        self.beside(pairs)


class ConvMixers(Stage):

    def __init__(self, k, z, y, work):
        super().__init__(k)
        self.z, self.y = z, y
        self.xc, self.r, self.i, self.b, self.t, self.g = (work[:, n * 1024:(n + 1) * 1024].rearrange(
            "p (c t) -> p c t", c=2) for n in range(6))
        self.v = self.count("mixer_vector", 5)
        self.a = self.count("mixer_scalar", 5)
        self.p = self.count("mixer_gates", 1)

    def conv(self, dve, out, x, taps, w, lo):
        for sh in range(lo, taps):
            self.nc.vector.scalar_tensor_tensor(out=out[:, sh:SEQ], in0=x[:, 0:SEQ - sh], scalar=w(taps - 1 - sh),
                                                in1=out[:, sh:SEQ], op0=ALU.mult, op1=ALU.add)
            dve.drain()

    def vector(self, dve):
        v, C, z, sm = self.nc.vector, self.kern.const, self.z, self.kern.small
        for c in (0, 1):
            v.tensor_scalar(self.xc[:, c, :], z[:, c, :], C("lru_cw", c * 4 + 3), C("lru_cb", c), ALU.mult, ALU.add)
            dve.drain()
            self.conv(dve, self.xc[:, c, :], z[:, c, :], 4, lambda i, c=c: C("lru_cw", c * 4 + i), 1)
        lam = C("lru_lam", 0, 2)
        v.tensor_scalar(sm[:, 0:2], lam, -1.0, None, ALU.mult)
        dve.drain()
        v.tensor_tensor(out=sm[:, 2:4], in0=sm[:, 0:2], in1=lam, op=ALU.max)
        v.tensor_scalar(sm[:, 4:6], sm[:, 0:2], 0.0, None, ALU.max)
        dve.drain().then_inc(self.v[0], 1)
        for c in (0, 1):
            u = self.t[:, c, :]
            v.tensor_tensor(out=u, in0=z[:, 6 + c, :], in1=z[:, 8 + c, :], op=ALU.mult)
            dve.drain()
            s = self.g[:, c, :]
            v.tensor_scalar(s, u, C("sc_w", c * 3 + 2), None, ALU.mult)
            dve.drain()
            self.conv(dve, s, u, 3, lambda i, c=c: C("sc_w", c * 3 + i), 1)
            v.tensor_tensor(out=self.y[:, 2 + c, :], in0=s, in1=z[:, 4 + c, :], op=ALU.mult)
            dve.drain()
        dve.wait_ge(self.a[0], self.a[1] + 1)
        v.tensor_tensor(out=sm[:, 8:10], in0=sm[:, 4:6], in1=sm[:, 6:8], op=ALU.add)
        dve.drain()
        v.tensor_scalar(sm[:, 8:10], sm[:, 8:10], -8.0, None, ALU.mult)
        dve.drain()
        dve.wait_ge(self.a[0], self.a[1] + 2)
        for c in (0, 1):
            v.tensor_scalar(self.r[:, c, :], self.r[:, c, :], sm[:, 8 + c:9 + c], None, ALU.mult)
            v.tensor_tensor(out=self.i[:, c, :], in0=self.i[:, c, :], in1=self.xc[:, c, :], op=ALU.mult)
        dve.drain().then_inc(self.v[0], 1)
        dve.wait_ge(self.a[0], self.a[1] + 3)
        v.tensor_scalar(self.b[:, :, :], self.t[:, :, :], 1.0, None, ALU.add)
        dve.drain()
        v.reciprocal(self.b[:, :, :], self.b[:, :, :])
        dve.drain()
        v.tensor_tensor(out=self.b[:, :, :], in0=self.b[:, :, :], in1=self.t[:, :, :], op=ALU.mult)
        dve.drain().then_inc(self.v[0], 1)
        dve.wait_ge(self.a[0], self.a[1] + 4)
        v.tensor_tensor(out=self.b[:, :, :], in0=self.b[:, :, :], in1=self.i[:, :, :], op=ALU.mult)
        dve.drain()
        for c in (0, 1):
            v.tensor_tensor_scan(self.t[:, c, :], self.xc[:, c, :], self.b[:, c, :], 0.0, ALU.mult, ALU.add)
        dve.drain()
        dve.wait_ge(self.a[0], self.a[1] + 5)
        for c in (0, 1):
            v.tensor_tensor(out=self.y[:, c, :], in0=self.t[:, c, :], in1=self.g[:, c, :], op=ALU.mult)

    def tensor(self, pe):
        pe.wait_ge(self.v[0], self.v[1] + 1)
        for n in range(4):
            last = self.nc.tensor.matmul(self.kern.ps[n][:, :], self.kern.const("lru_wg", n * P, P),
                                         self.xc[:, n % 2, :], start=True, stop=True)
        last.then_inc(self.p[0], 1)

    def scalar(self, act):
        s, C, sm = self.nc.scalar, self.kern.const, self.kern.small
        act.wait_ge(self.v[0], self.v[1] + 1)
        s.activation(sm[:, 6:8], sm[:, 2:4], ACT.Exp, scale=-1.0)
        act.drain()
        s.activation(sm[:, 6:8], sm[:, 6:8], ACT.Ln, bias=self.kern.one[:, 0:1])
        act.drain().then_inc(self.a[0], 1)
        act.wait_ge(self.p[0], self.p[1] + 1)
        for n in range(4):
            dst = (self.r if n < 2 else self.i)[:, n % 2, :]
            s.activation(dst, self.kern.ps[n][:, :], ACT.Sigmoid, bias=C("lru_gb", n))
        act.drain().then_inc(self.a[0], 1)
        act.wait_ge(self.v[0], self.v[1] + 2)
        s.activation(self.xc[:, :, :], self.r[:, :, :], ACT.Exp)
        s.activation(self.t[:, :, :], self.r[:, :, :], ACT.Tanh, scale=-1.0)
        act.drain().then_inc(self.a[0], 1)
        act.wait_ge(self.v[0], self.v[1] + 3)
        s.activation(self.b[:, :, :], self.b[:, :, :], ACT.Sqrt, scale=2.0)
        act.drain().then_inc(self.a[0], 1)
        s.activation(self.g[:, :, :], self.z[:, 2:4, :], ACT.Gelu_apprx_tanh)
        act.drain().then_inc(self.a[0], 1)


class FoxRows(Stage):

    def __init__(self, k, toks, rows):
        super().__init__(k)
        self.toks, self.rows = toks, rows
        self.turned = self.count("fox_turned", 1)

    def tensor(self, pe):
        for t in range(SEQ // P):
            last = self.nc.tensor.transpose(self.kern.ps[0][0:4, t * P:(t + 1) * P], self.toks[:, t, 396:400],
                                            self.kern.ident)
        last.then_inc(self.turned[0], 1)

    def scalar(self, act):
        act.wait_ge(self.turned[0], self.turned[1] + 1)
        self.nc.scalar.activation(self.rows, self.kern.ps[0][0:4, :], ACT.Copy)


class Scale(Stage):

    def __init__(self, k, items):
        super().__init__(k)
        self.items = items

    def vector(self, dve):
        for dst, src, factor in self.items:
            self.nc.vector.tensor_scalar(dst, src, factor, None, ALU.mult)


class FoxGates(Stage):

    def __init__(self, k, f, q_rows, k_rows, work):
        super().__init__(k)
        self.f, self.q_rows, self.k_rows = f, q_rows, k_rows
        self.x, self.e, self.c = (work[0:4, n * SEQ:(n + 1) * SEQ] for n in range(3))
        self.one = work[0:4, 3 * SEQ:4 * SEQ]
        self.v = self.count("fox_vector", 2)
        self.a = self.count("fox_scalar", 1)
        self.stored = self.count("fox_rows_stored", 64)

    def vector(self, dve):
        v = self.nc.vector
        v.memset(self.one, 1.0)
        v.tensor_scalar(self.f, self.f, self.kern.const("fox_fb", 0)[0:4, :], None, ALU.add)
        dve.drain()
        v.tensor_scalar(self.x, self.f, -1.0, None, ALU.mult)
        dve.drain()
        v.tensor_tensor(out=self.x, in0=self.x, in1=self.f, op=ALU.max)
        v.tensor_scalar(self.f, self.f, 0.0, None, ALU.min)
        dve.drain().then_inc(self.v[0], 1)
        dve.wait_ge(self.a[0], self.a[1] + 1)
        v.tensor_tensor(out=self.f, in0=self.f, in1=self.e, op=ALU.subtract)
        dve.drain()
        v.tensor_tensor_scan(self.c, self.one, self.f, 0.0, ALU.mult, ALU.add)
        dve.drain()
        v.tensor_scalar(self.x, self.c, -1.0, None, ALU.mult)
        dve.drain().then_inc(self.v[0], 1)

    def scalar(self, act):
        s = self.nc.scalar
        act.wait_ge(self.v[0], self.v[1] + 1)
        s.activation(self.e, self.x, ACT.Exp, scale=-1.0)
        act.drain()
        s.activation(self.e, self.e, ACT.Ln, bias=self.kern.one[0:4, 0:1])
        act.drain().then_inc(self.a[0], 1)

    def gpsimd(self, pool):
        pool.wait_ge(self.v[0], self.v[1] + 2)
        for dst, src in ((self.q_rows[0], self.c), (self.q_rows[1], self.one), (self.k_rows[0], self.one),
                         (self.k_rows[1], self.x)):
            pool.dma_start(dst, src).then_inc(self.stored[0], 16)
        pool.wait_ge(self.stored[0], self.stored[1] + 64)


class Compress(Stage):

    def __init__(self, k, xk, xv, w1, w2, pos, kc, vc, work):
        super().__init__(k)
        self.x, self.w1, self.w2, self.pos, self.kc, self.vc = (xk, xv), w1, w2, pos, kc, vc
        n = CMP_LEN * 32
        self.blocks = [work[0:HD, j * n:(j + 1) * n].rearrange("p (l n) -> p l n", n=32) for j in (0, 1)]
        self.hid = [work[:, 2 * n + j * 32:2 * n + (j + 1) * 32] for j in (0, 1)]
        self.v = self.count("compress_blocks", 2)
        self.p = self.count("compress_summed", 4)
        self.a = self.count("compress_hidden", 2)

    def vector(self, dve):
        v = self.nc.vector
        for j in (0, 1):
            for l in range(CMP_LEN):
                x = self.x[j][:, l:l + CMP_STRIDE * (N_CMP - 1) + 1:CMP_STRIDE]
                last = v.tensor_scalar(self.blocks[j][:, l, 0:N_CMP], x, self.pos[:, j * CMP_LEN + l:j * CMP_LEN + l + 1],
                                       None, ALU.add)
            last.then_inc(self.v[0], 1)
        dve.wait_ge(self.p[0], self.p[1] + 4)
        v.tensor_copy(self.kc, self.kern.ps[2][0:HD, 0:N_CMP])
        v.tensor_copy(self.vc, self.kern.ps[3][0:N_CMP, 0:HD])

    def tensor(self, pe):
        t = self.nc.tensor
        for j in (0, 1):
            pe.wait_ge(self.v[0], self.v[1] + j + 1)
            for l in range(CMP_LEN):
                last = t.matmul(self.kern.ps[j][:, 0:N_CMP], self.w1[j][:, l, :], self.blocks[j][:, l, 0:N_CMP],
                                start=(l == 0), stop=(l == CMP_LEN - 1))
            last.then_inc(self.p[0], 1)
        pe.wait_ge(self.a[0], self.a[1] + 1)
        t.matmul(self.kern.ps[2][0:HD, 0:N_CMP], self.w2[:, 0, :], self.hid[0][:, 0:N_CMP], start=True,
                 stop=True).then_inc(self.p[0], 1)
        pe.wait_ge(self.a[0], self.a[1] + 2)
        t.matmul(self.kern.ps[3][0:N_CMP, 0:HD], self.hid[1][:, 0:N_CMP], self.w2[:, 1, :], start=True,
                 stop=True).then_inc(self.p[0], 1)

    def scalar(self, act):
        for j in (0, 1):
            act.wait_ge(self.p[0], self.p[1] + j + 1)
            self.nc.scalar.activation(self.hid[j][:, 0:N_CMP], self.kern.ps[j][:, 0:N_CMP],
                                      ACT.Gelu_apprx_tanh).then_inc(self.a[0], 1)


class NsaGates(Stage):

    def __init__(self, k, gates):
        super().__init__(k)
        self.gates = gates
        self.v = self.count("nsa_biased", 1)
        self.a = self.count("nsa_gates", 1)

    def vector(self, dve):
        for t in range(SEQ // P):
            last = self.nc.vector.tensor_tensor(out=self.gates[:, t, :], in0=self.gates[:, t, :],
                                                in1=self.kern.const("nsa_gb", 0, 12), op=ALU.add)
        last.then_inc(self.v[0], 1)
        dve.wait_ge(self.a[0], self.a[1] + 1)
        self.nc.vector.tensor_scalar(self.gates[:, 0, 0:4], self.gates[:, 0, 0:4], self.kern.const("cmp_valid", 0),
                                     None, ALU.mult)

    def scalar(self, act):
        act.wait_ge(self.v[0], self.v[1] + 1)
        self.nc.scalar.activation(self.gates, self.gates, ACT.Sigmoid).then_inc(self.a[0], 1)


class RelBias(Stage):

    def __init__(self, k, onehot, onehot_fwd, rel, r, line, toe, cmp_bias):
        super().__init__(k)
        self.onehot, self.fwd, self.rel, self.r, self.line, self.toe, self.cmp_bias = (
            onehot, onehot_fwd, rel, r, line, toe, cmp_bias)
        self.p = self.count("bias_summed", 2)
        self.a = self.count("bias_rows", 1)
        self.moved = self.count("bias_moved", 128)

    def tensor(self, pe):
        t = self.nc.tensor
        for c in (0, 1):
            last = t.matmul(self.kern.ps[c][0:4, :], self.rel, self.onehot[:, c * 512:(c + 1) * 512], start=True, stop=True)
        last.then_inc(self.p[0], 1)
        for tile in range(SEQ // P):
            for n in range(N_CMP):
                at = P * tile - CMP_STRIDE * n - (CMP_LEN - 1) + (SEQ - 1)
                last = t.matmul(self.kern.ps[2 + tile][:, n * 4:n * 4 + 4], self.fwd[:, at:at + P], self.rel,
                                start=True, stop=True)
        last.then_inc(self.p[0], 1)

    def scalar(self, act):
        act.wait_ge(self.p[0], self.p[1] + 1)
        for c in (0, 1):
            self.nc.scalar.activation(self.r[:, c * 512:(c + 1) * 512], self.kern.ps[c][0:4, :], ACT.Copy)
        act.drain().then_inc(self.a[0], 1)

    def vector(self, dve):
        dve.wait_ge(self.p[0], self.p[1] + 2)
        for tile in range(SEQ // P):
            for h in range(4):
                self.nc.vector.tensor_copy(self.cmp_bias[:, tile, h, 0:N_CMP],
                                           self.kern.ps[2 + tile][:, h:4 * N_CMP:4])

    def gpsimd(self, pool):
        pool.wait_ge(self.a[0], self.a[1] + 1)
        for h in range(4):
            src = self.r[h:h + 1, :].rearrange("h (a x) -> h a x", a=1).broadcast_to([1, P, 1024])
            pool.dma_start(self.line[h:h + 1, :, :], src).then_inc(self.moved[0], 16)
        pool.wait_ge(self.moved[0], self.moved[1] + 64)
        for h in range(4):
            src = bass.AP(tensor=self.line.tensor, offset=h * P * 1024 + P - 1, ap=[[1023, P], [1, 896]])
            pool.dma_start(self.toe[:, h, :], src).then_inc(self.moved[0], 16)
        pool.wait_ge(self.moved[0], self.moved[1] + 128)


class Ada(Stage):

    def __init__(self, k, c_t, mod, bias, rows):
        super().__init__(k)
        self.c_t, self.mod, self.bias, self.rows = c_t, mod, bias, rows
        self.tiles = 6 * D // P
        self.items = self.tiles // 2
        self.first = k.ring.take(self.items)
        k.tally.claim("weights_used", self.items)
        self.summed = self.count("ada_summed", self.items)
        self.moved = self.count("ada_moved", self.items)
        self.turned = self.count("ada_turned", 1)

    def tensor(self, pe):
        kern = self.kern
        with pe.Fori(0, self.items // SLOTS) as i:
            for j in range(SLOTS):
                w = kern.slot_ready(pe, self.first + j, turn=i).rearrange("p (k c) -> p k c", k=KT)
                pe.wait_ge(self.moved[0], i * SLOTS + (self.moved[1] + j + 1 - SLOTS))
                for kt in range(KT):
                    last = self.nc.tensor.matmul(kern.ps[j][0:2, 0:256], self.c_t[:, kt, :], w[:, kt, :], start=(kt == 0),
                                                 stop=(kt == KT - 1))
                last.then_inc(self.summed[0], 1)
                pe.drain().then_inc(self.tally.sem("weights_used"), 1)
        pe.wait_ge(self.moved[0], self.moved[1] + self.items)
        for m in range(self.tiles):
            last = self.nc.tensor.transpose(kern.ps[7][:, 2 * m:2 * m + 2], self.rows[0:2, m * P:(m + 1) * P],
                                            kern.ident[0:2, 0:2])
        last.then_inc(self.turned[0], 1)

    def vector(self, dve):
        with dve.Fori(0, self.items // SLOTS) as i:
            for j in range(SLOTS):
                dve.wait_ge(self.summed[0], i * SLOTS + (self.summed[1] + j + 1))
                self.nc.vector.tensor_copy(self.rows[0:2, bass.ds(i * (256 * SLOTS) + j * 256, 256)],
                                           self.kern.ps[j][0:2, 0:256]).then_inc(self.moved[0], 1)
        dve.wait_ge(self.turned[0], self.turned[1] + 1)
        for s in (0, 1):
            self.nc.vector.tensor_tensor(out=self.mod[:, :, s], in0=self.kern.ps[7][:, s:2 * self.tiles:2],
                                         in1=self.bias, op=ALU.add)


class Silu(Stage):

    def __init__(self, k, x, tmp):
        super().__init__(k)
        self.x, self.tmp = x, tmp
        self.a = self.count("silu_sigmoid", 1)

    def scalar(self, act):
        self.nc.scalar.activation(self.tmp, self.x, ACT.Sigmoid).then_inc(self.a[0], 1)

    def vector(self, dve):
        dve.wait_ge(self.a[0], self.a[1] + 1)
        self.nc.vector.tensor_tensor(out=self.x, in0=self.x, in1=self.tmp, op=ALU.mult)


class ModGains(Stage):

    def __init__(self, k, items):
        super().__init__(k)
        self.items = items

    def vector(self, dve):
        for dst, scale, g in self.items:
            for s in (0, 1):
                self.nc.vector.scalar_tensor_tensor(out=dst[:, :, s], in0=scale[:, :, s], scalar=1.0, in1=g,
                                                    op0=ALU.add, op1=ALU.mult)


class LocalProject(Stage):

    def __init__(self, k, groups):
        super().__init__(k)
        self.groups = groups
        self.summed = self.count("local_summed", len(groups))
        self.moved = [self.count(f"local_moved_{e}", (len(groups) + 1 - e) // 2) for e in (0, 1)]

    def bank(self, n):
        dst = self.groups[n][1]
        return self.kern.ps[n % 8][0:dst.shape[0], 0:dst.shape[-1]]

    def tensor(self, pe):
        for n, (pairs, _) in enumerate(self.groups):
            if n >= 8:
                s, base = self.moved[n % 2]
                pe.wait_ge(s, base + (n - 8) // 2 + 1)
            for i, (w, x) in enumerate(pairs):
                last = self.nc.tensor.matmul(self.bank(n), w, x, start=(i == 0), stop=(i == len(pairs) - 1))
            last.then_inc(self.summed[0], 1)

    def move(self, eng, which):
        for n in range(which, len(self.groups), 2):
            eng.wait_ge(self.summed[0], self.summed[1] + n + 1)
            dst = self.groups[n][1]
            if which:
                ins = self.nc.vector.tensor_copy(dst, self.bank(n))
            else:
                ins = self.nc.scalar.activation(dst, self.bank(n), ACT.Copy)
            ins.then_inc(self.moved[which][0], 1)

    def scalar(self, act):
        self.move(act, 0)

    def vector(self, dve):
        self.move(dve, 1)


class ShiftMix(Stage):

    def __init__(self, k, p, tiles, mu, tmp, tanh, sigm):
        super().__init__(k)
        self.p, self.tiles, self.mu, self.tmp, self.tanh, self.sigm = p, tiles, mu, tmp, tanh, sigm
        self.v = self.count("shift_mixed", 1)

    def vector(self, dve):
        v = self.nc.vector
        for j in range(self.tiles):
            x, t = self.p[:, j, :], self.tmp[:, j % 2, :]
            for a, b in segments(ALLTOK):
                v.tensor_tensor(out=t[:, a + 1:b - 1], in0=x[:, a:b - 2], in1=x[:, a + 2:b], op=ALU.add)
                v.tensor_copy(t[:, a:a + 1], x[:, a + 1:a + 2])
                v.tensor_copy(t[:, b - 1:b], x[:, b - 2:b - 1])
            dve.drain()
            v.scalar_tensor_tensor(out=t, in0=t, scalar=0.5, in1=x, op0=ALU.mult, op1=ALU.subtract)
            dve.drain()
            v.scalar_tensor_tensor(out=x, in0=t, scalar=self.mu[:, j:j + 1], in1=x, op0=ALU.mult, op1=ALU.add)
        dve.drain().then_inc(self.v[0], 1)

    def scalar(self, act):
        act.wait_ge(self.v[0], self.v[1] + 1)
        self.nc.scalar.activation(self.tanh, self.tanh, ACT.Tanh)
        self.nc.scalar.activation(self.sigm, self.sigm, ACT.Sigmoid)


class Wkv(Stage):

    LEVELS = 6

    def __init__(self, k, w, y, ksum):
        super().__init__(k)
        self.w, self.y, self.ksum = w, y, ksum
        n = 4 * N_CH
        self.steps = {}
        for name, per in (("operands", 1), ("logits", 1), ("sigmoids", 1), ("key_squares", 1), ("key_sums", 1),
                          ("key_roots", 1), ("logs", 1), ("exps", 1), ("more_exps", 1), ("factors", 1), ("more_factors", 1), ("tokens", 1), ("token_rows", 1),
                          ("grams", 1), ("more_grams", 1), ("last_grams", 1), ("low_masked", 2), ("masked", 2), ("more_masked", 1),
                          ("level_blocks", 2 * self.LEVELS), ("level_half", 2 * self.LEVELS),
                          ("level_half_copied", 2 * self.LEVELS), ("level_summed", 2 * self.LEVELS),
                          ("level_added", 2 * self.LEVELS), ("w_summed", 1), ("w_copied", 1), ("u_summed", 2),
                          ("u_copied", 2), ("outputs", 1)):
            self.steps[name] = (*self.count("wkv_" + name, per * n), per)
        self.staged = self.count("wkv_tile_staged", 4)

    def at(self, name, u, i=0):
        s, base, per = self.steps[name]
        return s, u * per + (base + i + 1)

    def turns(self, eng, tile, chunk):
        with eng.Fori(0, 4) as c:
            tile(c)
            for ch in range(N_CH):
                chunk(c, c * N_CH + ch, ch)

    @staticmethod
    def first_tokens(ch):
        lo, hi = (0, CTX // CH) if ch < CTX // CH else (CTX // CH, N_CH)
        return ch * CH, (lo + hi - 1 - ch) * CH

    def gram(self, n, e):
        bank, half = 3 * e + (1 if n in (2, 3) else 0), n % 2
        return self.kern.ps[bank][:, half * 2 * CH:(half + 1) * 2 * CH]

    def half_bank(self, g):
        return self.kern.ps[(5, 2)[g]]

    def level_bank(self, g):
        x = self.kern.ps[6 + g].rearrange("p (a t) -> p a t", a=4)
        return x[:, 0:2, :], x[:, 2:4, :]

    def nat(self, x, c, off, d):
        return x[:, bass.ds(c * ALLTOK + off[d], CH)]

    @staticmethod
    def ordered(x, d):
        return x[:, ::-1] if d else x

    def tensor(self, pe):
        t, w, ps = self.nc.tensor, self.w, self.kern.ps
        ident = self.kern.ident

        def key_sums(u):
            pe.wait_ge(*self.at("key_squares", u))
            t.matmul(ps[2][:, 0:2 * CH], w.head_ones, w.sq, start=True, stop=True).then_inc(self.steps["key_sums"][0], 1)

        def chunk(c, u, ch):
            pe.wait_ge(self.staged[0], c + (self.staged[1] + 1))
            pe.wait_ge(*self.at("operands", u))
            if ch == 0:
                key_sums(u)
            for i in range(4):
                d, x = i % 2, (w.w1c if i < 2 else w.a1c)
                ws = w.w2s if i < 2 else w.a2s
                last = t.matmul(ps[d][:, i // 2 * CH:(i // 2 + 1) * CH], ws[64 * d:64 * d + 64, :], x[64 * d:64 * d + 64, :],
                                start=True, stop=True)
            last.then_inc(self.steps["logits"][0], 1)
            pe.wait_ge(*self.at("factors", u))

            def grams(n, qs):
                lhs, rhs = ((w.bt, w.at), (w.at, w.bt), (w.kt, w.at), (w.bt, w.rt), (w.kt, w.rt))[n]
                for q in qs:
                    d, e = q % 2, slice(64 * (q // 2), 64 * (q // 2) + 64)
                    last = t.matmul(self.gram(n, q // 2)[:, d * CH:(d + 1) * CH], lhs[e, d, :], rhs[e, d, :],
                                    start=True, stop=True)
                return last

            grams(0, (0, 2, 1, 3))
            grams(1, (0, 2, 1, 3)).then_inc(self.steps["grams"][0], 1)
            pe.wait_ge(*self.at("more_factors", u))
            for d in (0, 1):
                t.transpose(ps[5][:, d * CH:(d + 1) * CH], w.bt[:, d, :], ident)
                t.transpose(ps[5][:, (2 + d) * CH:(3 + d) * CH], w.kt[:, d, :], ident)
                last = t.transpose(ps[6][:, d * CH:(d + 1) * CH], w.vc[:, d, :], ident)
            last.then_inc(self.steps["tokens"][0], 1)
            grams(2, (0, 2, 1, 3))
            grams(3, (0, 2, 1, 3)).then_inc(self.steps["more_grams"][0], 1)

            def half(lv, g):
                if lv:
                    pe.wait_ge(*self.at("level_added", u, 2 * lv - 2 + g))
                else:
                    pe.wait_ge(*self.at("masked", u, g))
                pe.wait_ge(*self.at("level_blocks", u, 2 * lv + g))
                for q in (2 * g, 2 * g + 1):
                    last = t.matmul(self.half_bank(g)[:, q % 2 * CH:(q % 2 + 1) * CH], w.lo[:, lv % 2, q, :], w.x[:, q, :], start=True, stop=True)
                last.then_inc(self.steps["level_half"][0], 1)

            def whole(lv, g):
                pe.wait_ge(*self.at("level_half_copied", u, 2 * lv + g))
                x, xt = self.level_bank(g)
                for q in (2 * g, 2 * g + 1):
                    last = t.matmul(xt[:, q % 2, :], w.t1[:, q, :], w.xt[:, q, :], start=True, stop=True)
                    if lv < self.LEVELS - 1:
                        last = t.matmul(x[:, q % 2, :], w.xt[:, q, :], w.t1[:, q, :], start=True, stop=True)
                last.then_inc(self.steps["level_summed"][0], 1)

            def right_side():
                pe.wait_ge(*self.at("more_masked", u))
                for q in range(4):
                    d, e = q % 2, slice(64 * (q // 2), 64 * (q // 2) + 64)
                    o = ps[q // 2][:, d * HD:(d + 1) * HD]
                    t.matmul(o, w.at[e, d, :], w.s[e, d, :], start=True, stop=False)
                    last = t.matmul(o, w.lkt[:, q, :], w.vr[:, d, e], start=False, stop=True)
                last.then_inc(self.steps["w_summed"][0], 1)

            pe.wait_ge(*self.at("token_rows", u))
            for lv in range(self.LEVELS):
                half(lv, 0)
                half(lv, 1)
                whole(lv, 0)
                whole(lv, 1)
                if lv == 0:
                    grams(4, (0, 2, 1, 3)).then_inc(self.steps["last_grams"][0], 1)
                if lv == self.LEVELS - 2:
                    right_side()
            pe.wait_ge(*self.at("w_copied", u))
            for g in (0, 1):
                pe.wait_ge(*self.at("level_added", u, 2 * self.LEVELS - 2 + g))
                for q in (2 * g, 2 * g + 1):
                    last = t.matmul(self.half_bank(g)[:, q % 2 * HD:(q % 2 + 1) * HD], w.xt[:, q, :], w.wv[:, q, :], start=True, stop=True)
                last.then_inc(self.steps["u_summed"][0], 1)
            for g in (0, 1):
                pe.wait_ge(*self.at("u_copied", u, g))
                for q in (2 * g, 2 * g + 1):
                    d, e = q % 2, slice(64 * g, 64 * g + 64)
                    o = ps[3][e, d * CH:(d + 1) * CH]
                    t.matmul(o, w.uv[:, q, :], w.rbt[:, q, :], start=True, stop=False)
                    t.matmul(o, w.s[e, d, :], w.rt[e, d, :], start=False, stop=False)
                    t.matmul(o, w.vr[:, d, e], w.rkt[:, q, :], start=False, stop=True)
                    o = ps[4][e, d * HD:(d + 1) * HD]
                    t.matmul(o, w.br[:, d, e], w.uv[:, q, :], start=True, stop=False)
                    last = t.matmul(o, w.kr[:, d, e], w.vr[:, d, e], start=False, stop=True)
            last.then_inc(self.steps["outputs"][0], 1)
            if ch + 1 < N_CH:
                key_sums(u + 1)

        self.turns(pe, lambda c: None, chunk)

    def scalar(self, act):
        s, w, ps = self.nc.scalar, self.w, self.kern.ps

        def tile(c):
            act.wait_ge(self.staged[0], c + (self.staged[1] + 1))

        def chunk(c, u, ch):
            act.wait_ge(*self.at("key_sums", u))
            s.activation(w.root, ps[2][:, 0:2 * CH], ACT.Sqrt, bias=w.tiny).then_inc(self.steps["key_roots"][0], 1)
            act.wait_ge(*self.at("logits", u))
            for d in (0, 1):
                s.activation(w.lw[:, d, :], ps[d][:, 0:CH], ACT.Sigmoid, bias=w.cst[:, d:d + 1])
                s.activation(w.a[:, d, :], ps[d][:, CH:2 * CH], ACT.Sigmoid, bias=w.cst[:, 2 + d:3 + d])
            act.drain().then_inc(self.steps["sigmoids"][0], 1)
            act.wait_ge(*self.at("logs", u))
            rate = float(np.exp(-0.5))
            s.activation(w.en, w.e1, ACT.Exp, scale=rate)
            s.activation(w.ea, w.ea, ACT.Exp, scale=-rate)
            act.drain().then_inc(self.steps["exps"][0], 1)
            s.activation(w.half, w.half, ACT.Exp, scale=-rate)
            s.activation(w.e1, w.e1, ACT.Exp, scale=-rate)
            act.drain().then_inc(self.steps["more_exps"][0], 1)
            act.wait_ge(*self.at("tokens", u))
            s.activation(w.br, ps[5][:, 0:2 * CH].rearrange("p (d t) -> p d t", d=2), ACT.Copy)
            s.activation(w.kr, ps[5][:, 2 * CH:4 * CH].rearrange("p (d t) -> p d t", d=2), ACT.Copy)
            s.activation(w.vr, ps[6][:, 0:2 * CH].rearrange("p (d t) -> p d t", d=2), ACT.Copy)
            act.drain().then_inc(self.steps["token_rows"][0], 1)
            for lv in range(self.LEVELS):
                for g in (0, 1):
                    act.wait_ge(*self.at("level_half", u, 2 * lv + g))
                    half = slice(2 * g * CH, (2 * g + 2) * CH)
                    s.activation(w.t1_flat[:, half], self.half_bank(g)[:, 0:2 * CH], ACT.Copy).then_inc(self.steps["level_half_copied"][0], 1)
            act.wait_ge(*self.at("w_summed", u))
            for e in (0, 1):
                s.activation(w.wv_flat[:, e * P:(e + 1) * P], ps[e][:, 0:P], ACT.Copy)
            act.drain().then_inc(self.steps["w_copied"][0], 1)
            for g in (0, 1):
                act.wait_ge(*self.at("u_summed", u, g))
                half = slice(2 * g * HD, (2 * g + 2) * HD)
                s.activation(w.uv_flat[:, half], self.half_bank(g)[:, 0:2 * HD], ACT.Copy).then_inc(self.steps["u_copied"][0], 1)

        self.turns(act, tile, chunk)

    def vector(self, dve):
        v, w, ps = self.nc.vector, self.w, self.kern.ps

        def mask2(m):
            return m.rearrange("p (a t) -> p a t", a=1).broadcast_to([P, 2, CH])

        def tile(c):
            dve.drain()
            v.tensor_copy(w.w2s, w.w2[:, bass.ds(c * P, P)])
            v.tensor_copy(w.a2s, w.a2[:, bass.ds(c * P, P)])
            v.tensor_copy(w.cst, w.csts[:, bass.ds(c * 8, 8)])
            v.memset(w.s_flat, 0.0)
            dve.drain().then_inc(self.staged[0], 1)

        def operands(c, ch):
            off = self.first_tokens(ch)
            for d in (0, 1):
                e = slice(64 * d, 64 * d + 64)
                for dst, src in ((w.w1c, w.w1), (w.a1c, w.a1)):
                    v.tensor_copy(self.ordered(dst[e, :], d), src[e, bass.ds(off[d], CH)])
                v.tensor_copy(self.ordered(w.kc[:, d, :], d), self.nat(w.k, c, off, d))
                v.tensor_copy(self.ordered(w.vc[:, d, :], d), self.nat(w.v, c, off, d))
            dve.drain().then_inc(self.steps["operands"][0], 1)
            v.tensor_scalar(w.kk, w.kc_flat, w.cst[:, 4:5], None, ALU.mult)
            dve.drain()
            v.tensor_tensor(out=w.sq, in0=w.kk, in1=w.kk, op=ALU.mult)
            dve.drain().then_inc(self.steps["key_squares"][0], 1)

        def chunk(c, u, ch):
            off = self.first_tokens(ch)
            if ch == 0:
                operands(c, ch)
            dve.wait_ge(*self.at("key_roots", u))
            v.reciprocal(w.root, w.root)
            dve.drain()
            v.tensor_tensor(out=w.kk, in0=w.kk, in1=w.root, op=ALU.mult)
            dve.drain()
            dve.wait_ge(*self.at("sigmoids", u))
            for d in (0, 1):
                v.tensor_tensor_scan(w.e1d[:, d, :], w.ones_row, w.lw[:, d, :], 0.0, ALU.mult, ALU.add)
            dve.drain()
            v.tensor_scalar(w.half, w.e1d[:, :, CH - 1], 0.5, None, ALU.mult)
            dve.drain()
            for d in (0, 1):
                v.tensor_scalar(w.e1d[:, d, :], w.e1d[:, d, :], w.half[:, d:d + 1], None, ALU.subtract)
            dve.drain()
            v.tensor_tensor(out=w.ea, in0=w.e1, in1=w.lw_flat, op=ALU.subtract)
            dve.drain().then_inc(self.steps["logs"][0], 1)
            v.tensor_tensor(out=w.bt_flat, in0=w.kk, in1=w.a_flat, op=ALU.mult)
            v.tensor_scalar(w.kd_flat, w.a_flat, w.cst[:, 5:6], w.cst[:, 7:8], ALU.mult, ALU.add)
            dve.drain()
            dve.wait_ge(*self.at("exps", u))
            v.scalar_tensor_tensor(out=w.at_flat, in0=w.kk, scalar=-1.0, in1=w.ea, op0=ALU.mult, op1=ALU.mult)
            v.tensor_tensor(out=w.bt_flat, in0=w.bt_flat, in1=w.en, op=ALU.mult)
            dve.drain().then_inc(self.steps["factors"][0], 1)
            v.tensor_tensor(out=w.kd_flat, in0=w.kd_flat, in1=w.kc_flat, op=ALU.mult)
            dve.drain()
            v.tensor_tensor(out=w.kt_flat, in0=w.kd_flat, in1=w.en, op=ALU.mult)
            dve.wait_ge(*self.at("more_exps", u))
            for d in (0, 1):
                v.tensor_tensor(out=self.ordered(w.rt[:, d, :], d), in0=self.nat(w.r, c, off, d),
                                in1=self.ordered(w.e1d[:, d, :], d), op=ALU.mult)
                v.tensor_scalar(w.s[:, d, :], w.s[:, d, :], w.half[:, d:d + 1], None, ALU.mult)
            dve.drain().then_inc(self.steps["more_factors"][0], 1)
            for d in (0, 1):
                ks = self.nat(self.ksum, c, off, d)
                v.tensor_tensor(out=ks, in0=ks, in1=self.ordered(w.kd[:, d, :], d), op=ALU.add)
                dve.drain()

            def mask(n, dst, m, e):
                v.tensor_tensor(out=dst[:, 2 * e:2 * e + 2, :], op=ALU.mult,
                                in0=self.gram(n, e).rearrange("p (a t) -> p a t", a=2), in1=mask2(m))

            dve.wait_ge(*self.at("grams", u))
            for g in (0, 1):
                pair = slice(2 * g, 2 * g + 2)
                mask(0, w.lt, w.strict, g)
                dve.drain().then_inc(self.steps["low_masked"][0], 1)
                mask(1, w.x, w.first_low, g)
                v.tensor_tensor(out=w.xt[:, pair, :], in0=w.lt[:, pair, :], in1=mask2(w.first_up), op=ALU.mult)
                dve.drain()
                v.tensor_tensor(out=w.x[:, pair, :], in0=w.x[:, pair, :], in1=mask2(self.kern.ident), op=ALU.add)
                v.tensor_tensor(out=w.xt[:, pair, :], in0=w.xt[:, pair, :], in1=mask2(self.kern.ident), op=ALU.add)
                dve.drain().then_inc(self.steps["masked"][0], 1)
            more = ((2, w.lkt, w.strict), (3, w.rbt, w.incl), (4, w.rkt, w.incl))
            for lv in range(self.LEVELS):
                for g in (0, 1):
                    pair = slice(2 * g, 2 * g + 2)
                    dve.wait_ge(*self.at("level_summed", u, 2 * lv + g))
                    x, xt = self.level_bank(g)
                    if lv < self.LEVELS - 1:
                        v.tensor_tensor(out=w.x[:, pair, :], in0=w.x[:, pair, :], in1=x, op=ALU.add)
                    v.tensor_tensor(out=w.xt[:, pair, :], in0=w.xt[:, pair, :], in1=xt, op=ALU.add)
                    dve.drain().then_inc(self.steps["level_added"][0], 1)
                    if lv < len(more):
                        dve.wait_ge(*self.at("last_grams" if lv == 2 else "more_grams", u))
                        mask(*more[lv], g)
                if lv == len(more) - 1:
                    dve.drain().then_inc(self.steps["more_masked"][0], 1)
            if ch + 1 < N_CH:
                operands(c, ch + 1)
            dve.wait_ge(*self.at("outputs", u))
            v.tensor_tensor(out=w.s_flat, in0=w.s_flat, in1=ps[4][:, 0:2 * HD], op=ALU.add)
            for d in (0, 1):
                yv = self.nat(self.y, c, off, d)
                v.tensor_tensor(out=yv, in0=yv, in1=self.ordered(ps[3][:, d * CH:(d + 1) * CH], d), op=ALU.add)
                dve.drain()
            for d in (0, 1):
                v.tensor_scalar(w.s[:, d, :], w.s[:, d, :], w.half[:, d:d + 1], None, ALU.mult)
            dve.drain()

        v.memset(w.ones_row, 1.0)
        v.memset(self.y, 0.0)
        v.memset(self.ksum, 0.0)
        for c in range(4):
            v.tensor_scalar(w.csts[:, c * 8 + 7:c * 8 + 8], w.csts[:, c * 8 + 5:c * 8 + 6], -1.0, 1.0, ALU.mult, ALU.add)
        self.turns(dve, tile, chunk)

    def gpsimd(self, pool):
        w = self.w

        def chunk(c, u, ch):
            for lv in range(self.LEVELS):
                m = w.joins[:, lv * CH:(lv + 1) * CH].rearrange("p (a t) -> p a t", a=1).broadcast_to([P, 2, CH])
                for g in (0, 1):
                    if lv == 0:
                        pool.wait_ge(*self.at("low_masked", u, g))
                    elif lv >= 2:
                        pool.wait_ge(*self.at("level_half", u, 2 * lv - 4 + g))
                    pair = slice(2 * g, 2 * g + 2)
                    self.nc.gpsimd.tensor_tensor(out=w.lo[:, lv % 2, pair], in0=w.lt[:, pair], in1=m,
                                                 op=ALU.mult).then_inc(self.steps["level_blocks"][0], 1)

        self.turns(pool, lambda c: None, chunk)


class RwkvOut(Stage):

    def __init__(self, k, y, ksum, r, v, g, mean_ones, sum_ones, vecs, eps, tmp):
        super().__init__(k)
        self.y, self.ks, self.r, self.v_, self.g = y, ksum, r, v, g
        self.mean_ones, self.sum_ones, self.vecs, self.eps, self.tmp = mean_ones, sum_ones, vecs, eps, tmp
        self.units = [(c, s) for c in range(4) for s in segments(ALLTOK)]
        n = len(self.units)
        self.keys = self.count("rwout_keys", n)
        self.sums = self.count("rwout_sums", n)
        self.squares = self.count("rwout_squares", n)
        self.variances = self.count("rwout_variances", n)
        self.roots = self.count("rwout_roots", n)

    def parts(self, n):
        c, (a, b) = self.units[n]
        return c, b - a, [x[:, c, a:b] for x in (self.y, self.ks, self.r, self.v_, self.g)] + [self.tmp[:, n % 2, 0:b - a]]

    def bank(self, n, i):
        return self.kern.ps[n % 2 * 3 + i][:, 0:self.parts(n)[1]]

    def tensor(self, pe):
        t = self.nc.tensor

        def variance(n):
            pe.wait_ge(self.squares[0], self.squares[1] + n + 1)
            t.matmul(self.bank(n, 2), self.mean_ones, self.parts(n)[2][5], start=True,
                     stop=True).then_inc(self.variances[0], 1)

        for n in range(len(self.units)):
            _, _, (y, ks, r, v, g, tmp) = self.parts(n)
            pe.wait_ge(self.keys[0], self.keys[1] + n + 1)
            t.matmul(self.bank(n, 0), self.mean_ones, y, start=True, stop=True)
            t.matmul(self.bank(n, 1), self.sum_ones, ks, start=True, stop=True).then_inc(self.sums[0], 1)
            if n:
                variance(n - 1)
        variance(len(self.units) - 1)

    def scalar(self, act):
        for n in range(len(self.units)):
            act.wait_ge(self.variances[0], self.variances[1] + n + 1)
            self.nc.scalar.activation(self.parts(n)[2][5], self.bank(n, 2), ACT.Sqrt,
                                      bias=self.eps).then_inc(self.roots[0], 1)

    def vector(self, dve):
        e = self.nc.vector

        def keys(n):
            c, _, (y, ks, r, v, g, tmp) = self.parts(n)
            e.scalar_tensor_tensor(out=ks, in0=ks, scalar=self.vecs[:, 8 + c:9 + c], in1=r, op0=ALU.mult, op1=ALU.mult)
            dve.drain().then_inc(self.keys[0], 1)

        def centre(n):
            c, _, (y, ks, r, v, g, tmp) = self.parts(n)
            dve.wait_ge(self.sums[0], self.sums[1] + n + 1)
            e.tensor_tensor(out=y, in0=y, in1=self.bank(n, 0), op=ALU.subtract)
            e.tensor_tensor(out=ks, in0=v, in1=self.bank(n, 1), op=ALU.mult)
            dve.drain()
            e.tensor_tensor(out=tmp, in0=y, in1=y, op=ALU.mult)
            dve.drain().then_inc(self.squares[0], 1)

        def finish(n):
            c, _, (y, ks, r, v, g, tmp) = self.parts(n)
            dve.wait_ge(self.roots[0], self.roots[1] + n + 1)
            e.reciprocal(tmp, tmp)
            dve.drain()
            e.scalar_tensor_tensor(out=y, in0=y, scalar=self.vecs[:, c:c + 1], in1=tmp, op0=ALU.mult, op1=ALU.mult)
            dve.drain()
            e.scalar_tensor_tensor(out=y, in0=y, scalar=self.vecs[:, 4 + c:5 + c], in1=ks, op0=ALU.add, op1=ALU.add)
            dve.drain()
            e.tensor_tensor(out=y, in0=y, in1=g, op=ALU.mult)

        keys(0)
        for n in range(len(self.units)):
            centre(n)
            if n + 1 < len(self.units):
                keys(n + 1)
            if n:
                finish(n - 1)
        finish(len(self.units) - 1)


class Copy(Stage):
    def __init__(self, k, pairs):
        super().__init__(k)
        self.pairs = pairs

    def scalar(self, act):
        for dst, src in self.pairs:
            self.nc.scalar.activation(dst, src, ACT.Copy)


class Router(Stage):

    def __init__(self, k, h, tiles, rw, rb, work, rows):
        super().__init__(k)
        self.h, self.tiles, self.rw, self.rb, self.rows = h, tiles, rw, rb, rows
        n = self.n = len(tiles)
        e, g = n * N_EXP, n * 4
        at = [0]

        def take(cols):
            at[0] += cols
            return work[:, at[0] - cols:at[0]]

        self.scores, self.biased, self.lost, self.cmp = take(e), take(e), take(e), take(g)
        self.sums, self.best, self.glost, self.den = take(g), take(g), take(g), take(n)
        self.comb = take(n * 17).rearrange("p (t e) -> p t e", e=17)
        self.summed = self.count("router_summed", 1)
        self.sig = self.count("router_scores", 1)
        self.done = self.count("router_combined", 1)
        self.turned = self.count("router_turned", 1)

    def tensor(self, pe):
        t, ps = self.nc.tensor, self.kern.ps
        for i, tile in enumerate(self.tiles):
            for kt in range(KT):
                last = t.matmul(ps[0][:, i * N_EXP:(i + 1) * N_EXP], self.h[:, kt, tile * P:(tile + 1) * P],
                                self.rw[:, kt * N_EXP:(kt + 1) * N_EXP], start=(kt == 0), stop=(kt == KT - 1))
        last.then_inc(self.summed[0], 1)
        pe.wait_ge(self.done[0], self.done[1] + 1)
        for i in range(self.n):
            last = t.transpose(self.kern.ps[1 + i // 4][0:17, (i % 4) * P:(i % 4 + 1) * P], self.comb[:, i, :], self.kern.ident)
        last.then_inc(self.turned[0], 1)

    def scalar(self, act):
        act.wait_ge(self.summed[0], self.summed[1] + 1)
        self.nc.scalar.activation(self.scores, self.kern.ps[0][:, 0:self.n * N_EXP], ACT.Sigmoid).then_inc(self.sig[0], 1)
        act.wait_ge(self.turned[0], self.turned[1] + 1)
        for i, tile in enumerate(self.tiles):
            self.nc.scalar.activation(self.rows[0:17, tile * P:(tile + 1) * P],
                                      self.kern.ps[1 + i // 4][0:17, (i % 4) * P:(i % 4 + 1) * P], ACT.Copy)

    def vector(self, dve):
        v, n = self.nc.vector, self.n

        def tt(out, a, b, op):
            v.tensor_tensor(out=out, in0=a, in1=b, op=op)
            dve.drain()

        def member(x, i):
            return x[:, i:n * N_EXP:4]

        def group(x, i):
            return x[:, i:n * 4:4]

        dve.wait_ge(self.sig[0], self.sig[1] + 1)
        for i in range(n):
            v.tensor_tensor(out=self.biased[:, i * N_EXP:(i + 1) * N_EXP], in0=self.scores[:, i * N_EXP:(i + 1) * N_EXP],
                            in1=self.rb, op=ALU.add)
        v.memset(self.lost, 0.0)
        v.memset(self.glost, 0.0)
        v.memset(self.sums, NEG)
        v.memset(self.comb, 1.0)
        dve.drain()
        for i in range(4):
            for j in range(i + 1, 4):
                a, b = member(self.biased, i), member(self.biased, j)
                tt(self.cmp, a, b, ALU.add)
                tt(self.sums, self.sums, self.cmp, ALU.max)
                tt(self.cmp, a, b, ALU.is_ge)
                tt(member(self.lost, j), member(self.lost, j), self.cmp, ALU.add)
                tt(self.cmp, a, b, ALU.is_lt)
                tt(member(self.lost, i), member(self.lost, i), self.cmp, ALU.add)
        for i in range(4):
            for j in range(i + 1, 4):
                a, b, c = group(self.sums, i), group(self.sums, j), self.cmp[:, 0:n]
                tt(c, a, b, ALU.is_ge)
                tt(group(self.glost, j), group(self.glost, j), c, ALU.add)
                tt(c, a, b, ALU.is_lt)
                tt(group(self.glost, i), group(self.glost, i), c, ALU.add)
        v.tensor_scalar(self.lost, self.lost, 2.0, None, ALU.is_lt)
        v.tensor_scalar(self.best, self.glost, 1.0, None, ALU.is_lt)
        dve.drain()
        for i in range(4):
            tt(member(self.lost, i), member(self.lost, i), self.best, ALU.mult)
        tt(self.scores, self.scores, self.lost, ALU.mult)
        v.reduce_sum(self.den, self.scores.rearrange("p (t e) -> p t e", e=N_EXP), AX_X)
        dve.drain()
        v.reciprocal(self.den, self.den)
        dve.drain()
        for i in range(n):
            v.tensor_scalar(self.comb[:, i, 0:N_EXP], self.scores[:, i * N_EXP:(i + 1) * N_EXP], self.den[:, i:i + 1],
                            None, ALU.mult)
        dve.drain().then_inc(self.done[0], 1)


ARENA = 24000


class Kernel:

    def __init__(self, nc, ctx, A):
        self.nc, self.A = nc, A
        self.tally = Tally(nc, ctx)
        self.stages = []
        self.ring = Ring()

        def sb(name, shape):
            return ctx.enter_context(nc.sbuf_tensor(name, shape, F32))

        self.psum = ctx.enter_context(nc.psum_tensor("psum", [P, 8, 512], F32))
        self.ps = [self.psum[:, i, :] for i in range(8)]
        def sb_twice(name, shape):
            x = sb(name, shape)
            at = nc.sbuf_base - 4 * int(np.prod(shape[1:]))
            return x, nc.alloc_sbuf_tensor_at(name + "_r", shape, F32R, offset=at)

        self.slots, self.slots_r = sb_twice("weight_slots", [P, SLOTS, SLOT_COLS])
        self.x_t = sb("x_t", [P, KT, ALLTOK])
        self.h_t, self.h_r = sb_twice("h_t", [P, KT, ALLTOK])
        self.consts = sb("consts", [P, A["consts"].shape[1]])
        self.arena, self.arena_r = sb_twice("arena", [P, ARENA])
        self.rstd = sb("rstd", [P, 4, 512])
        self.scratch = self.rstd
        self.small = sb("small", [P, 24])
        self.mod_all = sb("mod_all", [P, 256])
        self.h_flat = self.h_t[:, :, :].rearrange("p a b -> p (a b)")
        self.stat = sb("stat", [P, 16])
        self.row_max, self.neg_max = self.stat[:, 0:2], self.stat[:, 2:4]
        self.row_sum, self.row_inv = self.stat[:, 4:6], self.stat[:, 6:8]
        self.q_stage = sb("q_stage", [P, 2, P])
        c = self.const
        self.ident, self.eps, self.one = c("ident", 0, P), c("eps", 0), c("one", 0)

    def const(self, name, at, n=1):
        off = CONST_AT[name]
        return self.consts[:, off + at:off + at + n]

    def slot(self, item):
        return self.slots[:, item % SLOTS, :]

    def slot_ready(self, pe, item, turn=0):
        pe.wait_ge(self.tally.sem(f"slot_{item % SLOTS}_loaded"), turn * 16 + 16 * (item // SLOTS + 1))
        return self.slot(item)

    def part_r(self, at, *dims):
        return self.part(at, *dims, arena=self.arena_r)

    def part(self, at, *dims, parts=P, arena=None):
        n = int(np.prod(dims))
        assert at + n <= ARENA, (at, dims)
        v = (self.arena if arena is None else arena)[0:parts, at:at + n]
        if len(dims) == 1:
            return v
        names = "abc"[:len(dims)]
        return v.rearrange(f"p ({' '.join(names)}) -> p {' '.join(names)}", **{x: d for x, d in zip(names[1:], dims[1:])})

    def attention_buffers(self, at, keys):
        self.biased = self.part(at, 2, keys)
        self.probs = self.part(at + 2 * keys, 2, keys)
        self.probs_t = self.part(at + 4 * keys, 2, max(keys, P))
        return at + 4 * keys + 2 * max(keys, P)

    def block_one(self):
        A, c = self.A, self.const
        x, h = self.x_t, self.h_t
        lat = slice(CTX, ALLTOK)
        segs = segments(SEQ)
        FromHbm(self, [(self.consts[:, :], A["consts"]), (x[:, :, lat], A["x"])])
        Norm(self, x, h, KT, KT, segs, lambda t, a: c("norm_mix", t), c("ones_1024", 0, P))
        z = self.part(0, 10, SEQ)
        toks = self.part(5120, 4, 400)
        o_tok = self.part(6720, 4, 512)
        heads = self.part(8768, 16, SEQ, parts=66)
        work_at = 16960
        f4 = self.part(work_at, SEQ, parts=4)
        y = h[:, :, lat]
        TokenProject(self, h, [2, 3, 4, 5], [256, 144], lambda t, i: toks[:, t - 2, i * 256:i * 256 + (256, 144)[i]])
        h_lat = (self.part_r(work_at, KT, SEQ), self.h_r[:, :, lat])
        Split(self, h[:, :, lat], *h_lat)
        here = [(0, SEQ)]
        Project(self, h_lat, here, 10, lambda t, a, b: z[:, t, :], work_at + KT * SEQ)
        Project(self, h_lat, here, 8, lambda i, a, b: heads[0:HD, i, :], work_at + KT * SEQ, heads=True)
        FoxRows(self, toks, f4)
        ConvMixers(self, z, y, self.part(work_at + 512, 6144))
        sm = self.small
        Scale(self, [(sm[:, 16:17], c("fox_gq", 0), HD ** -0.5), (sm[:, 17:18], c("nsa_gq", 0), HD ** -0.5)])
        gains = [sm[0:HD, 16:17]] * 4 + [c("fox_gk", 0)[0:HD, :]] * 4 + [sm[0:HD, 17:18]] * 4
        units = [(heads[0:HD, i, :], g) for i, g in enumerate(gains)]
        units += [(heads[0:HD, 14, :], c("nsa_gks", 0)[0:HD, :]), (heads[0:HD, 15, :], c("nsa_gkw", 0)[0:HD, :])]
        HeadNorm(self, units, c("ones_64", 0, HD)[0:HD, :], HD)
        FoxGates(self, f4, (heads[64:65, 0:4, :], heads[65:66, 0:4, :]), (heads[64:65, 4:8, :], heads[65:66, 4:8, :]),
                 self.part(work_at + 512, 4 * SEQ))
        w1 = [self.part(0, 32, P, parts=HD), self.part(work_at, 32, P, parts=HD)]
        kc, vc = self.part(4096, 32, parts=HD), self.part(4160, HD, parts=32)
        FromHbm(self, [(w1[0], A["cmp_w1"][:, 0]), (w1[1], A["cmp_w1"][:, 1])])
        Compress(self, heads[0:HD, 12, :], heads[0:HD, 13, :], w1, c("cmp_w2", 0, 2 * HD).rearrange("p (a b) -> p a b", a=2),
                 c("cmp_pos", 0, 2 * CMP_LEN)[0:HD, :], kc[:, 0:N_CMP], vc[0:N_CMP, :], self.part(work_at + 4096, 2112))
        HeadNorm(self, [(kc[:, 0:N_CMP], c("nsa_gkc", 0)[0:HD, :])], c("ones_64", 0, HD)[0:HD, :], HD)
        compressed = self.stages[-1]
        toe = self.part(0, 4, 896)
        cmp_bias = self.part(3584, 4, 4, 32)
        onehots = self.part(work_at, 2, 1024, parts=33)
        rel = self.part(work_at + 2048, 4, parts=33)
        compressed.beside([(onehots, A["onehots"]), (rel, A["rel"])])
        RelBias(self, onehots[:, 0, :], onehots[:, 1, :], rel, self.part(work_at, 1024, parts=4), A["bias_line"], toe,
                cmp_bias)
        self.stages[-1].beside([(self.part(work_at + 3072, 896), A["causal"])])
        gates = toks[:, :, 384:396]
        NsaGates(self, gates)
        self.attention_buffers(work_at, SEQ)
        mask = self.part(work_at + 3072, 896)
        Attention(self, 66, SEQ, 4, 1, 4, lambda hh, t: heads[0:66, hh, bass.ds(t * P, P)],
                  lambda hk, a, b: heads[0:66, 4 + hk, a:b], lambda kt, n, hk: toks[:, kt, bass.ds(hk * HD, HD)],
                  lambda hh, t: o_tok[:, t, bass.ds(hh * HD, HD)], bias=lambda hh, t: mask[:, bass.ds(384 - t * P, SEQ)])
        gate = lambda br: (lambda hh, t: gates[:, t, bass.ds(br * 4 + hh, 1)])
        q = lambda hh, t: heads[0:HD, 8 + hh, bass.ds(t * P, P)]
        o = lambda hh, t: o_tok[:, t, bass.ds(hh * HD + 256, HD)]
        Attention(self, HD, N_CMP, 4, 1, 4, q, lambda hk, a, b: kc[:, a:b], lambda kt, n, hk: vc[0:N_CMP, :], o,
                  bias=lambda hh, t: cmp_bias[:, t, hh, 0:N_CMP], factor=gate(0))
        for br, key, v in ((1, 14, 256), (2, 15, 320)):
            Attention(self, HD, SEQ, 4, 1, 4, q, lambda hk, a, b, key=key: heads[0:HD, key, a:b],
                      lambda kt, n, hk, v=v: toks[:, kt, v:v + HD], o,
                      bias=lambda hh, t: toe[:, hh, bass.ds(384 - t * P, SEQ)], factor=gate(br), add=True)
        Turn(self, [([o_tok[:, t, f * P:(f + 1) * P] for t in range(4)], y[:, 4 + f, :]) for f in range(4)])
        mixed = self.part(0, KT, SEQ)
        mixed_all = self.part(0, KT, ALLTOK)
        Norm(self, h, mixed_all, KT, 2, segs, lambda t, a: c("out_norm", t), c("ones_256", 0, P))
        mixed_lat = (self.h_r[:, :, lat], self.part_r(0, KT, ALLTOK)[:, :, lat])
        Split(self, mixed_all[:, :, lat], *mixed_lat)
        Project(self, mixed_lat, here, KT, lambda t, a, b: x[:, t, lat], KT * ALLTOK, gate=lambda t, a: self.one)
        Norm(self, x, h, KT, KT, segs, lambda t, a: c("norm_ffn", t), c("ones_1024", 0, P))
        self.experts_buffers()
        h_lat = (self.h_hi[:, :, lat], self.h_r[:, :, lat])
        Split(self, h[:, :, lat], *h_lat)
        Experts(self, h_lat, x[:, :, lat], here, D_FF // FF_CHUNK, lambda t, a: self.one)
        self.stages[-1].beside([(x[:, :, 0:CTX], A["ctx"]), (self.part(23000, 16), A["c"])])

    def experts_buffers(self):
        self.hidden = (self.part_r(0, 2, 2, 512), self.part_r(2048, 2, 2, 512))
        self.sigm = self.part(4096, 2, 512)
        self.sel_buf = self.part(5120, 2, P, parts=17)
        self.sel_rows = self.part(5376, 17 * P, parts=17)
        self.comb_rows = self.part(7552, ALLTOK, parts=17)
        self.h_hi = self.part_r(8320, KT, ALLTOK)
        self.w_hi = self.part_r(14464, 3, SLOT_COLS)

    def mods(self, layer):
        return [self.mod[layer][:, i * KT:(i + 1) * KT, :] for i in range(6)]

    def by_stream(self, x):
        return lambda t, a: x[:, t, (1 if a == 0 else 0):(1 if a == 0 else 0) + 1]

    def block_two(self):
        A, c, x, h = self.A, self.const, self.x_t, self.h_t
        every, lat = segments(ALLTOK), segments(SEQ)
        vec = self.mod_all
        self.mod = [vec[:, i * 96:(i + 1) * 96].rearrange("p (m s) -> p m s", s=2) for i in (0, 1)]
        gains = [vec[:, 192 + i * 16:208 + i * 16].rearrange("p (m s) -> p m s", s=2) for i in range(4)]
        c_t = self.part(23000, KT, 2)
        Silu(self, self.part(23000, 16), self.part(23016, 16))
        for layer in (0, 1):
            Ada(self, c_t, self.mod[layer], c("ada_b", layer * 48, 48), self.part(32, 6 * D, parts=2))
        m = [self.mods(0), self.mods(1)]
        ModGains(self, [(gains[2 * l + j], m[l][3 * j + 1], c("norm12", (2 * l + j) * KT, KT)) for l in (0, 1) for j in (0, 1)])

        Norm(self, x, h, KT, KT, every, self.by_stream(gains[0]), c("ones_1024", 0, P), shift=self.by_stream(m[0][0]))
        p = self.part(0, 6, ALLTOK)
        q = self.part(4608, 8, ALLTOK)
        kk = self.part(10752, 8, ALLTOK)
        v = self.part(16896, 6, 512)
        wq = self.part(19968, 3, 768)
        wk, wv = self.part(19968, 2, 8, 96), self.part(21504, 2, 512)
        cos, sin = self.part(22528, 512, parts=96), self.part(23040, 512, parts=96)
        h_parts = (self.part_r(4608, KT, ALLTOK), self.part_r(4608 + 6144, KT, ALLTOK))
        Split(self, h, *h_parts)
        Project(self, h_parts, every, 6, lambda t, a, b: p[:, t, a:b], 4608 + 2 * 6144)
        self.stages[-1].beside([(wq, A["mla_q_up"]), (self.part(22528, 1024, parts=96), A["mla_rope"])])
        qn = self.part(10752, 3, ALLTOK)
        Norm(self, p, qn, 3, 3, every, lambda t, a: c("g_qa", t), c("ones_384", 0, P))
        LocalProject(self, [([(wq[:, kt, hh * 96:(hh + 1) * 96], qn[:, kt, a:b]) for kt in range(3)], q[0:96, hh, a:b])
                            for hh in range(8) for a, b in every])
        kvn = self.part(0, 2, ALLTOK)
        Norm(self, p[:, 3:5, :], kvn, 2, 2, every, lambda t, a: c("g_kva", t), c("ones_256", 0, P))
        self.stages[-1].beside([(self.part(19968, 2560), A["mla_kv_up"])])
        LocalProject(self, [([(wk[:, kt, hh, :], kvn[:, kt, a:b]) for kt in range(2)]
                             + [(c("place", 0, 96)[0:32, :], p[0:32, 5, a:b])], kk[0:96, hh, a:b])
                            for hh in range(8) for a, b in every]
                     + [([(kvn[:, kt, t * P:(t + 1) * P], wv[:, kt, :]) for kt in range(2)], v[:, t, :]) for t in range(6)])
        Scale(self, [(self.small[:, 16:17], c("mla_gq", 0), MLA_QK ** -0.5), (self.small[:, 17:18], c("gqa_gq", 0), HD ** -0.5)])
        HeadNorm(self, [(y[0:96, hh, a:b], g) for y, g in ((q, self.small[0:96, 16:17]), (kk, c("mla_gk", 0)[0:96, :]))
                        for hh in range(8) for a, b in every], c("ones_96", 0, 96)[0:96, :], 96)
        Rope(self, [y[0:96, hh, CTX:ALLTOK] for y in (q, kk) for hh in range(8)], c("mla_rot", 0, 96)[0:96, :], cos, sin, 96)
        self.attention_buffers(0, ALLTOK)
        o_tok = self.part(19968, 6, 512)
        q_all = self.part(4608, 8 * ALLTOK)
        for tile0, tiles, keys in ((0, 2, CTX), (2, 4, ALLTOK)):
            Attention(self, 96, keys, 8, 1, tiles,
                      lambda hh, t, t0=tile0: q_all[0:96, bass.ds(hh * ALLTOK + (t * P + t0 * P), P)],
                      lambda hk, a, b: kk[0:96, hk, a:b], lambda kt, n, hk: v[:, kt, bass.ds(hk * HD, HD)],
                      lambda hh, t, t0=tile0: self.part(19968, 3072)[:, bass.ds(t * 512 + (t0 * 512) + hh * HD, HD)])
        mla_t = self.part(0, 4, ALLTOK)
        Turn(self, [([o_tok[:, t, f * P:(f + 1) * P] for t in ts], mla_t[:, f, ts[0] * P:(ts[-1] + 1) * P])
                    for f in range(4) for ts in ([0, 1], [2, 3, 4, 5])])

        rw = self.part(3072, 15, ALLTOK)
        work = 3072 + 15 * ALLTOK
        h_parts = (self.part_r(work, KT, ALLTOK), self.h_r)
        Split(self, h, *h_parts)
        Project(self, h_parts, every, 15, lambda t, a, b: rw[:, t, a:b], work + KT * ALLTOK)
        at = [work]

        def take(n, *dims):
            at[0] += n
            return self.part(at[0] - n, *(dims or (n,)))

        mu = take(16)
        FromHbm(self, [(mu[:, 0:15], A["rw_mu"])])
        ShiftMix(self, rw, 15, mu, self.part(ARENA - 2 * ALLTOK, 2, ALLTOK), rw[:, 12, :], rw[:, 14, :])
        mixed = self.stages[-1]
        w = Views()
        flat = lambda t0: self.part(3072 + t0 * ALLTOK, 4 * ALLTOK)
        w.r, w.k, w.v = flat(0), flat(4), flat(8)
        w.w1, w.a1 = rw[:, 12, :], rw[:, 13, :]
        y, ksum = self.h_flat[:, 0:3072], self.h_flat[:, 3072:6144]
        rwc = take(RWC_COLS)
        mixed.beside([(rwc, A["rw_consts"])])
        w.w2, w.a2 = rwc[:, 0:512], rwc[:, 512:1024]
        w.csts = rwc[:, 1024:1056]
        w.strict, w.incl, w.first_low, w.first_up = (rwc[:, 1056 + i * P:1056 + (i + 1) * P] for i in range(4))
        w.joins = rwc[:, 1568:1568 + 6 * P]
        w.head_ones = rwc[:, 2336:2464]
        head_mean = rwc[:, 2464:2592]
        out_vecs = rwc[:, 2592:2606]
        w.tiny, gn_eps = rwc[:, 2604:2605], rwc[:, 2605:2606]
        pair = lambda f: f.rearrange("p (d t) -> p d t", d=2)
        quad = lambda f: f.rearrange("p (q t) -> p q t", q=4)
        w.w2s, w.a2s, w.cst = take(P), take(P), take(8)
        w.kc_flat, w.kk = take(256), take(256)
        w.e1, w.ea, w.en = take(256), take(256), take(256)
        w.at_flat, w.rt_flat, w.bt_flat, w.kt_flat = (take(256) for _ in range(4))
        w.at, w.rt, w.bt, w.kt, w.kc, w.e1d = (pair(f) for f in (w.at_flat, w.rt_flat, w.bt_flat, w.kt_flat, w.kc_flat, w.e1))
        w.br, w.kr, w.vr = (pair(take(256)) for _ in range(3))
        lt = take(512)
        lkt, rbt, rkt = (self.rstd[:, i, :] for i in range(3))
        w.lt, w.lkt, w.rbt, w.rkt = quad(lt), quad(lkt), quad(rbt), quad(rkt)
        w.sq, w.root = lt[:, 0:256], lt[:, 256:512]
        w.lw_flat, w.a_flat, w.kd_flat = lkt[:, 0:256], rbt[:, 0:256], rkt[:, 0:256]
        w.lw, w.a, w.kd = pair(w.lw_flat), pair(w.a_flat), pair(w.kd_flat)
        w.lo = take(1024).rearrange("p (l q t) -> p l q t", l=2, q=4)
        xf, xtf, t1f = take(512), take(512), take(512)
        w.x, w.xt, w.t1, w.t1_flat = quad(xf), quad(xtf), quad(t1f), t1f
        w.w1c, w.a1c, w.vc = xf[:, 0:P], xf[:, P:2 * P], pair(t1f[:, 0:256])
        w.wv_flat, w.uv_flat = w.en, w.ea
        w.wv, w.uv = quad(w.wv_flat), quad(w.uv_flat)
        w.s_flat, w.half, w.ones_row = take(128), take(2), take(P)
        w.s = pair(w.s_flat)
        Wkv(self, w, y, ksum)
        g2, g = self.part(work + 16, 512), self.part(at[0] - 3072, 4, ALLTOK)
        assert at[0] - 3072 > work + 16 + RWC_COLS + 512
        g2 = self.part(work + 16 + RWC_COLS, 512)
        FromHbm(self, [(g2, A["rw_g2"])])
        LocalProject(self, [([(g2[:, f * P:(f + 1) * P], rw[:, 14, a:b])], g[:, f, a:b]) for f in range(4) for a, b in every])
        y4, ks4 = h[:, 0:4, :], h[:, 4:8, :]
        RwkvOut(self, y4, ks4, rw[:, 0:4, :], rw[:, 8:12, :], g, head_mean, w.head_ones, out_vecs, gn_eps, self.rstd)
        Copy(self, [(h[:, 4 + f, :], mla_t[:, f, :]) for f in range(4)])
        h_parts = (self.part_r(0, KT, ALLTOK), self.h_r)
        Split(self, h, *h_parts)
        Project(self, h_parts, every, KT, lambda t, a, b: x[:, t, a:b], KT * ALLTOK, gate=self.by_stream(m[0][2]))
        self.moe(every, gains[1], m[0][3], m[0][5], 0)

        Norm(self, x, h, KT, KT, every, self.by_stream(gains[2]), c("ones_1024", 0, P), shift=self.by_stream(m[1][0]))
        q1 = self.part(0, 16, SEQ)
        k1 = self.part(8192, 4, ALLTOK)
        v1 = self.part(11264, 6, 256)
        o1 = self.part(17408, 4, D)
        cos, sin = self.part(21504, 512, parts=HD), self.part(22016, 512, parts=HD)
        TokenProject(self, h, list(range(6)), [256], lambda t, i: v1[:, t, :])
        h_parts = (self.part_r(12800, KT, ALLTOK), self.h_r)
        Split(self, h, *h_parts)
        Project(self, h_parts, lat, 8, lambda i, a, b: q1[0:HD, i, :], 12800 + KT * ALLTOK, heads=True)
        Project(self, h_parts, every, 2, lambda i, a, b: k1[0:HD, i, a:b], 12800 + KT * ALLTOK, heads=True)
        self.stages[-1].beside([(self.part(21504, 1024, parts=HD), A["gqa_rope"])])
        units = [(q1[0:HD, i, :], self.small[0:HD, 17:18]) for i in range(16)]
        units += [(k1[0:HD, i, a:b], c("gqa_gk", 0)[0:HD, :]) for i in range(4) for a, b in every]
        HeadNorm(self, units, c("ones_64", 0, HD)[0:HD, :], HD)
        self.stages[-1].beside(zeros=[self.part(0, 11264)[HD:96, :]])
        Rope(self, [q1[0:HD, i, :] for i in range(16)] + [k1[0:HD, i, CTX:ALLTOK] for i in range(4)],
             c("gqa_rot", 0, HD)[0:HD, :], cos, sin, HD)
        self.attention_buffers(12800, ALLTOK)
        q_rows, o_all = self.part(0, 16 * SEQ), self.part(17408, 4 * D)
        Attention(self, 96, ALLTOK, GQA_KV, GQA_H // GQA_KV, 4, lambda hh, t: q_rows[0:96, bass.ds(hh * SEQ + t * P, P)],
                  lambda hk, a, b: k1[0:96, hk, a:b], lambda kt, n, hk: v1[:, kt, bass.ds(hk * HD, HD)],
                  lambda hh, t: o_all[:, bass.ds(t * D + hh * HD, HD)])
        Turn(self, [([o1[:, t, f * P:(f + 1) * P] for t in range(4)], h[:, f, CTX:ALLTOK]) for f in range(8)])
        h_parts = (self.part_r(0, KT, ALLTOK), self.h_r)
        Split(self, h[:, :, CTX:], h_parts[0][:, :, CTX:], h_parts[1][:, :, CTX:])
        Project(self, h_parts, lat, KT, lambda t, a, b: x[:, t, a:b], KT * ALLTOK, gate=self.by_stream(m[1][2]))
        self.moe(lat, gains[3], m[1][3], m[1][5], 1)

    def moe(self, segs, gain, shift, gate, layer):
        c = self.const
        Norm(self, self.x_t, self.h_t, KT, KT, segs, self.by_stream(gain), c("ones_1024", 0, P), shift=self.by_stream(shift))
        self.experts_buffers()
        self.stages[-1].beside([(self.sel_rows, self.A["sel_rows"])])
        rows = self.comb_rows
        tiles = list(range(segs[0][0] // P, ALLTOK // P))
        Router(self, self.h_t, tiles, c("router_w", 0, KT * N_EXP), c("router_b", 0, N_EXP), self.part(8320, 1024), rows)
        h = self.h_t
        here = slice(segs[0][0], ALLTOK)
        Split(self, h[:, :, here], self.h_hi[:, :, here], self.h_r[:, :, here])
        Experts(self, (self.h_hi, self.h_r), self.x_t, segs[::-1], N_EXP + 1, self.by_stream(gate), comb=rows)


ENGINE_NAMES = ("tensor", "scalar", "vector", "gpsimd")
PRIMED = ("hidden_made", "hidden_ready", "down_added", "combine_spread", "scores_summed", "exp_done", "probs_copied",
          "pv_summed", "head_out", "ada_moved")
PRIME = 16


def build(nc, A, out):
    with ExitStack() as ctx:
        k = Kernel(nc, ctx, A)
        for name in PRIMED:
            k.tally.claim(name, PRIME)
        k.block_one()
        if not A.get("stop"):
            k.block_two()
        items = k.ring.n
        stored = k.tally.sem("output_stored")
        loaded = [k.tally.sem(f"slot_{i}_loaded") for i in range(SLOTS)]
        used = k.tally.sem("weights_used")
        done = {n: k.tally.sem(n + "_stage_done") for n in ENGINE_NAMES}
        block = ctx.enter_context(nc.Block())

        @block.sync
        def _(sp):
            def load(item, slot):
                sp.dma_start(k.slots[:, slot, :], A["weights"][bass.ds(item, 1), :, :].rearrange("a p c -> p (a c)")
                             ).then_inc(loaded[slot], 16)

            sp.wait_ge(k.tally.sem("extra_arrived"), 32)
            for slot in range(SLOTS):
                load(slot, slot)
            with sp.Fori(1, items // SLOTS) as i:
                for slot in range(SLOTS):
                    sp.wait_ge(used, i * SLOTS + (slot - SLOTS + 1))
                    load(i * SLOTS + slot, slot)
            for item in range(items // SLOTS * SLOTS, items):
                sp.wait_ge(used, item - SLOTS + 1)
                load(item, item % SLOTS)
            for name in ENGINE_NAMES:
                sp.wait_ge(done[name], len(k.stages))
            sp.dma_start(out, k.x_t[:, :, CTX:ALLTOK]).then_inc(stored, 16)
            sp.wait_ge(stored, 16)

        @block.tensor
        def _(pe):
            for s in k.stages:
                enter(s, pe, "tensor")
                s.tensor(pe)
                leave(s, pe, "tensor")

        @block.scalar
        def _(act):
            for s in k.stages:
                enter(s, act, "scalar")
                s.scalar(act)
                leave(s, act, "scalar")

        @block.vector
        def _(dve):
            for s in k.stages:
                enter(s, dve, "vector")
                s.vector(dve)
                leave(s, dve, "vector")

        @block.gpsimd
        def _(pool):
            for name in PRIMED:
                pool.drain().then_inc(k.tally.sem(name), PRIME)
            for s in k.stages:
                enter(s, pool, "gpsimd")
                s.start_beside(pool)
                s.gpsimd(pool)
                s.end_beside(pool)
                leave(s, pool, "gpsimd")


def fmaj(v, tiles=None):
    v = np.asarray(v)
    v = v.reshape(v.shape[0], -1)
    return v.reshape(-1, P, v.shape[1]).transpose(1, 0, 2).reshape(P, -1)


def rows(v):
    v = np.asarray(v)
    v = v.reshape(v.shape[0], -1)
    o = np.zeros((P, v.shape[1]), np.float32)
    o[:v.shape[0]] = v
    return o


def bucket(d):
    exact = REL_BUCKETS // 2
    big = exact + (np.log(np.maximum(d, 1).astype(np.float32) / np.float32(exact)) / np.float32(np.log(REL_MAX / exact))
                   * np.float32(REL_BUCKETS - exact)).astype(np.int32)
    return np.where(d < exact, np.maximum(d, 0), np.minimum(big, REL_BUCKETS - 1))


def block_diag(blocks):
    n = len(blocks)
    o = np.zeros((P, P), np.float32)
    for i, b in enumerate(blocks):
        o[i * P // n:(i + 1) * P // n, i * P // n:(i + 1) * P // n] = b
    return o


CONST_AT = {}


def pack_consts(parts):
    at, cols = 0, []
    for name, v in parts:
        CONST_AT[name] = at
        at += v.shape[1]
        cols.append(np.asarray(v, np.float32))
    return np.ascontiguousarray(np.concatenate(cols, axis=1))


def pack_items(w):
    n = -(-w.shape[1] // 256) * 256
    o = np.zeros((D, n), np.float32)
    o[:, :w.shape[1]] = w
    return o.reshape(KT, P, n // 256, 256).transpose(2, 1, 0, 3).reshape(n // 256, P, SLOT_COLS)


def pack_down(w):
    return w.reshape(2, P, D).transpose(1, 0, 2).reshape(1, P, SLOT_COLS)


def expert_items(chunks, paired):
    out, n = [], len(chunks)
    for i in range(0, n, 2):
        pair = [(pack_items(g), pack_items(u), pack_down(d)) for g, u, d in chunks[i:i + 2]]
        if paired and len(pair) == 2:
            out += [pair[0][0], pair[0][1], pair[1][0], pair[1][1], pair[0][2], pair[1][2]]
        else:
            out += [x for p in pair for x in p]
    return out


def host_block_one(i):
    w = np.asarray(i["w_in"])[0]
    g = GROUP
    fox = 5 * g
    q, k_, v, f = (w[:, fox:fox + g], w[:, fox + g:fox + 2 * g], w[:, fox + 2 * g:fox + 3 * g],
                   w[:, fox + 3 * g:fox + 3 * g + 4])
    nq = fox + 3 * g + 4
    kv = [w[:, nq + g + j * HD:nq + g + (j + 1) * HD] for j in range(6)]
    gate = w[:, nq + g + 6 * HD:nq + g + 6 * HD + 12]
    items = [pack_items(v), pack_items(np.concatenate([kv[3], kv[5], gate, f], axis=1)), pack_items(w[:, 0:fox]),
             pack_items(np.concatenate([q, k_, w[:, nq:nq + g], kv[0], kv[1], kv[2], kv[4]], axis=1)),
             pack_items(np.asarray(i["w_out"])[0])]
    gu, dn = np.asarray(i["w_gate_up"])[0], np.asarray(i["w_down"])[0]
    items += expert_items([(gu[:, c:c + 256], gu[:, D_FF + c:D_FF + c + 256], dn[c:c + 256])
                           for c in range(0, D_FF, 256)], True)
    y = np.arange(896)[None, :]
    p = np.arange(P)[:, None]
    lw = np.asarray(i["lru_w_gates"])[0]
    lb = np.asarray(i["lru_b_gates"])[0]
    consts = [
        ("ident", np.eye(P)), ("eps", np.full((P, 1), EPS)), ("one", np.ones((P, 1))),
        ("ones_1024", np.full((P, P), 1 / D)), ("ones_256", np.full((P, P), 1 / 256)),
        ("ones_64", np.full((P, HD), 1 / HD)),
        ("norm_mix", fmaj(i["norm_mix"][0])), ("norm_ffn", fmaj(i["norm_ffn"][0])),
        ("lru_cw", fmaj(np.asarray(i["lru_conv_w"])[0].T)), ("lru_cb", fmaj(i["lru_conv_b"][0])),
        ("lru_wg", np.concatenate([block_diag(lw[a, 2 * c:2 * c + 2]) for a in (0, 1) for c in (0, 1)], axis=1)),
        ("lru_gb", np.concatenate([fmaj(lb[0]), fmaj(lb[1])], axis=1)), ("lru_lam", fmaj(i["lru_lambda"][0])),
        ("sc_w", fmaj(np.asarray(i["sc_conv_w"])[0].T)),
        ("fox_fb", rows(np.asarray(i["fox_f_bias"])[0])),
        ("fox_gq", rows(np.asarray(i["fox_qk_norm"])[0, 0])), ("fox_gk", rows(np.asarray(i["fox_qk_norm"])[0, 1])),
        ("nsa_gq", rows(np.asarray(i["nsa_qk_norm"])[0, 0])), ("nsa_gkc", rows(np.asarray(i["nsa_qk_norm"])[0, 1])),
        ("nsa_gks", rows(np.asarray(i["nsa_qk_norm"])[0, 2])), ("nsa_gkw", rows(np.asarray(i["nsa_qk_norm"])[0, 3])),
        ("cmp_w2", np.concatenate([np.asarray(i["nsa_cmp_w2"])[0, 0], np.asarray(i["nsa_cmp_w2"])[0, 1]], axis=1)),
        ("cmp_pos", rows(np.concatenate([np.asarray(i["nsa_cmp_pos"])[0, 0].T, np.asarray(i["nsa_cmp_pos"])[0, 1].T], axis=1))),
        ("nsa_gb", np.tile(np.asarray(i["nsa_gate_bias"])[0][None, :], (P, 1))),
        ("cmp_valid", (np.arange(P) >= CMP_LEN - 1).astype(np.float32)[:, None]),
        ("out_norm", fmaj(np.asarray(i["out_norm"])[0].reshape(-1))),
    ]
    dist = np.arange(1024) - (SEQ - 1)
    fwd = np.zeros((33, 1024), np.float32)
    fwd[np.where(dist >= 0, bucket(dist), 32), np.arange(1024)] = 1.0
    fwd[32] *= NEG
    rel = np.concatenate([np.asarray(i["rel_bias"]), np.ones((1, 4), np.float32)])
    back = np.zeros_like(fwd)
    back[:, 0:1023] = fwd[:, 0:1023][:, ::-1]
    extra = {
        "causal": np.where(y - 384 <= p, 0.0, NEG).astype(np.float32),
        "x": np.asarray(i["x"])[0].T.reshape(KT, P, SEQ).transpose(1, 0, 2),
        "onehots": np.stack([back, fwd], axis=1), "rel": rel,
        "cmp_w1": np.asarray(i["nsa_cmp_w1"])[0].transpose(2, 0, 1, 3),
    }
    return items, consts, extra


class Views:
    pass


def rope_tables(lead, half, repeat_cos=True):
    inv = (np.float32(ROPE_THETA) ** (-np.arange(half, dtype=np.float32) / half)).astype(np.float32)
    pos = np.arange(SEQ)
    axes = [(pos // GRID_W).astype(np.float32), (pos % GRID_W).astype(np.float32)]
    d = lead + 4 * half
    cos, sin, rot = np.ones((d, SEQ), np.float32), np.zeros((d, SEQ), np.float32), np.zeros((d, d), np.float32)
    for i, axis in enumerate(axes):
        ang = inv[:, None] * axis[None, :]
        for part in (0, 1):
            at = lead + 2 * half * i + half * part
            cos[at:at + half], sin[at:at + half] = np.cos(ang), np.sin(ang)
        for j in range(half):
            a = lead + 2 * half * i + j
            rot[a, a + half], rot[a + half, a] = -1.0, 1.0
    return np.concatenate([cos, sin], axis=1), np.ascontiguousarray(rot.T)


ROPE_THETA, GRID_W = 10000.0, 64
RWC_COLS = 2606


def host_block_two(i):
    n = lambda name: np.asarray(i[name + "_2"])
    items = []
    for layer in (0, 1):
        items.append(pack_items(n("ada_w")[layer]))
    w = n("ab_w_in")[0]
    rwc = 3 * RW_DIM + 384
    items += [pack_items(w[:, rwc:rwc + 672]), pack_items(w[:, 0:rwc]), pack_items(n("ab_w_out")[0])]

    def moe(layer):
        g, u, d = n("moe_w_gate")[layer], n("moe_w_up")[layer], n("moe_w_down")[layer]
        chunks = [(g[e], u[e], d[e]) for e in range(N_EXP)]
        chunks.append((n("shared_w_gate")[layer], n("shared_w_up")[layer], n("shared_w_down")[layer]))
        return expert_items(chunks, paired=layer == 1)

    items += moe(0)
    w = n("gqa_w_in")[0]
    items += [pack_items(w[:, 1280:1536]), pack_items(w[:, 0:1024]), pack_items(w[:, 1024:1280]),
              pack_items(n("gqa_w_out")[0])]
    items += moe(1)

    mla_rope, mla_rot = rope_tables(MLA_NOPE, MLA_ROPE // 4)
    gqa_rope, gqa_rot = rope_tables(0, HD // 4)
    place = np.zeros((32, 96), np.float32)
    place[np.arange(32), 64 + np.arange(32)] = 1.0
    consts = [
        ("ada_b", np.concatenate([fmaj(n("ada_b")[0]), fmaj(n("ada_b")[1])], axis=1)),
        ("norm12", np.concatenate([fmaj(n(f"norm{j}_g")[l]) for l in (0, 1) for j in (1, 2)], axis=1)),
        ("g_qa", fmaj(n("mla_g_qa")[0])), ("g_kva", fmaj(n("mla_g_kva")[0])),
        ("ones_384", np.full((P, P), 1 / 384)), ("ones_96", np.full((P, 96), 1 / 96)),
        ("mla_gq", rows(n("mla_g_q")[0])), ("mla_gk", rows(n("mla_g_k")[0])),
        ("gqa_gq", rows(n("gqa_g_q")[0])), ("gqa_gk", rows(n("gqa_g_k")[0])),
        ("mla_rot", rows(mla_rot)), ("gqa_rot", rows(gqa_rot)), ("place", rows(place)),
        ("router_w", fmaj(n("router_w"))), ("router_b", np.tile(n("router_b")[None, :], (P, 1))),
    ]
    kv = n("mla_w_kv_up")[0].reshape(2, P, MLA_H, 128)
    wk = np.zeros((P, 2, MLA_H, 96), np.float32)
    wk[..., 0:64] = kv[..., 0:64].transpose(1, 0, 2, 3)
    wv = kv[..., 64:128].transpose(1, 0, 2, 3)
    s, t = np.arange(P)[:, None], np.arange(P)[None, :]

    def joins(m):
        return ((s // (2 * m) == t // (2 * m)) & (s % (2 * m) < m) & (t % (2 * m) >= m)).astype(np.float32)

    csts = np.zeros((P, 4, 8), np.float32)
    vecs = [n("rw_w0")[0, 0], n("rw_w0")[0, 1], n("rw_a0")[0, 0], n("rw_a0")[0, 1], n("rw_k_k")[0], n("rw_k_a")[0]]
    for j, x in enumerate(vecs):
        csts[:, :, j] = fmaj(x)
    same = (s // 64 == t // 64).astype(np.float32)
    rw_consts = np.concatenate(
        [n("rw_w2")[0].reshape(P, RW_DIM), n("rw_a2")[0].reshape(P, RW_DIM), csts.reshape(P, 32),
         (s < t).astype(np.float32), (s <= t).astype(np.float32), joins(1).T, joins(1)]
        + [joins(2 ** l) for l in range(1, 7)]
        + [same, same / 64, fmaj(n("rw_ln_w")[0]), fmaj(n("rw_ln_b")[0]), fmaj(n("rw_r_k")[0].reshape(-1)),
           np.full((P, 1), 1e-12), np.full((P, 1), 64e-5)], axis=1).astype(np.float32)
    sel = np.zeros((17, 17, P), np.float32)
    sel[np.arange(17), np.arange(17), :] = 1.0
    c2 = np.stack([n("c")[0], n("c_ctx")], axis=1)
    extra = {
        "ctx": n("ctx")[0].T.reshape(KT, P, CTX).transpose(1, 0, 2), "c": fmaj(c2),
        "mla_q_up": n("mla_w_q_up")[0].reshape(3, P, 768).transpose(1, 0, 2), "mla_rope": mla_rope, "gqa_rope": gqa_rope,
        "mla_kv_up": np.concatenate([wk.reshape(P, -1), wv.reshape(P, -1)], axis=1),
        "rw_mu": fmaj(n("rw_mu")[0]), "rw_consts": rw_consts, "rw_g2": n("rw_g2")[0], "sel_rows": sel.reshape(17, 17 * P),
    }
    return items, consts, extra


def kernel(**inputs):
    import concourse.bacc as bacc
    from concourse.bass_utils import run_bass_kernel_spmd

    items1, consts1, extra1 = host_block_one(inputs)
    items2, consts2, extra2 = host_block_two(inputs)
    arrays = {"weights": np.concatenate(items1 + items2), "consts": pack_consts(consts1 + consts2), **extra1, **extra2}
    nc = bacc.Bacc("TRN2", target_bir_lowering=False, num_devices=1)
    A, feed = {}, {}
    for name, a in arrays.items():
        a = np.ascontiguousarray(a, dtype=np.float32)
        feed[f"in_{name}"] = a
        A[name] = nc.dram_tensor(f"in_{name}", a.shape, F32, kind="ExternalInput").ap()
    A["bias_line"] = nc.dram_tensor("bias_line", [4, P, 1024], F32, kind="Internal").ap()
    out = nc.dram_tensor("out_x", [P, KT, SEQ], F32, kind="ExternalOutput").ap()
    build(nc, A, out)
    r = run_bass_kernel_spmd(nc, [feed], core_ids=[0])
    return np.ascontiguousarray(r.results[0]["out_x"].transpose(1, 0, 2).reshape(D, SEQ).T)[None]
```
